# Optimizing a Trainium2 kernel written in Bass

```python
import jax, jax.numpy as jnp
from jax import lax
import numpy as np
import jax
import jax.numpy as jnp

D_MODEL = 1024
BATCH = 1
SEQ = 256
DEPTH = 2

POOL_WINDOWS = (2, 4, 8, 16)
N_POOL_GROUPS = 4
POOL_GROUP_DIM = D_MODEL // 16
POOL_WIDTH = N_POOL_GROUPS * POOL_GROUP_DIM
HEAD_DIM = 64
N_Q_HEADS = D_MODEL // 128
N_KV_HEADS = 2
GROUP = N_Q_HEADS // N_KV_HEADS
Q_WIDTH = N_Q_HEADS * HEAD_DIM
KV_WIDTH = N_KV_HEADS * HEAD_DIM
WINDOW = 128
ROT_DIM = HEAD_DIM // 4
ROPE_THETA = 500000.0
CONV_WIDTH = D_MODEL // 4
CONV_K = 3
N_BRANCHES = 3
IN_WIDTH = POOL_WIDTH + Q_WIDTH + 2 * KV_WIDTH + 3 * CONV_WIDTH + N_BRANCHES * D_MODEL
D_FF = ((8 * D_MODEL // 3 + 127) // 128) * 128
FFN_K = 3
ALPHA = (2 * DEPTH) ** 0.25
BETA = (8 * DEPTH) ** -0.25
LN_EPS = 1e-5
MASK_VALUE = -1e30


def _split_points(sizes):
    pts, acc = [], 0
    for s in sizes[:-1]:
        acc += s
        pts.append(acc)
    return pts

def layer_norm(x, g, b):
    xf = x.astype(jnp.float32)
    mu = jnp.mean(xf, axis=-1, keepdims=True)
    var = jnp.mean(jnp.square(xf - mu), axis=-1, keepdims=True)
    y = (xf - mu) * lax.rsqrt(var + LN_EPS)
    return (y * g.astype(jnp.float32) + b.astype(jnp.float32)).astype(x.dtype)

def causal_dwconv(u, w):
    K = w.shape[0]
    S = u.shape[1]
    up = jnp.pad(u, ((0, 0), (K - 1, 0), (0, 0)))
    y = up[:, 0:S] * w[0]
    for k in range(1, K):
        y = y + up[:, k:k + S] * w[k]
    return y

def rope_tables(positions):
    inv_freq = ROPE_THETA ** (-jnp.arange(0, ROT_DIM, 2, dtype=jnp.float32) / ROT_DIM)
    ang = positions.astype(jnp.float32)[..., None] * inv_freq
    return jnp.cos(ang), jnp.sin(ang)

def apply_partial_rope(t, cos, sin):
    tf = t.astype(jnp.float32)
    half = ROT_DIM // 2
    x1, x2, rest = tf[..., :half], tf[..., half:ROT_DIM], tf[..., ROT_DIM:]
    c, s = cos[:, :, None, :], sin[:, :, None, :]
    out = jnp.concatenate([x1 * c - x2 * s, x2 * c + x1 * s, rest], axis=-1)
    return out.astype(t.dtype)

def multiscale_pool_mixer(u, w_pool, pool_scale):
    B, S, _ = u.shape
    ug = u.reshape(B, S, N_POOL_GROUPS, POOL_GROUP_DIM).astype(jnp.float32)
    csum = jnp.cumsum(ug, axis=1)
    t = jnp.arange(S)
    outs = []
    for g, w in enumerate(POOL_WINDOWS):
        c = csum[:, :, g]
        c_lag = jnp.pad(c[:, :S - w], ((0, 0), (w, 0), (0, 0)))
        count = jnp.minimum(t + 1, w).astype(jnp.float32)[None, :, None]
        outs.append((c - c_lag) / count - ug[:, :, g])
    pooled = jnp.stack(outs, axis=2).astype(u.dtype)
    mixed = jnp.einsum('bsgc,gcd->bsgd', pooled, w_pool)
    return mixed.reshape(B, S, POOL_WIDTH) * pool_scale

def sliding_window_gqa_sinks(q, k, v, sinks):
    B, S, _, D = q.shape
    nb = S // WINDOW
    qb = q.reshape(B, nb, WINDOW, N_KV_HEADS, GROUP, D)
    kb = k.reshape(B, nb, WINDOW, N_KV_HEADS, D)
    vb = v.reshape(B, nb, WINDOW, N_KV_HEADS, D)
    pad = ((0, 0), (1, 0), (0, 0), (0, 0), (0, 0))
    kcat = jnp.concatenate([jnp.pad(kb[:, :-1], pad), kb], axis=2)
    vcat = jnp.concatenate([jnp.pad(vb[:, :-1], pad), vb], axis=2)
    scores = jnp.einsum('bnqhgd,bnkhd->bnhgqk', qb, kcat).astype(jnp.float32)
    scores = scores * (HEAD_DIM ** -0.5)
    i = jnp.arange(WINDOW)[:, None]
    j = jnp.arange(2 * WINDOW)[None, :]
    band = (j > i) & (j <= i + WINDOW)
    blk = jnp.arange(nb)[:, None, None]
    valid = band[None] & ((blk > 0) | (j[None] >= WINDOW))
    scores = jnp.where(valid[None, :, None, None], scores, MASK_VALUE)
    sink = jnp.broadcast_to(
        sinks.astype(jnp.float32).reshape(1, 1, N_KV_HEADS, GROUP, 1, 1),
        scores.shape[:-1] + (1,))
    probs = jax.nn.softmax(jnp.concatenate([scores, sink], axis=-1), axis=-1)[..., :-1]
    out = jnp.einsum('bnhgqk,bnkhd->bnqhgd', probs.astype(v.dtype), vcat)
    return out.reshape(B, S, N_Q_HEADS * D)

def short_gated_conv(xc, gate_b, gate_c, conv_w):
    return gate_b * causal_dwconv(gate_c * xc, conv_w)

def hybrid_layer(x, cos, sin, w_in, w_pool, pool_scale, attn_sinks, conv_w,
                 w_branch_a, w_branch_b, w_branch_c, w_o, ln1_g, ln1_b,
                 w_up, ffn_conv_w, w_down, ln2_g, ln2_b):
    B, S, _ = x.shape
    proj = jnp.einsum('bsd,de->bse', x, w_in)
    sizes = [POOL_WIDTH, Q_WIDTH, KV_WIDTH, KV_WIDTH,
             CONV_WIDTH, CONV_WIDTH, CONV_WIDTH, N_BRANCHES * D_MODEL]
    u_pool, q, k, v, xc, gate_b, gate_c, gate_logits = jnp.split(
        proj, _split_points(sizes), axis=-1)
    o_a = multiscale_pool_mixer(u_pool, w_pool, pool_scale)
    q = apply_partial_rope(q.reshape(B, S, N_Q_HEADS, HEAD_DIM), cos, sin)
    k = apply_partial_rope(k.reshape(B, S, N_KV_HEADS, HEAD_DIM), cos, sin)
    v = v.reshape(B, S, N_KV_HEADS, HEAD_DIM)
    o_b = sliding_window_gqa_sinks(q, k, v, attn_sinks)
    o_c = short_gated_conv(xc, gate_b, gate_c, conv_w)
    gates = jax.nn.sigmoid(gate_logits).reshape(B, S, N_BRANCHES, D_MODEL)
    merged = (gates[:, :, 0] * jnp.einsum('bsc,cd->bsd', o_a, w_branch_a)
              + gates[:, :, 1] * jnp.einsum('bsc,cd->bsd', o_b, w_branch_b)
              + gates[:, :, 2] * jnp.einsum('bsc,cd->bsd', o_c, w_branch_c))
    mix = jnp.einsum('bsd,de->bse', merged, w_o)
    x = layer_norm(ALPHA * x + mix, ln1_g, ln1_b)
    up = causal_dwconv(jnp.einsum('bsd,df->bsf', x, w_up), ffn_conv_w)
    a, b = jnp.split(up, 2, axis=-1)
    ffn = jnp.einsum('bsf,fd->bsd', jax.nn.silu(a) * b, w_down)
    return layer_norm(ALPHA * x + ffn, ln2_g, ln2_b)

def first_inputs(seed: int = 0) -> dict:
    key = jax.random.key(seed)
    ks = jax.random.split(key, 20)
    nrm = lambda k, shape, scale: jax.random.normal(k, shape, jnp.float32) * scale
    x = nrm(ks[0], (BATCH, SEQ, D_MODEL), 1.0)
    offset = jax.random.randint(ks[1], (BATCH, 1), 0, 1024, dtype=jnp.int32)
    positions = offset + jnp.arange(SEQ, dtype=jnp.int32)[None, :]
    return {
        "x": x,
        "positions": positions,
        "w_in": nrm(ks[2], (DEPTH, D_MODEL, IN_WIDTH), D_MODEL ** -0.5),
        "w_pool": nrm(ks[3], (DEPTH, N_POOL_GROUPS, POOL_GROUP_DIM, POOL_GROUP_DIM), POOL_GROUP_DIM ** -0.5),
        "pool_scale": 1.0 + nrm(ks[4], (DEPTH, POOL_WIDTH), 0.1),
        "attn_sinks": nrm(ks[5], (DEPTH, N_Q_HEADS), 0.5),
        "conv_w": nrm(ks[6], (DEPTH, CONV_K, CONV_WIDTH), CONV_K ** -0.5),
        "w_branch_a": nrm(ks[7], (DEPTH, POOL_WIDTH, D_MODEL), POOL_WIDTH ** -0.5),
        "w_branch_b": nrm(ks[8], (DEPTH, Q_WIDTH, D_MODEL), Q_WIDTH ** -0.5),
        "w_branch_c": nrm(ks[9], (DEPTH, CONV_WIDTH, D_MODEL), CONV_WIDTH ** -0.5),
        "w_o": nrm(ks[10], (DEPTH, D_MODEL, D_MODEL), BETA * D_MODEL ** -0.5),
        "ln1_g": 1.0 + nrm(ks[11], (DEPTH, D_MODEL), 0.02),
        "ln1_b": nrm(ks[12], (DEPTH, D_MODEL), 0.02),
        "w_up": nrm(ks[13], (DEPTH, D_MODEL, 2 * D_FF), D_MODEL ** -0.5),
        "ffn_conv_w": nrm(ks[14], (DEPTH, FFN_K, 2 * D_FF), FFN_K ** -0.5),
        "w_down": nrm(ks[15], (DEPTH, D_FF, D_MODEL), BETA * D_FF ** -0.5),
        "ln2_g": 1.0 + nrm(ks[16], (DEPTH, D_MODEL), 0.02),
        "ln2_b": nrm(ks[17], (DEPTH, D_MODEL), 0.02),
    }

def first_block(x, positions, w_in, w_pool, pool_scale, attn_sinks, conv_w,
              w_branch_a, w_branch_b, w_branch_c, w_o, ln1_g, ln1_b,
              w_up, ffn_conv_w, w_down, ln2_g, ln2_b):
    cos, sin = rope_tables(positions)
    for l in range(DEPTH):
        x = hybrid_layer(x, cos, sin, w_in[l], w_pool[l], pool_scale[l], attn_sinks[l],
                         conv_w[l], w_branch_a[l], w_branch_b[l], w_branch_c[l], w_o[l],
                         ln1_g[l], ln1_b[l], w_up[l], ffn_conv_w[l], w_down[l],
                         ln2_g[l], ln2_b[l])
    return x


ROT_DIM_2 = HEAD_DIM // 4
NORM_EPS = 1e-6
Q_BLOCK = 128
D_FF_2 = 2816
NEG_INF = -1e30

A_GROUPS = 4
A_CHUNK = 128
A_WIDTH = A_GROUPS * HEAD_DIM
B_HEADS = 12
B_KV_HEADS = 3
B_WIDTH = B_HEADS * HEAD_DIM
B_KV_WIDTH = B_KV_HEADS * HEAD_DIM
CMP_LEN = 32
CMP_STRIDE = 16
CMP_HIDDEN = 256
SLC_BLOCK = 64
SLC_TOPN = 8
WINDOW_2 = 512
N_BRANCH = 3
FORCE_SCORE = 1e4
C_HEADS = 8
C_WIDTH = C_HEADS * HEAD_DIM
IDX_HEADS = 4
IDX_DIM = 32
IDX_ROT = IDX_DIM // 4
DSA_TOPK = 256
D_HEADS = 8
D_WIDTH = D_HEADS * HEAD_DIM
MOBA_BLOCK = 256
MOBA_TOPK = 3

EVEN_SPLITS = (2 * A_WIDTH, B_WIDTH) + (B_KV_WIDTH,) * 6 + (B_HEADS * N_BRANCH,)
ODD_SPLITS = (C_WIDTH, HEAD_DIM, HEAD_DIM, IDX_HEADS * IDX_DIM, IDX_DIM, IDX_HEADS, D_WIDTH, D_WIDTH, D_WIDTH)
EVEN_IN = sum(EVEN_SPLITS)
ODD_IN = sum(ODD_SPLITS)
MIX_OUT = A_WIDTH + B_WIDTH
N_EVEN = (DEPTH + 1) // 2
N_ODD = DEPTH // 2


def rmsnorm(x, g):
    xf = x.astype(jnp.float32)
    y = xf * lax.rsqrt(jnp.mean(xf * xf, axis=-1, keepdims=True) + NORM_EPS)
    return (y * g.astype(jnp.float32)).astype(x.dtype)

def rope_tables_2(positions, rot_dim):
    inv_freq = ROPE_THETA ** (-jnp.arange(0, rot_dim, 2, dtype=jnp.float32) / rot_dim)
    ang = positions.astype(jnp.float32)[..., None] * inv_freq
    return jnp.cos(ang), jnp.sin(ang)

def partial_rope(x, cos, sin):
    half = cos.shape[-1]
    bshape = cos.shape[:2] + (1,) * (x.ndim - 3) + (half,)
    c = cos.reshape(bshape).astype(x.dtype)
    s = sin.reshape(bshape).astype(x.dtype)
    x1, x2, rest = x[..., :half], x[..., half:2 * half], x[..., 2 * half:]
    return jnp.concatenate([x1 * c - x2 * s, x2 * c + x1 * s, rest], axis=-1)

def masked_softmax(s, mask):
    s = jnp.where(mask, s.astype(jnp.float32), NEG_INF)
    return jnp.where(mask, jax.nn.softmax(s, axis=-1), 0.0)

def swiglu_ffn(x, g, w_gate, w_up, w_down):
    h = rmsnorm(x, g)
    return (jax.nn.silu(h @ w_gate) * (h @ w_up)) @ w_down

def split_cols(z, sizes):
    return jnp.split(z, [int(c) for c in np.cumsum(sizes)[:-1]], axis=-1)

def rows(a, b, q0):
    return lax.dynamic_slice_in_dim(a[b], q0, Q_BLOCK, axis=0)

def map_query_blocks(fn, batch, seq):
    n_qb = seq // Q_BLOCK

    def step(i):
        return fn(i // n_qb, (i % n_qb) * Q_BLOCK)

    out = lax.map(step, jnp.arange(batch * n_qb, dtype=jnp.int32))
    return out.reshape((batch, seq) + out.shape[2:])

def chunked_gmlp(z, sgu_norm, sgu_w, sgu_b):
    bsz, seq, _ = z.shape
    u, v = jnp.split(jax.nn.gelu(z), 2, axis=-1)
    v = rmsnorm(v, sgu_norm).reshape(bsz, seq // A_CHUNK, A_CHUNK, A_GROUPS, HEAD_DIM)
    causal = jnp.tril(jnp.ones((A_CHUNK, A_CHUNK), dtype=bool))
    w = jnp.where(causal, sgu_w, jnp.zeros_like(sgu_w))
    mixed = jnp.einsum('gts,bcsgd->bctgd', w, v) + sgu_b.T[:, :, None]
    return u * mixed.reshape(bsz, seq, A_WIDTH)

def compress_blocks(t, pos_emb, w1, w2):
    bsz, seq = t.shape[:2]
    n_cmp = (seq - CMP_LEN) // CMP_STRIDE + 1
    idx = jnp.arange(n_cmp)[:, None] * CMP_STRIDE + jnp.arange(CMP_LEN)[None, :]
    blk = t[:, idx] + pos_emb[:, None, :]
    blk = jnp.moveaxis(blk, 3, 2).reshape(bsz, n_cmp, B_KV_HEADS, CMP_LEN * HEAD_DIM)
    return jax.nn.gelu(blk @ w1) @ w2

def cmp_to_slc_overlap(n_cmp, n_slc):
    c0 = np.arange(n_cmp) * CMP_STRIDE
    s0 = np.arange(n_slc) * SLC_BLOCK
    m = (c0[:, None] < s0[None, :] + SLC_BLOCK) & (c0[:, None] + CMP_LEN > s0[None, :])
    return jnp.asarray(m, dtype=jnp.float32)

def nsa_attention(q_rot, q_raw, k_cmp, v_cmp, k_slc, v_slc, k_win, v_win, gates):
    bsz, seq = q_rot.shape[:2]
    grp = B_HEADS // B_KV_HEADS
    scale = HEAD_DIM ** -0.5
    n_cmp = k_cmp.shape[1]
    n_slc = seq // SLC_BLOCK
    top_n = min(SLC_TOPN, n_slc)
    overlap = cmp_to_slc_overlap(n_cmp, n_slc)
    cmp_end = jnp.arange(n_cmp) * CMP_STRIDE + CMP_LEN - 1
    blk_id = jnp.arange(n_slc)
    k_blk = k_slc.reshape(bsz, n_slc, SLC_BLOCK, B_KV_HEADS, HEAD_DIM).transpose(0, 3, 1, 2, 4)
    v_blk = v_slc.reshape(bsz, n_slc, SLC_BLOCK, B_KV_HEADS, HEAD_DIM).transpose(0, 3, 1, 2, 4)
    pad = jnp.zeros((bsz, WINDOW_2, B_KV_HEADS, HEAD_DIM), k_win.dtype)
    k_win_p = jnp.concatenate([pad, k_win], axis=1)
    v_win_p = jnp.concatenate([pad, v_win], axis=1)
    g_idx = jnp.arange(B_KV_HEADS)[:, None, None]
    win_off = jnp.arange(Q_BLOCK + WINDOW_2) - WINDOW_2

    def block(b, q0):
        t = q0 + jnp.arange(Q_BLOCK)
        qr = rows(q_rot, b, q0).reshape(Q_BLOCK, B_KV_HEADS, grp, HEAD_DIM)
        qn = rows(q_raw, b, q0).reshape(Q_BLOCK, B_KV_HEADS, grp, HEAD_DIM)
        s_c = jnp.einsum('qgrd,ngd->grqn', qn, k_cmp[b]) * scale
        p_c = masked_softmax(s_c, cmp_end[None, :] <= t[:, None])
        o_c = jnp.einsum('grqn,ngd->qgrd', p_c.astype(v_cmp.dtype), v_cmp[b])
        imp = jnp.einsum('grqn,nj->gqj', p_c, overlap)
        admissible = blk_id[None, :] * SLC_BLOCK <= t[:, None]
        forced = (blk_id[None, :] == 0) | (blk_id[None, :] == t[:, None] // SLC_BLOCK)
        imp = jnp.where(admissible, jnp.where(forced, FORCE_SCORE, imp), NEG_INF)
        _, sel = lax.top_k(imp, top_n)
        sel_ok = jnp.take_along_axis(jnp.broadcast_to(admissible, imp.shape), sel, axis=-1)
        ks = k_blk[b][g_idx, sel].reshape(B_KV_HEADS, Q_BLOCK, top_n * SLC_BLOCK, HEAD_DIM)
        vs = v_blk[b][g_idx, sel].reshape(B_KV_HEADS, Q_BLOCK, top_n * SLC_BLOCK, HEAD_DIM)
        tok = (sel[..., None] * SLC_BLOCK + jnp.arange(SLC_BLOCK)).reshape(B_KV_HEADS, Q_BLOCK, top_n * SLC_BLOCK)
        m_s = (tok <= t[None, :, None]) & jnp.repeat(sel_ok, SLC_BLOCK, axis=-1)
        s_s = jnp.einsum('qgrd,gqkd->grqk', qr, ks) * scale
        p_s = masked_softmax(s_s, m_s[:, None])
        o_s = jnp.einsum('grqk,gqkd->qgrd', p_s.astype(vs.dtype), vs)
        kw = lax.dynamic_slice_in_dim(k_win_p[b], q0, Q_BLOCK + WINDOW_2, axis=0)
        vw = lax.dynamic_slice_in_dim(v_win_p[b], q0, Q_BLOCK + WINDOW_2, axis=0)
        s_pos = q0 + win_off
        m_w = (s_pos[None, :] <= t[:, None]) & (s_pos[None, :] > t[:, None] - WINDOW_2) & (s_pos[None, :] >= 0)
        s_w = jnp.einsum('qgrd,kgd->grqk', qr, kw) * scale
        p_w = masked_softmax(s_w, m_w)
        o_w = jnp.einsum('grqk,kgd->qgrd', p_w.astype(vw.dtype), vw)
        g = rows(gates, b, q0).reshape(Q_BLOCK, B_KV_HEADS, grp, N_BRANCH)
        o = g[..., 0:1] * o_c + g[..., 1:2] * o_s + g[..., 2:3] * o_w
        return o.reshape(Q_BLOCK, B_WIDTH)

    return map_query_blocks(block, bsz, seq)

def dsa_attention(q, k, v, q_idx, k_idx, w_idx):
    bsz, seq = q.shape[:2]
    top_k = min(DSA_TOPK, seq // 4)
    scale = HEAD_DIM ** -0.5
    key_pos = jnp.arange(seq)

    def block(b, q0):
        t = q0 + jnp.arange(Q_BLOCK)
        qb = rows(q, b, q0)
        logits = jnp.einsum('qhd,sd->qhs', rows(q_idx, b, q0), k_idx[b]).astype(jnp.float32) * IDX_DIM ** -0.5
        score = jnp.einsum('qh,qhs->qs', rows(w_idx, b, q0).astype(jnp.float32), jax.nn.relu(logits)) * IDX_HEADS ** -0.5
        score = jnp.where(key_pos[None, :] <= t[:, None], score, NEG_INF)
        _, sel = lax.top_k(score, top_k)
        ok = sel <= t[:, None]
        ks = k[b][sel]
        vs = v[b][sel]
        s = jnp.einsum('qhd,qkd->hqk', qb, ks) * scale
        p = masked_softmax(s, ok[None])
        o = jnp.einsum('hqk,qkd->qhd', p.astype(vs.dtype), vs)
        return o.reshape(Q_BLOCK, C_WIDTH)

    return map_query_blocks(block, bsz, seq)

def moba_attention(q, k, v):
    bsz, seq = q.shape[:2]
    n_blk = -(-seq // MOBA_BLOCK)
    pad = n_blk * MOBA_BLOCK - seq
    scale = HEAD_DIM ** -0.5
    k_blk = jnp.pad(k, ((0, 0), (0, pad), (0, 0), (0, 0))).reshape(bsz, n_blk, MOBA_BLOCK, D_HEADS, HEAD_DIM).transpose(0, 3, 1, 2, 4)
    v_blk = jnp.pad(v, ((0, 0), (0, pad), (0, 0), (0, 0))).reshape(bsz, n_blk, MOBA_BLOCK, D_HEADS, HEAD_DIM).transpose(0, 3, 1, 2, 4)
    k_mean = k_blk.mean(axis=3)
    top_k = min(MOBA_TOPK, n_blk - 1)
    blk_id = jnp.arange(n_blk)
    h_idx = jnp.arange(D_HEADS)[:, None, None]

    def block(b, q0):
        t = q0 + jnp.arange(Q_BLOCK)
        qb = rows(q, b, q0)
        own = q0 // MOBA_BLOCK
        k_own = lax.dynamic_index_in_dim(k_blk[b], own, axis=1, keepdims=False)
        v_own = lax.dynamic_index_in_dim(v_blk[b], own, axis=1, keepdims=False)
        own_pos = own * MOBA_BLOCK + jnp.arange(MOBA_BLOCK)
        s_own = jnp.einsum('qhd,hkd->hqk', qb, k_own) * scale
        m_own = jnp.broadcast_to(own_pos[None, :] <= t[:, None], s_own.shape)
        if top_k == 0:
            p = masked_softmax(s_own, m_own)
            o = jnp.einsum('hqk,hkd->qhd', p.astype(v_own.dtype), v_own)
        else:
            gate = jnp.einsum('qhd,hjd->hqj', qb, k_mean[b]).astype(jnp.float32)
            gate = jnp.where(blk_id < own, gate, NEG_INF)
            _, sel = lax.top_k(gate, top_k)
            ok = sel < own
            n_sel = top_k * MOBA_BLOCK
            ks = k_blk[b][h_idx, sel].reshape(D_HEADS, Q_BLOCK, n_sel, HEAD_DIM)
            vs = v_blk[b][h_idx, sel].reshape(D_HEADS, Q_BLOCK, n_sel, HEAD_DIM)
            s_sel = jnp.einsum('qhd,hqkd->hqk', qb, ks) * scale
            m_sel = jnp.repeat(ok, MOBA_BLOCK, axis=-1)
            p = masked_softmax(jnp.concatenate([s_sel, s_own], axis=-1), jnp.concatenate([m_sel, m_own], axis=-1))
            o = (jnp.einsum('hqk,hqkd->qhd', p[..., :n_sel].astype(vs.dtype), vs)
                 + jnp.einsum('hqk,hkd->qhd', p[..., n_sel:].astype(v_own.dtype), v_own))
        return o.reshape(Q_BLOCK, D_WIDTH)

    return map_query_blocks(block, bsz, seq)

def even_mixer(h, cos, sin, w_in, sgu_norm, sgu_w, sgu_b, cmp_pos_k, cmp_w1_k, cmp_w2_k,
               cmp_pos_v, cmp_w1_v, cmp_w2_v, w_out):
    bsz, seq, _ = h.shape
    a_in, q, kc, vc, ksl, vsl, kw, vw, gl = split_cols(h @ w_in, EVEN_SPLITS)

    def kv(t):
        return t.reshape(bsz, seq, B_KV_HEADS, HEAD_DIM)

    q_raw = q.reshape(bsz, seq, B_HEADS, HEAD_DIM)
    a_out = chunked_gmlp(a_in, sgu_norm, sgu_w, sgu_b)
    b_out = nsa_attention(partial_rope(q_raw, cos, sin), q_raw,
                          compress_blocks(kv(kc), cmp_pos_k, cmp_w1_k, cmp_w2_k),
                          compress_blocks(kv(vc), cmp_pos_v, cmp_w1_v, cmp_w2_v),
                          partial_rope(kv(ksl), cos, sin), kv(vsl),
                          partial_rope(kv(kw), cos, sin), kv(vw),
                          jax.nn.sigmoid(gl).reshape(bsz, seq, B_HEADS, N_BRANCH))
    return jnp.concatenate([a_out, b_out], axis=-1) @ w_out

def odd_mixer(h, cos, sin, cos_i, sin_i, w_in, w_out):
    bsz, seq, _ = h.shape
    qc, kc, vc, qi, ki, wi, qd, kd, vd = split_cols(h @ w_in, ODD_SPLITS)
    c_out = dsa_attention(partial_rope(qc.reshape(bsz, seq, C_HEADS, HEAD_DIM), cos, sin),
                          partial_rope(kc, cos, sin), vc,
                          partial_rope(qi.reshape(bsz, seq, IDX_HEADS, IDX_DIM), cos_i, sin_i),
                          partial_rope(ki, cos_i, sin_i), wi)
    d_out = moba_attention(partial_rope(qd.reshape(bsz, seq, D_HEADS, HEAD_DIM), cos, sin),
                           partial_rope(kd.reshape(bsz, seq, D_HEADS, HEAD_DIM), cos, sin),
                           vd.reshape(bsz, seq, D_HEADS, HEAD_DIM))
    return jnp.concatenate([c_out, d_out], axis=-1) @ w_out

def second_inputs(seed: int = 0) -> dict:
    key = jax.random.key(seed)
    keys = iter(jax.random.split(key, 40))

    def nrm(shape, scale):
        return jax.random.normal(next(keys), shape, jnp.float32) * scale

    def gain(shape):
        return 1.0 + nrm(shape, 0.1)

    x = nrm((BATCH, SEQ, D_MODEL), 1.0)
    offset = jax.random.randint(next(keys), (BATCH, 1), 0, 4096, dtype=jnp.int32)
    positions = offset + jnp.arange(SEQ, dtype=jnp.int32)[None, :]
    return {
        'x': x,
        'positions': positions,
        'ffn1_norm': gain((DEPTH, D_MODEL)),
        'ffn1_w_gate': nrm((DEPTH, D_MODEL, D_FF_2), D_MODEL ** -0.5),
        'ffn1_w_up': nrm((DEPTH, D_MODEL, D_FF_2), D_MODEL ** -0.5),
        'ffn1_w_down': nrm((DEPTH, D_FF_2, D_MODEL), D_FF_2 ** -0.5),
        'mix_norm': gain((DEPTH, D_MODEL)),
        'ffn2_norm': gain((DEPTH, D_MODEL)),
        'ffn2_w_gate': nrm((DEPTH, D_MODEL, D_FF_2), D_MODEL ** -0.5),
        'ffn2_w_up': nrm((DEPTH, D_MODEL, D_FF_2), D_MODEL ** -0.5),
        'ffn2_w_down': nrm((DEPTH, D_FF_2, D_MODEL), D_FF_2 ** -0.5),
        'ev_w_in': nrm((N_EVEN, D_MODEL, EVEN_IN), D_MODEL ** -0.5),
        'ev_sgu_norm': gain((N_EVEN, A_WIDTH)),
        'ev_sgu_w': nrm((N_EVEN, A_GROUPS, A_CHUNK, A_CHUNK), A_CHUNK ** -0.5),
        'ev_sgu_b': gain((N_EVEN, A_GROUPS, A_CHUNK)),
        'ev_cmp_pos_k': nrm((N_EVEN, CMP_LEN, HEAD_DIM), 0.1),
        'ev_cmp_w1_k': nrm((N_EVEN, CMP_LEN * HEAD_DIM, CMP_HIDDEN), (CMP_LEN * HEAD_DIM) ** -0.5),
        'ev_cmp_w2_k': nrm((N_EVEN, CMP_HIDDEN, HEAD_DIM), CMP_HIDDEN ** -0.5),
        'ev_cmp_pos_v': nrm((N_EVEN, CMP_LEN, HEAD_DIM), 0.1),
        'ev_cmp_w1_v': nrm((N_EVEN, CMP_LEN * HEAD_DIM, CMP_HIDDEN), (CMP_LEN * HEAD_DIM) ** -0.5),
        'ev_cmp_w2_v': nrm((N_EVEN, CMP_HIDDEN, HEAD_DIM), CMP_HIDDEN ** -0.5),
        'ev_w_out': nrm((N_EVEN, MIX_OUT, D_MODEL), MIX_OUT ** -0.5),
        'od_w_in': nrm((N_ODD, D_MODEL, ODD_IN), D_MODEL ** -0.5),
        'od_w_out': nrm((N_ODD, MIX_OUT, D_MODEL), MIX_OUT ** -0.5),
        'final_norm': gain((D_MODEL,)),
    }

def second_block(x, positions, ffn1_norm, ffn1_w_gate, ffn1_w_up, ffn1_w_down, mix_norm,
              ffn2_norm, ffn2_w_gate, ffn2_w_up, ffn2_w_down, ev_w_in, ev_sgu_norm, ev_sgu_w,
              ev_sgu_b, ev_cmp_pos_k, ev_cmp_w1_k, ev_cmp_w2_k, ev_cmp_pos_v, ev_cmp_w1_v,
              ev_cmp_w2_v, ev_w_out, od_w_in, od_w_out, final_norm):
    cos, sin = rope_tables_2(positions, ROT_DIM_2)
    cos_i, sin_i = rope_tables_2(positions, IDX_ROT)
    for i in range(DEPTH):
        x = x + 0.5 * swiglu_ffn(x, ffn1_norm[i], ffn1_w_gate[i], ffn1_w_up[i], ffn1_w_down[i])
        h = rmsnorm(x, mix_norm[i])
        if i % 2 == 0:
            e = i // 2
            x = x + even_mixer(h, cos, sin, ev_w_in[e], ev_sgu_norm[e], ev_sgu_w[e], ev_sgu_b[e],
                               ev_cmp_pos_k[e], ev_cmp_w1_k[e], ev_cmp_w2_k[e],
                               ev_cmp_pos_v[e], ev_cmp_w1_v[e], ev_cmp_w2_v[e], ev_w_out[e])
        else:
            o = i // 2
            x = x + odd_mixer(h, cos, sin, cos_i, sin_i, od_w_in[o], od_w_out[o])
        x = x + 0.5 * swiglu_ffn(x, ffn2_norm[i], ffn2_w_gate[i], ffn2_w_up[i], ffn2_w_down[i])
    return rmsnorm(x, final_norm)


def setup_inputs(seed=0):
    out = dict(first_inputs(seed))
    for name, value in second_inputs(seed + 1).items():
        if name != "x":
            out[name + "_2"] = value
    return out


def reference(
    x, positions, w_in, w_pool, pool_scale, attn_sinks, conv_w, w_branch_a, w_branch_b,
    w_branch_c, w_o, ln1_g, ln1_b, w_up, ffn_conv_w, w_down, ln2_g, ln2_b, positions_2,
    ffn1_norm_2, ffn1_w_gate_2, ffn1_w_up_2, ffn1_w_down_2, mix_norm_2, ffn2_norm_2,
    ffn2_w_gate_2, ffn2_w_up_2, ffn2_w_down_2, ev_w_in_2, ev_sgu_norm_2, ev_sgu_w_2, ev_sgu_b_2,
    ev_cmp_pos_k_2, ev_cmp_w1_k_2, ev_cmp_w2_k_2, ev_cmp_pos_v_2, ev_cmp_w1_v_2, ev_cmp_w2_v_2,
    ev_w_out_2, od_w_in_2, od_w_out_2, final_norm_2,
):
    x = first_block(
        x, positions, w_in, w_pool, pool_scale, attn_sinks, conv_w, w_branch_a, w_branch_b,
        w_branch_c, w_o, ln1_g, ln1_b, w_up, ffn_conv_w, w_down, ln2_g, ln2_b,
    )
    return second_block(
        x, positions_2, ffn1_norm_2, ffn1_w_gate_2, ffn1_w_up_2, ffn1_w_down_2, mix_norm_2,
        ffn2_norm_2, ffn2_w_gate_2, ffn2_w_up_2, ffn2_w_down_2, ev_w_in_2, ev_sgu_norm_2,
        ev_sgu_w_2, ev_sgu_b_2, ev_cmp_pos_k_2, ev_cmp_w1_k_2, ev_cmp_w2_k_2, ev_cmp_pos_v_2,
        ev_cmp_w1_v_2, ev_cmp_w2_v_2, ev_w_out_2, od_w_in_2, od_w_out_2, final_norm_2,
    )


_drawn_inputs = setup_inputs


def setup_inputs(seed=0):
    import zlib

    import numpy as np

    out = dict(_drawn_inputs(seed))
    spreads = {}
    factors = {'attn_sinks': 7.951, 'ev_cmp_pos_k_2': 6.583}
    for name, (base, spread) in spreads.items():
        noise = np.random.default_rng([zlib.crc32(name.encode()), seed]).standard_normal(out[name].shape)
        drawn = base * np.exp(spread * noise) if base else spread * noise
        out[name] = jnp.asarray(drawn.astype(out[name].dtype))
    for name, factor in factors.items():
        out[name] = (out[name] * factor).astype(out[name].dtype)
    return out
```

```python
from contextlib import ExitStack, contextmanager

import numpy as np

import concourse.bass as bass
from concourse import mybir

F32 = mybir.dt.float32
F32R = mybir.dt.float32r
I32 = mybir.dt.int32
ALU = mybir.AluOpType
ACT = mybir.ActivationFunctionType
AX = mybir.AxisListType

P = 128
D = 1024
KT = D // P
T = 256
QT = T // P
DEPTH = 2
DH = 64
D_FF = 2816
FT = D_FF // P
CH = 2048
RING = 3
PAIRS = FT // 2
FFN_CHUNKS = FT + PAIRS
ALPHA = (2 * DEPTH) ** 0.25
LN_EPS = 1e-5
RMS_EPS = 1e-6
NEG = -1e30
TAKEN = -3e38
TOPK = min(256, T // 4)
SCALE = DH ** -0.5
IDX_HEADS, IDX_DIM = 4, 32
B_HEADS, B_KV = 12, 3
CMP_LEN, CMP_STRIDE = 32, 16
NCMP = T // CMP_STRIDE
SEQ_K = T + P
POOL_PAD = 16
ROPE_THETA = 500000.0

IN1, GATE1, OUT = 7, 16, 4
EV_IN, CMP, OD_IN = 10, 4, 10


def panel(w):
    return w.reshape(KT, P, 2 * P).transpose(1, 0, 2).reshape(P, CH)


def down_pair(w):
    return w.reshape(2, P, D).transpose(1, 0, 2).reshape(P, CH)


def per_partition(v):
    return v.reshape(-1, P).T


def ffn_chunks(a, b, down):
    u = [panel(np.concatenate([a[:, j * P:(j + 1) * P], b[:, j * P:(j + 1) * P]], 1)) for j in range(FT)]
    d = [down_pair(down[2 * P * m:2 * P * (m + 1)]) for m in range(PAIRS)]
    out = u[:2]
    for m in range(PAIRS - 1):
        out += [u[2 * m + 2], d[m], u[2 * m + 3]]
    return out + [d[-1]]


def panels(w):
    return [panel(w[:, c:c + 2 * P]) for c in range(0, w.shape[1], 2 * P)]


def weight_stream(a):
    s = []
    for l in range(DEPTH):
        w = a["w_in"][l]
        pool, q, k, v, xc, gb, gc, gates = np.split(w, np.cumsum([256, 512, 128, 128, 256, 256, 256]), 1)
        s += panels(np.concatenate([q, k, v, pool, xc, gb, gc], 1))
        branch = np.concatenate([a["w_branch_a"][l], a["w_branch_b"][l], a["w_branch_c"][l]], 0)
        for j in range(KT // 2):
            cols = slice(2 * P * j, 2 * P * (j + 1))
            s += [panel(gates[:, b * D:(b + 1) * D][:, cols]) for b in range(3)] + [panel(branch[:, cols])]
        s += panels(a["w_o"][l])
        s += ffn_chunks(a["w_up"][l][:, :D_FF], a["w_up"][l][:, D_FF:], a["w_down"][l])
    for l in range(DEPTH):
        for n in (1, 2):
            if n == 2:
                if l % 2 == 0:
                    z, q, kc, vc, ks, vs, kw, vw, gl = np.split(
                        a["ev_w_in_2"][0], np.cumsum([512, 768] + [192] * 6), 1)
                    fill = np.zeros((D, P - gl.shape[1]), np.float32)
                    s += panels(np.concatenate([z, q, kc, vc, ks, kw, vs, vw, gl, fill], 1))
                    for x in "kv":
                        w1 = a[f"ev_cmp_w1_{x}_2"][0].reshape(2, CMP_STRIDE, DH, 256)
                        w1 = w1.transpose(1, 0, 2, 3).reshape(2 * D, 256)
                        s += [panel(w1[:D]), panel(w1[D:])]
                    s += panels(a["ev_w_out_2"][0])
                else:
                    q, kc, vc, qi, ki, wi, qd, kd, vd = np.split(
                        a["od_w_in_2"][0], np.cumsum([512, 64, 64, 128, 32, 4, 512, 512]), 1)
                    fill = np.zeros((D, P - 68), np.float32)
                    s += panels(np.concatenate([q, kc, kc, vc, wi, fill, qi, ki, ki, ki, ki, qd, kd, vd], 1))
                    s += panels(a["od_w_out_2"][0])
            s += ffn_chunks(a[f"ffn{n}_w_gate_2"][l], a[f"ffn{n}_w_up_2"][l], a[f"ffn{n}_w_down_2"][l])
    return np.stack(s)


def small_parameters(a):
    p = np.arange(P)
    t = np.arange(T)
    c = {"ident": np.eye(P)}
    for name, dim, half in (("rotate", DH, 8), ("rotate_i", IDX_DIM, 4)):
        r = np.zeros((P, P))
        for i in p:
            if i % dim < half:
                r[i, i + half] = -1
            elif i % dim < 2 * half:
                r[i, i - half] = 1
        c[name] = r.T
        freq = np.float32(ROPE_THETA) ** (-np.arange(0, 2 * half, 2, dtype=np.float32) / np.float32(2 * half))
        c["freq" + name[6:]] = np.where(p % dim < 2 * half, freq[(p % dim) % half], 0)[:, None]
    causal = np.where(t[None] <= p[:, None], 0, NEG)
    later = np.where(t[None] <= p[:, None] + P, 0, NEG)
    window = np.where((t[None] <= p[:, None] + P) & (t[None] > p[:, None]), 0, NEG)
    c["causal"] = np.concatenate([causal[:, :P], later], 1)
    c["window"] = np.concatenate([causal[:, :P], window], 1)
    n = np.arange(NCMP)
    tok = p[:, None, None] + P * np.arange(QT)[None, :, None]
    ok = (n * CMP_STRIDE + CMP_LEN - 1 <= tok) & (n * CMP_STRIDE + CMP_LEN <= T)
    c["cmp_mask"] = np.where(ok, 0, NEG).reshape(P, QT * NCMP)
    c["cmp_any"] = ok.any(-1)
    win = np.array([[2, 8], [4, 16]])[p // DH]
    c["per_count"] = (1 / np.minimum(t + 1, win[..., None])).reshape(P, 2 * T)
    for l in range(DEPTH):
        wp = np.zeros((P, 2, P), np.float32)
        for g in range(4):
            b = DH * (g % 2)
            wp[b:b + DH, g // 2, b:b + DH] = a["w_pool"][l, g]
        c[f"w_pool{l}"] = wp.reshape(P, 2 * P)
        c[f"pool_scale{l}"] = per_partition(a["pool_scale"][l])
        c[f"sinks{l}"] = np.broadcast_to(a["attn_sinks"][l], (P, 8))
        c[f"conv_w{l}"] = a["conv_w"][l].reshape(3, 2, P).transpose(2, 1, 0).reshape(P, 6)
        c[f"ffn_conv{l}"] = a["ffn_conv_w"][l].reshape(3, 2, FT, P).transpose(3, 2, 1, 0).reshape(P, FT * 6)
        for x in ("ln1_g", "ln1_b", "ln2_g", "ln2_b"):
            c[f"{x}{l}"] = per_partition(a[x][l])
        for x in ("ffn1_norm", "mix_norm", "ffn2_norm"):
            c[f"{x}{l}"] = per_partition(a[x + "_2"][l])
    c["final_norm"] = per_partition(a["final_norm_2"])
    c["sgu_norm"] = per_partition(a["ev_sgu_norm_2"][0])
    c["sgu_w"] = a["ev_sgu_w_2"][0].transpose(2, 0, 1).reshape(P, 4 * P)
    c["sgu_b"] = np.repeat(a["ev_sgu_b_2"][0].reshape(2, 2, P), DH, 1).transpose(1, 0, 2).reshape(P, 2 * P)
    for x in "kv":
        c[f"pos_{x}"] = a[f"ev_cmp_pos_{x}_2"][0].reshape(2, CMP_STRIDE, DH).transpose(0, 2, 1).reshape(P, CMP_STRIDE)
    w2 = a["ev_cmp_w2_k_2"][0].reshape(2, P, DH).transpose(1, 0, 2)
    c["cmp_w2_k"] = np.concatenate([w2, w2], 2).reshape(P, 2 * P)
    c["cmp_w2_v"] = a["ev_cmp_w2_v_2"][0].reshape(2, P, DH).transpose(1, 0, 2).reshape(P, 2 * DH)
    at, off = {}, 0
    for name, v in c.items():
        at[name] = (off, v.shape[1])
        off += v.shape[1]
    return np.concatenate([np.asarray(v, np.float32) for v in c.values()], 1), at


class Counts:

    def __init__(self, nc, ctx, seen):
        self.nc, self.ctx, self.seen = nc, ctx, seen
        self.sems, self.total, self.now, self.loop = {}, {}, {}, None

    def sem(self, name):
        if name not in self.sems:
            self.sems[name] = self.ctx.enter_context(self.nc.semaphore(name))
        return self.sems[name]

    def raised(self, name, event, by=1):
        assert event not in self.now, event
        self.total[name] = self.total.get(name, 0) + by
        self.now[event] = (name, self.total[name], 0, 1)
        if self.loop is not None:
            self.loop.append(event)
        return self.sem(name), by

    def alias(self, event, other):
        self.now[event] = self.now[other]
        if self.loop is not None:
            self.loop.append(event)

    @contextmanager
    def fori(self, eng, n):
        start = dict(self.total)
        self.loop = []
        with eng.Fori(0, n) as i:
            yield i
        for event in self.loop:
            name, count, _, _ = self.now[event]
            self.now[event] = (name, count, self.total[name] - start.get(name, 0), n)
        for name, count in self.total.items():
            self.total[name] = start.get(name, 0) + n * (count - start.get(name, 0))
        self.loop = None

    def done(self, event, i=None, lag=0):
        if self.seen is None:
            return self.sem("first_build"), 1
        name, count, slope, n = self.seen[event]
        if i is None or not slope:
            return self.sem(name), count + slope * (n - 1)
        assert count - lag * slope > 0, event
        return self.sem(name), i * slope + (count - lag * slope)


def build(nc, weights, params, at, x_in, pos1, pos2, out, seen):
    n_chunks = weights.shape[0]
    with ExitStack() as ctx:
        def sb(name, shape, dt=F32):
            return ctx.enter_context(nc.sbuf_tensor(name, shape, dt))

        K = Counts(nc, ctx, seen)
        done, raised = K.done, K.raised

        raw = sb("raw", [P, RING, CH])
        w_high = sb("w_high", [P, RING, CH], F32R)
        w_low = sb("w_low", [P, RING, CH], F32R)
        X = sb("X", [P, KT, T])
        XH = sb("XH", [P, KT, T], F32R)
        XL = sb("XL", [P, KT, T], F32R)
        OH = sb("OH", [P, KT, T], F32R)
        OL = sb("OL", [P, KT, T], F32R)
        W = sb("W", [P, KT, T])
        RS = sb("RS", [P, T])
        FEAT = sb("FEAT", [P, 20, T])
        QR = sb("QR", [P, 6, T])
        KD = sb("KD", [P, 6, T])
        VT = sb("VT", [P, QT, 512])
        PRM = sb("PRM", [P, params.shape[1]])
        ropes = sb("ropes", [P, 4, T])
        ones_d = sb("ones_d", [P, P])
        ones_v = sb("ones_v", [P, P])
        posi = QR[:, 0:2, :].bitcast(I32)
        posf = W[:, 7, :]
        small = sb("small", [P, 144])
        SM = sb("SM", [P, 4, SEQ_K])
        PT = sb("PT", [P, 4, SEQ_K])
        UP = sb("UP", [P, 2, 2, T + 2])
        G2 = sb("G2", [P, 2, 2, T])
        SIL = sb("SIL", [P, 2, T])
        A = sb("A", [P, 2, T])
        AH = sb("AH", [P, 2, T], F32R)
        AL = sb("AL", [P, 2, T], F32R)

        PS = [ctx.enter_context(nc.psum_tensor(f"PS{b}", [P, 512], F32)) for b in range(2)]
        ACC = ctx.enter_context(nc.psum_tensor("ACC", [P, 4, 512], F32))
        OUTP = ctx.enter_context(nc.psum_tensor("OUTP", [P, 512], F32))
        MISC = ctx.enter_context(nc.psum_tensor("MISC", [P, 512], F32))

        def prm(name):
            off, n = at[name]
            return PRM[:, off:off + n]

        def two(ap):
            return ap.rearrange("p (a t) -> p a t", a=2)

        def over(ap, n):
            return ap.rearrange("p (a t) -> p a t", a=1).broadcast_to([P, n, ap.shape[1]])

        ident = prm("ident")
        banks = [two(PS[0][:, :]), two(PS[1][:, :])]
        acc = [two(ACC[:, b, :]) for b in range(4)]
        misc = two(MISC[:, :])
        outp = two(OUTP[:, :])
        Wr = W[:, :, :].rearrange("p k t -> p t k")

        def split_high(act, c, i=None):
            s = c % RING
            act.wait_ge(K.sem(f"chunk_loaded{s}"), 16 * (c // RING + 1) if i is None else i * 16 + 16 * (c // RING + 1))
            act.activation(w_high[:, s, :], raw[:, s, :], ACT.Copy).then_inc(K.sem("w_high_ready"), 1)

        def split_low(dve, c, i=None):
            s = c % RING
            dve.wait_ge(K.sem("w_high_ready"), c + 1 if i is None else i * RING + (c + 1))
            dve.tensor_tensor(w_low[:, s, :], raw[:, s, :], w_high[:, s, :].bitcast(F32),
                              ALU.subtract).then_inc(K.sem("w_low_ready"), 1)

        def act_ahead(act, c):
            if c + 2 < n_chunks:
                if c >= 1:
                    act.wait_ge(*done(("used", c - 1)))
                split_high(act, c + 2)

        def dve_ahead(dve, c):
            if c + 2 < n_chunks:
                split_low(dve, c + 2)

        def weights_ready(pe, c, i=None):
            pe.wait_ge(K.sem("w_low_ready"), c + 1 if i is None else i * RING + (c + 1))

        def multiply(pe, bank, s, XH=XH, XL=XL, ks=range(KT)):
            ks = list(ks)
            for n in range(2):
                for k in ks:
                    w = slice(k * 2 * P + n * P, k * 2 * P + (n + 1) * P)
                    pe.matmul(bank[:, n, :], w_high[:, s, w], XH[:, k, :], start=k == ks[0], stop=False)
                    pe.matmul(bank[:, n, :], w_high[:, s, w], XL[:, k, :], start=False, stop=False)
                    mm = pe.matmul(bank[:, n, :], w_low[:, s, w], XH[:, k, :], start=False, stop=k == ks[-1])
            return mm

        def multiply_down(pe, s, half, buf):
            for n in range(KT):
                w = slice(half * D + n * P, half * D + (n + 1) * P)
                for a, b in ((w_high, AH), (w_high, AL), (w_low, AH)):
                    mm = pe.matmul(acc[n // 2][:, n % 2, :], a[:, s, w], b[:, buf, :], start=False,
                                   stop=False, skip_group_check=True)
            return mm

        class Bank:
            read = [None, None]

        def pe_panel(pe, c, b, event):
            weights_ready(pe, c)
            if Bank.read[b] is not None:
                pe.wait_ge(*done(Bank.read[b]))
            mm = multiply(pe, banks[b], c % RING)
            mm.then_inc(*raised("panel_done", event))
            K.alias(("used", c), event)
            Bank.read[b] = event + ("read",)

        block = ctx.enter_context(nc.Block())


        def ffn_pe(pe, f, c0):
            def up(c, i, ev, lag_ev):
                b = ev in ("p1", "b")
                weights_ready(pe, c, i)
                if i is not None:
                    pe.wait_ge(*done(("ffn_read", f, ev), i, 1))
                elif Bank.read[b] is not None:
                    pe.wait_ge(*done(Bank.read[b]))
                multiply(pe, banks[b], c % RING).then_inc(*raised("panel_done", ("up", f, ev)))

            def down(c, i, half, ev, act_ev, lag):
                if i is None:
                    pe.wait_ge(*done(act_ev))
                else:
                    pe.wait_ge(*done(act_ev, i, lag))
                weights_ready(pe, c, i)
                multiply_down(pe, c % RING, half, half).then_inc(*raised("acc_done", ev))

            pe.wait_ge(*done(("x_split", f)))
            up(c0, None, "p0", None)
            up(c0 + 1, None, "p1", None)
            pe.wait_ge(*done(("acc_zero", f)))
            with K.fori(pe, PAIRS - 1) as i:
                up(c0 + 2, i, "a", None)
                down(c0 + 3, i, 0, ("down", f, "a"), ("act", f, "a"), 1)
                up(c0 + 4, i, "b", None)
                down(c0 + 3, i, 1, ("down", f, "b"), ("act", f, "b"), 1)
            down(c0 + FFN_CHUNKS - 1, None, 0, ("down", f, "last0"), ("act", f, "a"), 0)
            down(c0 + FFN_CHUNKS - 1, None, 1, ("down", f, "last1"), ("act", f, "b"), 0)
            Bank.read[0], Bank.read[1] = ("ffn_read", f, "a"), ("ffn_read", f, "b")
            last = c0 + FFN_CHUNKS
            K.alias(("used", last - 3), ("down", f, "b"))
            K.alias(("used", last - 2), ("up", f, "b"))
            K.alias(("used", last - 1), ("down", f, "last1"))

        def ffn_act(act, f, c0, conv):
            def take(b, i, ev):
                if conv is not None:
                    act.wait_ge(*done(("up", f, ev), i))
                    if i is not None:
                        act.wait_ge(*done(("conv", f, ev), i, 1))
                    act.activation(UP[:, b, :, 2:], banks[b], ACT.Copy)\
                        .then_inc(*raised("panel_read", ("ffn_read", f, ev)))

            def silu(b, i, ev):
                act.wait_ge(*done(("gated_in", f, ev), i))
                act.activation(SIL[:, b, :], G2[:, b, 0, :], ACT.Silu)\
                    .then_inc(*raised("silu_ready", ("silu", f, ev)))

            act_ahead(act, c0)
            take(0, None, "p0")
            silu(0, None, "p0")
            take(1, None, "p1")
            silu(1, None, "p1")
            act.wait_ge(*done(("up", f, "p1")))
            with K.fori(act, PAIRS - 1) as i:
                act.wait_ge(*done(("down", f, "b"), i, 1))
                split_high(act, c0 + 3, i)
                act.wait_ge(*done(("up", f, "b"), i, 1))
                split_high(act, c0 + 4, i)
                take(0, i, "a")
                silu(0, i, "a")
                act.wait_ge(*done(("up", f, "a"), i))
                split_high(act, c0 + 5, i)
                take(1, i, "b")
                silu(1, i, "b")
            last = c0 + FFN_CHUNKS
            for c in (last - 2, last - 1):
                act_ahead(act, c)

        def ffn_dve(dve, f, c0, conv):
            def enter(b, i, ev):
                if conv is None:
                    dve.wait_ge(*done(("up", f, ev), i))
                    if ev == "p0":
                        dve.wait_ge(*done(("rms", f)))
                    dve.tensor_tensor(G2[:, b], banks[b], over(RS[:, :], 2), ALU.mult)\
                        .then_inc(*raised("panel_read" if conv is not None else "panel_scaled", ("ffn_read", f, ev)))
                    K.alias(("gated_in", f, ev), ("ffn_read", f, ev))
                    return
                w = prm(f"ffn_conv{conv}").rearrange("p (j x) -> p j x", x=6)
                j = {"p0": 0, "p1": 1}[ev] if i is None else i * 2 + (2 + b)
                dve.wait_ge(*done(("ffn_read", f, ev), i))
                for tap in range(3):
                    if tap:
                        dve.wait_ge(*done(("conv", f, ev, tap - 1), i))
                    for ab in range(2):
                        k = w[:, j:j + 1, ab * 3 + tap] if i is None else w[:, bass.ds(j, 1), ab * 3 + tap]
                        src = UP[:, b, ab, tap:tap + T]
                        if tap == 0:
                            ins = dve.tensor_scalar(G2[:, b, ab, :], src, k, None, ALU.mult)
                        else:
                            ins = dve.scalar_tensor_tensor(out=G2[:, b, ab, :], in0=src, scalar=k,
                                                           in1=G2[:, b, ab, :], op0=ALU.mult, op1=ALU.add)
                    ins.then_inc(*raised("conv_ready", ("conv", f, ev, tap)))
                K.alias(("conv", f, ev), ("conv", f, ev, 2))
                K.alias(("gated_in", f, ev), ("conv", f, ev, 2))

            def leave(b, i, ev):
                dve.wait_ge(*done(("silu", f, ev), i))
                dve.tensor_tensor(A[:, b, :], SIL[:, b, :], G2[:, b, 1, :], ALU.mult)\
                    .then_inc(*raised("product_ready", ("product", f, ev)))
                if i is not None:
                    dve.wait_ge(*done(("down", f, ev), i))
                dve.wait_ge(*done(("product", f, ev), i))
                dve.tensor_copy(AH[:, b, :], A[:, b, :]).then_inc(*raised("product_ready", ("act_high", f, ev)))
                dve.wait_ge(*done(("act_high", f, ev), i))
                dve.tensor_tensor(AL[:, b, :], A[:, b, :], AH[:, b, :].bitcast(F32), ALU.subtract)\
                    .then_inc(*raised("act_split", ("act", f, ev)))

            dve_ahead(dve, c0)
            dve.memset(ACC[:, :, :], 0.0).then_inc(*raised("acc_zeroed", ("acc_zero", f)))
            enter(0, None, "p0")
            leave(0, None, "p0")
            enter(1, None, "p1")
            leave(1, None, "p1")
            with K.fori(dve, PAIRS - 1) as i:
                split_low(dve, c0 + 3, i)
                split_low(dve, c0 + 4, i)
                enter(0, i, "a")
                split_low(dve, c0 + 5, i)
                leave(0, i, "a")
                enter(1, i, "b")
                leave(1, i, "b")
            last = c0 + FFN_CHUNKS
            for c in (last - 2, last - 1):
                dve_ahead(dve, c)

        def residual_from_acc(dve, f, first):
            dve.wait_ge(*done(("down", f, "last1")))
            for b in range(4):
                x = X[:, 2 * b:2 * b + 2, :]
                if first:
                    ins = dve.scalar_tensor_tensor(out=x, in0=x, scalar=ALPHA, in1=acc[b], op0=ALU.mult, op1=ALU.add)
                else:
                    ins = dve.scalar_tensor_tensor(out=x, in0=acc[b], scalar=0.5, in1=x, op0=ALU.mult, op1=ALU.add)
                ins.then_inc(*raised("residual_added", ("resid", f, b)))

        def out_pe(pe, m, c0):
            pe.wait_ge(*done(("o_split", m)))
            for j in range(OUT):
                weights_ready(pe, c0 + j)
                pe.wait_ge(*done(Bank.read[j % 2]))
                multiply(pe, banks[j % 2], (c0 + j) % RING, OH, OL).then_inc(*raised("panel_done", ("out", m, j)))
                K.alias(("used", c0 + j), ("out", m, j))
                Bank.read[j % 2] = ("resid", m, j)

        def out_dve(dve, m, c0, first):
            for j in range(OUT):
                dve_ahead(dve, c0 + j)
                dve.wait_ge(*done(("out", m, j)))
                x = X[:, 2 * j:2 * j + 2, :]
                dve.scalar_tensor_tensor(out=x, in0=x, scalar=ALPHA if first else 1.0, in1=banks[j % 2],
                                         op0=ALU.mult, op1=ALU.add).then_inc(*raised("residual_added", ("resid", m, j)))

        def out_act(act, m, c0):
            for j in range(OUT):
                act_ahead(act, c0 + j)

        def ln_pe(pe, m):
            pe.wait_ge(*done(("sums", m)))
            pe.matmul(MISC[:, 0:T], ones_d[:, :], RS[:, :], start=True, stop=True)\
                .then_inc(*raised("mean_ready", ("mean", m)))
            pe.wait_ge(*done(("sums2", m)))
            pe.matmul(MISC[:, 0:T], ones_d[:, :], RS[:, :], start=True, stop=True)\
                .then_inc(*raised("second_mean", ("mean2", m)))

        def ln_dve(dve, m, n, g, b):
            dve.wait_ge(*done(("resid", m, 3)))
            dve.tensor_reduce(RS[:, :], X[:, :, :].rearrange("p k t -> p t k"), AX.X, ALU.add)\
                .then_inc(*raised("feature_sums", ("sums", m)))
            dve.wait_ge(*done(("mean", m)))
            dve.tensor_tensor(X[:, :, :], X[:, :, :], over(MISC[:, 0:T], KT), ALU.subtract)\
                .then_inc(*raised("centered", ("centered", m)))
            dve.wait_ge(*done(("squares", m)))
            dve.tensor_reduce(RS[:, :], Wr, AX.X, ALU.add).then_inc(*raised("square_sums", ("sums2", m)))
            dve.wait_ge(*done(("mean2", m)))
            dve.tensor_scalar(RS[:, :], MISC[:, 0:T], LN_EPS, None, ALU.add).then_inc(*raised("variance", ("var", m)))
            dve.wait_ge(*done(("root", m)))
            dve.reciprocal(RS[:, :], RS[:, :]).then_inc(*raised("ln_factor", ("rstd", m)))
            dve.wait_ge(*done(("rstd", m)))
            dve.tensor_tensor(W[:, :, :], X[:, :, :], over(RS[:, :], KT), ALU.mult)\
                .then_inc(*raised("normed", ("normed", m)))
            dve.wait_ge(*done(("normed", m)))
            for k in range(KT):
                ins = dve.tensor_scalar(X[:, k, :], W[:, k, :], prm(g)[:, k:k + 1], prm(b)[:, k:k + 1],
                                        ALU.mult, ALU.add)
            ins.then_inc(*raised("ln_out", ("ln_out", m)))
            dve.wait_ge(*done(("ln_out", m)))
            if n is None:
                for q in range(4):
                    K.alias(("resid", "stack2", q), ("ln_out", m))
                return
            dve.wait_ge(*done(("x_high", n)))
            dve.tensor_tensor(XL[:, :, :], X[:, :, :], XH[:, :, :].bitcast(F32), ALU.subtract)\
                .then_inc(*raised("x_split", ("x_split", n)))

        def ln_act(act, m, n, g, b):
            act.wait_ge(*done(("centered", m)))
            act.activation(W[:, :, :], X[:, :, :], ACT.Square).then_inc(*raised("squares_ready", ("squares", m)))
            act.wait_ge(*done(("var", m)))
            act.activation(RS[:, :], RS[:, :], ACT.Sqrt).then_inc(*raised("deviation", ("root", m)))
            if n is None:
                return
            act.wait_ge(*done(("normed", m)))
            for k in range(KT):
                ins = act.activation(XH[:, k, :], W[:, k, :], ACT.Identity, scale=prm(g)[:, k:k + 1],
                                     bias=prm(b)[:, k:k + 1])
            ins.then_inc(*raised("x_high", ("x_high", n)))

        def rms_act(act, m, n, g):
            for b in range(4):
                act.wait_ge(*done(("resid", m, b)))
                if n is None:
                    continue
                for k in (2 * b, 2 * b + 1):
                    ins = act.activation(XH[:, k, :], X[:, k, :], ACT.Identity, scale=prm(g)[:, k:k + 1])
                ins.then_inc(*raised("x_tile_high", ("xh", n, b)))
            act.activation(W[:, :, :], X[:, :, :], ACT.Square).then_inc(*raised("squares_ready", ("squares", m)))
            act.wait_ge(*done(("var", m)))
            act.activation(RS[:, :], RS[:, :], ACT.Sqrt).then_inc(*raised("deviation", ("root", m)))

        def rms_pe(pe, m):
            pe.wait_ge(*done(("sums", m)))
            pe.matmul(MISC[:, 0:T], ones_d[:, :], RS[:, :], start=True, stop=True)\
                .then_inc(*raised("mean_ready", ("mean", m)))

        def rms_dve(dve, m, n, g):
            for b in range(4 if n is not None else 0):
                dve.wait_ge(*done(("xh", n, b)))
                for k in (2 * b, 2 * b + 1):
                    ins = dve.scalar_tensor_tensor(out=XL[:, k, :], in0=X[:, k, :], scalar=prm(g)[:, k:k + 1],
                                                   in1=XH[:, k, :].bitcast(F32), op0=ALU.mult, op1=ALU.subtract)
                ins.then_inc(*raised("x_split", ("x_split", n) if b == 3 else ("xl", n, b)))
            dve.wait_ge(*done(("squares", m)))
            dve.tensor_reduce(RS[:, :], Wr, AX.X, ALU.add).then_inc(*raised("feature_sums", ("sums", m)))
            dve.wait_ge(*done(("mean", m)))
            dve.tensor_scalar(RS[:, :], MISC[:, 0:T], RMS_EPS, None, ALU.add).then_inc(*raised("variance", ("var", m)))
            dve.wait_ge(*done(("root", m)))
            dve.reciprocal(RS[:, :], RS[:, :]).then_inc(*raised("rms_factor", ("rms", n)))
            dve.wait_ge(*done(("rms", n)))

        def in_pe(pe, m, c0, n):
            pe.wait_ge(*done(("x_split", m)))
            for j in range(n):
                pe_panel(pe, c0 + j, j % 2, ("in", m, j))

        def in_act(act, m, c0, n, copy):
            for j in range(n):
                act_ahead(act, c0 + j)
                if copy:
                    act.wait_ge(*done(("in", m, j)))
                    act.activation(FEAT[:, 2 * j:2 * j + 2, :], banks[j % 2], ACT.Copy)\
                        .then_inc(*raised("panel_read", ("in", m, j, "read")))

        def in_dve(dve, m, c0, n, scale):
            for j in range(n):
                dve_ahead(dve, c0 + j)
                if scale:
                    dve.wait_ge(*done(("in", m, j)))
                    dve.tensor_tensor(FEAT[:, 2 * j:2 * j + 2, :], banks[j % 2], over(RS[:, :], 2), ALU.mult)\
                        .then_inc(*raised("panel_scaled", ("in", m, j, "read")))

        def rope_pe(pe, tag, src, after, matrix):
            n = src.shape[1]
            for j in range(0, n, 2):
                pe.wait_ge(*done(after))
                if j:
                    pe.wait_ge(*done((tag, j - 2, "sin")))
                else:
                    misc_free(pe)
                for t in range(j, min(j + 2, n)):
                    mm = pe.matmul(misc[:, t - j, :], prm(matrix), src[:, t, :], start=True, stop=True)
                mm.then_inc(*raised("rotated", (tag, j, "rotated")))
            Misc.read = (tag, (n - 1) // 2 * 2, "sin")

        def rope_dve(dve, tag, src, dst, after, cs, tmp):
            n = src.shape[1]
            dve.wait_ge(*done(after))
            for j in range(0, n, 2):
                w = min(2, n - j)
                dve.wait_ge(*done((tag, j, "rotated")))
                if j:
                    dve.wait_ge(*done((tag, j - 2, "done")))
                dve.tensor_tensor(tmp[:, 0:w, :], misc[:, 0:w, :], over(ropes[:, cs + 1, :], w), ALU.mult)\
                    .then_inc(*raised("sin_part", (tag, j, "sin")))
                dve.tensor_tensor(dst[:, j:j + w, :], src[:, j:j + w, :], over(ropes[:, cs, :], w), ALU.mult)\
                    .then_inc(*raised("cos_part", (tag, j, "cos")))
                dve.wait_ge(*done((tag, j, "cos")))
                dve.tensor_tensor(dst[:, j:j + w, :], dst[:, j:j + w, :], tmp[:, 0:w, :], ALU.add)\
                    .then_inc(*raised("rotation_added", (tag, j, "done")))

        class Misc:
            read = None
            outp = None
            accs = None
            sm = None

        def misc_free(pe):
            if Misc.read is not None:
                pe.wait_ge(*done(Misc.read))

        def turn_pe(pe, tag, tiles, after):
            pe.wait_ge(*done(after))
            misc_free(pe)
            for r in range(QT):
                for n, t in enumerate(tiles):
                    mm = pe.transpose(MISC[:, (r * len(tiles) + n) * P:(r * len(tiles) + n + 1) * P],
                                      t[:, r * P:(r + 1) * P], ident)
            mm.then_inc(*raised("turned", (tag, "turned")))
            Misc.read = (tag, "copied")

        def turn_act(act, tag, n, dst, func=ACT.Copy):
            act.wait_ge(*done((tag, "turned")))
            act.activation(dst, MISC[:, 0:QT * n * P].rearrange("p (r c) -> p r c", r=QT)[:, :, 0:dst.shape[2]],
                           func).then_inc(*raised("psum_copied", (tag, "copied")))

        def attend_pe(pe, tag, q, k, v, after, zero_after):
            for e in after:
                pe.wait_ge(*done(e))
            if Misc.accs is not None:
                pe.wait_ge(*done(Misc.accs))
            for h in range(4):
                pe.matmul(ACC[:, h, 0:P], q[h][:, 0:P], k[h][:, 0:P], start=True, stop=True)
                mm = pe.matmul(ACC[:, h, P:SEQ_K], q[h][:, P:T], k[h][:, 0:T], start=True, stop=True)
            mm.then_inc(*raised("scores_done", (tag, "scores")))
            pe.wait_ge(*done((tag, "probs")))
            for h in range(4):
                for b in range(3):
                    mm = pe.transpose(ACC[:, h, b * P:(b + 1) * P], SM[:, h, b * P:(b + 1) * P], ident)
            mm.then_inc(*raised("turned", (tag, "turned")))
            pe.wait_ge(*done((tag, "copied")))
            pe.wait_ge(*done(zero_after))
            for h in range(4):
                o = OUTP[(h % 2) * DH:(h % 2 + 1) * DH, (h // 2) * T:(h // 2 + 1) * T]
                pe.matmul(o, v(h, 0), PT[:, h, 0:T], start=False, stop=False, skip_group_check=True)
                mm = pe.matmul(o[:, P:T], v(h, 1), PT[:, h, T:SEQ_K], start=False, stop=False,
                               skip_group_check=True)
            mm.then_inc(*raised("attended", (tag, "out")))
            Misc.accs = (tag, "copied")

        MX, NM, SU, RC, G8 = (small[:, 8 * n:8 * n + 8] for n in range(5))

        def attend_act(act, tag, busy=None):
            act.wait_ge(*done((tag, "max")))
            for h in range(4):
                for r, (lo, hi) in enumerate(((0, P), (P, SEQ_K))):
                    n = 2 * h + r
                    ins = act.activation(SM[:, h, lo:hi], SM[:, h, lo:hi], ACT.Exp, bias=NM[:, n:n + 1],
                                         accum_out=SU[:, n:n + 1])
            ins.then_inc(*raised("exps_ready", (tag, "exps")))
            act.wait_ge(*done((tag, "turned")))
            if busy is not None:
                act.wait_ge(*done(busy))
            act.activation(PT[:, :, :], ACC[:, :, 0:SEQ_K], ACT.Copy).then_inc(*raised("psum_copied", (tag, "copied")))

        def normalise(dve, tag, sink, gate):
            dve.wait_ge(*done((tag, "exps")))
            if sink is not None:
                dve.wait_ge(*done((tag, "sink_exp")))
                dve.tensor_tensor(SU, SU, G8, ALU.add).then_inc(*raised("row_sum", (tag, "sum")))
                dve.wait_ge(*done((tag, "sum")))
            dve.reciprocal(RC, SU).then_inc(*raised("sum_inverted", (tag, "rc")))
            dve.wait_ge(*done((tag, "rc")))
            if gate is not None:
                dve.tensor_tensor(RC.rearrange("p (h r) -> p h r", r=2), RC.rearrange("p (h r) -> p h r", r=2),
                                  gate, ALU.mult).then_inc(*raised("gate_applied", (tag, "gated")))
                dve.wait_ge(*done((tag, "gated")))

        def attend_dve(dve, tag, mask, sink=None, gate=None, busy=None):
            dve.wait_ge(*done((tag, "scores")))
            if busy is not None:
                dve.wait_ge(*done(busy))
            dve.scalar_tensor_tensor(out=SM[:, :, :], in0=ACC[:, :, 0:SEQ_K], scalar=SCALE, in1=over(mask, 4),
                                     op0=ALU.mult, op1=ALU.add).then_inc(*raised("scores_masked", (tag, "masked")))
            dve.wait_ge(*done((tag, "masked")))
            m = MX.rearrange("p (h r) -> p h r", r=2)
            for r, (lo, hi) in enumerate(((0, P), (P, SEQ_K))):
                ins = dve.tensor_reduce(m[:, :, r], SM[:, :, lo:hi], AX.X, ALU.max)
            ins.then_inc(*raised("row_max", (tag, "mx")))
            dve.wait_ge(*done((tag, "mx")))
            if sink is not None:
                s = sink.rearrange("p (h r) -> p h r", r=1).broadcast_to([P, 4, 2])
                dve.tensor_tensor(m, m, s, ALU.max).then_inc(*raised("row_max_with_sink", (tag, "mxs")))
                dve.wait_ge(*done((tag, "mxs")))
                dve.tensor_tensor(G8.rearrange("p (h r) -> p h r", r=2), s, m, ALU.subtract)\
                    .then_inc(*raised("sink_less", (tag, "sink_less")))
            dve.tensor_scalar(NM, MX, -1.0, None, ALU.mult).then_inc(*raised("negated_max", (tag, "max")))
            normalise(dve, tag, sink, gate)
            rc = RC.rearrange("p (h r) -> p h r", r=2)
            for r, (lo, hi) in enumerate(((0, P), (P, SEQ_K))):
                ins = dve.tensor_tensor(SM[:, :, lo:hi], SM[:, :, lo:hi],
                                        rc[:, :, r:r + 1].broadcast_to([P, 4, hi - lo]), ALU.mult)
            ins.then_inc(*raised("probs_ready", (tag, "probs")))

        def sink_act(act, tag):
            act.wait_ge(*done((tag, "sink_less")))
            act.activation(G8, G8, ACT.Exp).then_inc(*raised("sink_exp", (tag, "sink_exp")))

        def heads_out_dve(dve, tag, tile):
            dve.wait_ge(*done((tag, "out")))
            dve.tensor_copy(W[:, tile:tile + 2, :], outp).then_inc(*raised("heads_copied", (tag, "heads")))

        def zero_out_dve(dve, tag):
            dve.memset(OUTP[:, :], 0.0).then_inc(*raised("out_zeroed", (tag, "zero")))

        def split_o_act(act, m, after):
            for e in after:
                act.wait_ge(*done(e))
            act.activation(OH[:, :, :], W[:, :, :], ACT.Copy).then_inc(*raised("o_high_ready", ("oh", m)))

        def split_o_dve(dve, m, event):
            dve.wait_ge(*done(("oh", m)))
            dve.tensor_tensor(OL[:, :, :], W[:, :, :], OH[:, :, :].bitcast(F32), ALU.subtract)\
                .then_inc(*raised("table_step", event))

        POOL0 = 6
        PU = [PT[:, :, :].rearrange("p a b -> p (a b)")[:, n * 2 * (T + POOL_PAD):(n + 1) * 2 * (T + POOL_PAD)]
              .rearrange("p (a t) -> p a t", a=2) for n in range(2)]
        SMf = SM[:, :, :].rearrange("p a b -> p (a b)")
        SUMS = SMf[:, 0:2 * T].rearrange("p (a t) -> p a t", a=2)
        CV = SMf[:, 2 * T:2 * T + 2 * (T + 2)].rearrange("p (a t) -> p a t", a=2)

        def mix1_heads(h0):
            q = [FEAT[(h % 2) * DH:(h % 2 + 1) * DH, 2 * h0 + h // 2, :] for h in range(4)]
            k = [KD[(h % 2) * DH:(h % 2 + 1) * DH, h0, :] for h in range(4)]
            return q, k, lambda h, r: VT[:, r, h0 * DH:(h0 + 1) * DH]

        def merge_pe(pe, l, c1):
            for j in range(KT // 2):
                for g in range(3):
                    pe_panel(pe, c1 + 4 * j + g, (j + g) % 2, ("gate", l, j, g))
                c = c1 + 4 * j + 3
                weights_ready(pe, c)
                if j == 0:
                    pe.wait_ge(*done(("o_split", ("mix", l))))
                else:
                    pe.wait_ge(*done(("merge", l, j - 1, 2)))
                for b, ks in enumerate((range(0, 2), range(2, 6), range(6, 8))):
                    mm = multiply(pe, acc[b], c % RING, OH, OL, ks)
                mm.then_inc(*raised("acc_done", ("branch", l, j)))
                K.alias(("used", c), ("branch", l, j))
            Misc.accs = ("merge", l, KT // 2 - 1, 2)

        GS = FEAT

        def merge_act(act, l, c1):
            for j in range(KT // 2):
                for g in range(3):
                    act_ahead(act, c1 + 4 * j + g)
                    act.wait_ge(*done(("gate", l, j, g)))
                    if j:
                        act.wait_ge(*done(("merge", l, j - 1, g)))
                    act.activation(GS[:, 14 + 2 * g:16 + 2 * g, :], banks[(j + g) % 2], ACT.Sigmoid)\
                        .then_inc(*raised("panel_read", ("gate", l, j, g, "read")))
                act_ahead(act, c1 + 4 * j + 3)
            act.wait_ge(*done(("branch", l, KT // 2 - 1)))
            split_o_act(act, ("merged", l), [("merge_sum", l, KT // 2 - 1, 1)])

        def merge_dve(dve, l, c1):
            for j in range(KT // 2):
                for g in range(4):
                    dve_ahead(dve, c1 + 4 * j + g)
                dve.wait_ge(*done(("branch", l, j)))
                w = W[:, 2 * j:2 * j + 2, :]
                for g in range(3):
                    dve.wait_ge(*done(("gate", l, j, g, "read")))
                    t = GS[:, 14 + 2 * g:16 + 2 * g, :]
                    dst = w if g == 0 else (G2[:, g - 1])
                    if g and j:
                        dve.wait_ge(*done(("merge_sum", l, j - 1, g - 1)))
                    dve.tensor_tensor(dst, t, acc[g], ALU.mult).then_inc(*raised("gate_times_branch", ("merge", l, j, g)))
                for g in range(2):
                    dve.wait_ge(*done(("merge", l, j, g + 1)))
                    if g:
                        dve.wait_ge(*done(("merge_sum", l, j, 0)))
                    dve.tensor_tensor(w, w, G2[:, g], ALU.add).then_inc(*raised("merged", ("merge_sum", l, j, g)))
            split_o_dve(dve, ("merged", l), ("o_split", ("mix_out", l)))

        def mix1_pe(pe, l, c0):
            m = ("mix", l)
            in_pe(pe, m, c0, IN1)
            rope_pe(pe, ("rope", l), FEAT[:, 0:5, :], ("in", m, 2, "read"), "rotate")
            turn_pe(pe, ("v", l), [FEAT[:, 5, :]], ("in", m, 2, "read"))
            pe.wait_ge(*done(("pooled", l)))
            misc_free(pe)
            for t in range(2):
                mm = pe.matmul(misc[:, t, :], prm(f"w_pool{l}")[:, t * P:(t + 1) * P], SUMS[:, t, :],
                               start=True, stop=True)
            mm.then_inc(*raised("pool_mixed", ("pool_mixed", l)))
            Misc.read = ("pool_out", l)
            for b in range(2):
                q, k, v = mix1_heads(b)
                attend_pe(pe, ("att", l, b), q, k, v, [("kd", l), (("v", l), "copied")], (("att", l, b), "zero"))
            merge_pe(pe, l, c0 + IN1)
            out_pe(pe, ("mix_out", l), c0 + IN1 + GATE1)

        def mix1_act(act, l, c0):
            m = ("mix", l)
            in_act(act, m, c0, IN1, True)
            act.wait_ge(*done((("rope", l), 4, "done")))
            for g in range(2):
                for h in range(2):
                    ins = act.activation(KD[h * DH:(h + 1) * DH, g, :], FEAT[g * DH:(g + 1) * DH, 4, :], ACT.Copy)
            ins.then_inc(*raised("keys_doubled", ("kd", l)))
            turn_act(act, ("v", l), 1, VT[:, :, 0:P])
            act.wait_ge(*done(("pool_mixed", l)))
            for t in range(2):
                ins = act.activation(W[:, t, :], misc[:, t, :], ACT.Copy,
                                     scale=prm(f"pool_scale{l}")[:, t:t + 1])
            ins.then_inc(*raised("pool_out", ("pool_out", l)))
            for b in range(2):
                tag = ("att", l, b)
                sink_act(act, tag)
                attend_act(act, tag, busy=(("att", l, 0), "out") if b else None)
            split_o_act(act, m, [(("att", l, 1), "heads"), ("conv_out", l)])
            merge_act(act, l, c0 + IN1)
            out_act(act, ("mix_out", l), c0 + IN1 + GATE1)

        def mix1_dve(dve, l, c0):
            m = ("mix", l)
            in_dve(dve, m, c0, IN1, False)
            rope_dve(dve, ("rope", l), FEAT[:, 0:5, :], FEAT[:, 0:5, :], ("in", m, 2, "read"), 0, G2[:, 0])
            dve.wait_ge(*done(("in", m, 3, "read")))
            dve.memset(PT[:, :, :], 0.0).then_inc(*raised("pool_zero", ("pool_zero", l)))
            dve.wait_ge(*done(("pool_zero", l)))
            u = FEAT[:, POOL0:POOL0 + 2, :]
            dve.tensor_copy(PU[0][:, :, POOL_PAD:], u).then_inc(*raised("pool_sum", ("pool_sum", l, 0)))
            for n in range(4):
                src, dst, shift = PU[n % 2], PU[(n + 1) % 2], 1 << n
                dve.wait_ge(*done(("pool_sum", l, n)))
                if n:
                    dve.wait_ge(*done(("pool_pick", l, n - 1)))
                dve.tensor_tensor(dst[:, :, POOL_PAD:], src[:, :, POOL_PAD:],
                                  src[:, :, POOL_PAD - shift:POOL_PAD - shift + T], ALU.add)\
                    .then_inc(*raised("pool_sum", ("pool_sum", l, n + 1)))
                dve.wait_ge(*done(("pool_sum", l, n + 1)))
                half = slice((n % 2) * DH, (n % 2 + 1) * DH)
                cnt = prm("per_count").rearrange("p (a t) -> p a t", a=2)
                dve.tensor_tensor(SUMS[half, n // 2, :], dst[half, n // 2, POOL_PAD:], cnt[half, n // 2, :],
                                  ALU.mult).then_inc(*raised("pool_pick", ("pool_pick", l, n)))
            dve.wait_ge(*done(("pool_pick", l, 3)))
            dve.tensor_tensor(SUMS, SUMS, u, ALU.subtract).then_inc(*raised("pooled", ("pooled", l)))
            dve.wait_ge(*done(("in", m, 6, "read")))
            dve.memset(CV[:, :, 0:2], 0.0).then_inc(*raised("conv_pad_zeroed", ("cv_zero", l)))
            dve.tensor_tensor(CV[:, :, 2:], FEAT[:, 12:14, :], FEAT[:, 8:10, :], ALU.mult)\
                .then_inc(*raised("conv_input", ("cv_in", l)))
            dve.wait_ge(*done(("cv_in", l)))
            cw = prm(f"conv_w{l}")
            for tap in range(3):
                if tap:
                    dve.wait_ge(*done(("cv_tap", l, tap - 1)))
                for t in range(2):
                    k = cw[:, 3 * t + tap:3 * t + tap + 1]
                    src = CV[:, t, tap:tap + T]
                    dst = W[:, 6 + t, :]
                    if tap == 0:
                        ins = dve.tensor_scalar(dst, src, k, None, ALU.mult)
                    else:
                        ins = dve.scalar_tensor_tensor(out=dst, in0=src, scalar=k, in1=dst, op0=ALU.mult, op1=ALU.add)
                ins.then_inc(*raised("conv_tap", ("cv_tap", l, tap)))
            dve.wait_ge(*done(("cv_tap", l, 2)))
            dve.tensor_tensor(W[:, 6:8, :], W[:, 6:8, :], FEAT[:, 10:12, :], ALU.mult)\
                .then_inc(*raised("conv_out", ("conv_out", l)))
            dve.wait_ge(*done(("pool_mixed", l)))
            for b in range(2):
                tag = ("att", l, b)
                if b:
                    dve.wait_ge(*done((("att", l, 0), "heads")))
                zero_out_dve(dve, tag)
                attend_dve(dve, tag, prm("window"), sink=prm(f"sinks{l}")[:, 4 * b:4 * b + 4],
                           busy=(("att", l, 0), "turned") if b else None)
                heads_out_dve(dve, tag, 2 + 2 * b)
            split_o_dve(dve, m, ("o_split", m))
            merge_dve(dve, l, c0 + IN1)
            out_dve(dve, ("mix_out", l), c0 + IN1 + GATE1, True)

        def half(col):
            return FEAT[(col % 2) * DH:(col % 2 + 1) * DH, col // 2, :]

        PTf = PT[:, :, :].rearrange("p a b -> p (a b)")
        UPf = UP[:, :, :, :].rearrange("p a b c -> p (a b c)")
        G2f = G2[:, :, :, :].rearrange("p a b c -> p (a b c)")
        SHW = T + CMP_STRIDE
        NB = B_KV * NCMP
        SHIFT = {x: t[:, 0:B_KV * SHW].rearrange("p (g t) -> p g t", g=B_KV) for x, t in (("k", SMf), ("v", PTf))}
        BLOCKS = {x: t[:, 0:CMP_STRIDE * NB] for x, t in (("k", G2f), ("v", UPf))}
        OHf = OH[:, :, :].rearrange("p k t -> p (k t)")
        OLf = OL[:, :, :].rearrange("p k t -> p (k t)")
        VG = A
        RV = SIL[:, 0, :]
        GT = small[:, 64:64 + QT * 36].rearrange("p (r c) -> p r c", r=QT)
        GTh = small[:, 64:64 + QT * 36].rearrange("p (r h b) -> p b h r", r=QT, b=3)
        SMc = SMf[:, 0:4 * QT * NCMP]

        def ev_pe(pe, m, c0):
            in_pe(pe, m, c0, EV_IN)
            for n, x in enumerate("kv"):
                pe.wait_ge(*done(("blocks", x)))
                for j in range(2):
                    c = c0 + EV_IN + 2 * n + j
                    weights_ready(pe, c)
                    for o in range(2):
                        for k in range(KT):
                            w = slice(k * 2 * P + o * P, k * 2 * P + (o + 1) * P)
                            at0 = n * 768 + (j * KT + k) * NB
                            hi, lo = OHf[:, at0:at0 + NB], OLf[:, at0:at0 + NB]
                            dst = ACC[:, 2 * n + o, 0:NB]
                            s = c % RING
                            first, last = j == 0 and k == 0, j == 1 and k == KT - 1
                            pe.matmul(dst, w_high[:, s, w], hi, start=first, stop=False)
                            pe.matmul(dst, w_high[:, s, w], lo, start=False, stop=False)
                            mm = pe.matmul(dst, w_low[:, s, w], hi, start=False, stop=last)
                    mm.then_inc(*raised("panel_done", ("cmp", x, j)))
                    K.alias(("used", c), ("cmp", x, j))
            pe.wait_ge(*done(("v_squares",)))
            misc_free(pe)
            for t in range(2):
                mm = pe.matmul(MISC[:, 0:T], ones_v[:, :], W[:, 6 + t, :], start=t == 0, stop=t == 1)
            mm.then_inc(*raised("v_mean", ("v_mean",)))
            Misc.read = ("v_var",)
            turn_pe(pe, ("vg",), [W[:, 4, :], W[:, 5, :]], ("v_scaled",))
            pe.wait_ge(*done((("vg",), "copied")))
            for c in range(QT):
                for g in range(4):
                    mm = pe.matmul(misc[(g % 2) * DH:(g % 2 + 1) * DH, g // 2, c * P:(c + 1) * P],
                                   VG[:, c, g * DH:(g + 1) * DH], prm("sgu_w")[:, g * P:(g + 1) * P],
                                   start=True, stop=True)
            mm.then_inc(*raised("tokens_mixed", ("sgu",)))
            Misc.read = ("sgu_bias",)
            rope_pe(pe, ("rope_q", m), FEAT[:, 4:10, :], ("in", m, 9, "read"), "rotate")
            rope_pe(pe, ("rope_k", m), FEAT[:, 13:16, :], ("in", m, 9, "read"), "rotate")
            turn_pe(pe, ("v1",), [FEAT[:, 16, :], FEAT[:, 17, :]], ("in", m, 9, "read"))
            turn_pe(pe, ("v2",), [FEAT[:, 18, :], FEAT[:, 19, :]], ("in", m, 9, "read"))
            pe.wait_ge(*done(("hidden",)))
            misc_free(pe)
            w2k = prm("cmp_w2_k").rearrange("p (k c) -> p k c", k=2)
            w2v = prm("cmp_w2_v").rearrange("p (k c) -> p k c", k=2)
            for k in range(2):
                pe.matmul(MISC[:, 0:NB], w2k[:, k, :], HID[:, k, :], start=k == 0, stop=k == 1)
            for g in range(B_KV):
                for k in range(2):
                    mm = pe.matmul(MISC[0:NCMP, 64 + g * DH:64 + (g + 1) * DH],
                                   HID[:, 2 + k, g * NCMP:(g + 1) * NCMP], w2v[:, k, :], start=k == 0, stop=k == 1)
            mm.then_inc(*raised("compressed", ("compressed",)))
            Misc.read = ("kc",)
            for g in range(B_KV):
                hs = [((h % 2) * DH, (4 * g + h) // 2) for h in range(4)]
                q_raw = [FEAT[p:p + DH, 4 + t, :] for p, t in hs]
                q_rot = [QR[p:p + DH, t, :] for p, t in hs]
                tag = ("cmp_att", g)
                pe.wait_ge(*done(("kc",)))
                if Misc.accs is not None:
                    pe.wait_ge(*done(Misc.accs))
                for h in range(4):
                    for r in range(QT):
                        n = (h * QT + r) * NCMP
                        p = hs[h][0]
                        mm = pe.matmul(ACC[:, h, r * NCMP:(r + 1) * NCMP], q_raw[h][:, r * P:(r + 1) * P],
                                       KC[p:p + DH, g, :], start=True, stop=True)
                mm.then_inc(*raised("scores_done", (tag, "scores")))
                pe.wait_ge(*done((tag, "probs")))
                for h in range(4):
                    for r in range(QT):
                        n = (h * QT + r) * NCMP
                        mm = pe.transpose(ACC[0:NCMP, h, r * P:(r + 1) * P], SMc[:, n:n + NCMP], ident)
                mm.then_inc(*raised("turned", (tag, "turned")))
                pe.wait_ge(*done((tag, "copied")))
                pe.wait_ge(*done((("sel_att", g), "zero")))
                for h in range(4):
                    o = OUTP[(h % 2) * DH:(h % 2 + 1) * DH, (h // 2) * T:(h // 2 + 1) * T]
                    mm = pe.matmul(o, VC[0:NCMP, g, :], PT[0:NCMP, h, 0:T], start=False, stop=False,
                                   skip_group_check=True)
                mm.then_inc(*raised("attended", (tag, "out")))
                Misc.accs = (tag, "copied")
                for n, name in enumerate(("sel_att", "win_att")):
                    k = [KD[p:p + DH, 3 * n + g, :] for p, _ in hs]
                    attend_pe(pe, (name, g), q_rot, k,
                              lambda h, r, n=n, g=g: VT[:, r, (3 * n + g) * DH:(3 * n + g + 1) * DH],
                              [("kd", m), (("v1",), "copied"), (("v2",), "gates")], (("sel_att", g), "zero"))
            out_pe(pe, ("mix_out", m), c0 + EV_IN + CMP)

        def ev_act(act, m, c0):
            in_act(act, m, c0, EV_IN, False)
            act.wait_ge(*done(("in", m, 9, "read")))
            for n, x in enumerate("kv"):
                act.wait_ge(*done(("shift_zero",)))
                for g in range(B_KV):
                    src = half(20 + 3 * n + g)
                    act.activation(SHIFT[x][0:DH, g, 0:T], src, ACT.Copy)
                    ins = act.activation(SHIFT[x][DH:P, g, 0:T - CMP_STRIDE], src[:, CMP_STRIDE:], ACT.Copy)
                ins.then_inc(*raised("tokens_shifted", ("shift", x)))
                act.wait_ge(*done(("blocks_full", x)))
                act.activation(OHf[:, 768 * n:768 * (n + 1)], BLOCKS[x], ACT.Copy)\
                    .then_inc(*raised("blocks_high", ("blocks_high", x)))
            for j in range(CMP):
                act_ahead(act, c0 + EV_IN + j)
            act.activation(FEAT[:, 0:4, :], FEAT[:, 0:4, :], ACT.Gelu_apprx_tanh).then_inc(*raised("gelu", ("gelu",)))
            act.wait_ge(*done(("cmp", "v", 1)))
            act.activation(HID[:, :, :], ACC[:, :, 0:NB], ACT.Gelu_apprx_tanh)\
                .then_inc(*raised("hidden", ("hidden",)))
            act.wait_ge(*done(("gelu",)))
            act.activation(W[:, 6:8, :], FEAT[:, 2:4, :], ACT.Square).then_inc(*raised("v_squares", ("v_squares",)))
            act.wait_ge(*done(("v_var",)))
            act.activation(RV, RV, ACT.Sqrt).then_inc(*raised("v_root", ("v_root",)))
            turn_act(act, ("vg",), 2, VG[:, :, :])
            act.wait_ge(*done((("rope_k", m), 2, "done")))
            for n in range(6):
                for h in range(2):
                    ins = act.activation(KD[h * DH:(h + 1) * DH, n, :], half(26 + n), ACT.Copy)
            ins.then_inc(*raised("keys_doubled", ("kd", m)))
            turn_act(act, ("v1",), 2, VT[:, :, 0:2 * P])
            act.wait_ge(*done((("v2",), "turned")))
            mr = MISC[:, 0:512].rearrange("p (r c) -> p r c", r=QT)
            act.activation(VT[:, :, 2 * P:3 * P], mr[:, :, 0:P], ACT.Copy)
            act.activation(GT, mr[:, :, P:P + 36], ACT.Sigmoid).then_inc(*raised("v2_gates", (("v2",), "gates")))
            K.alias((("v2",), "copied"), (("v2",), "gates"))
            act.wait_ge(*done(("compressed",)))
            act.activation(KC[:, :, :], MISC[:, 0:NB].rearrange("p (g n) -> p g n", g=B_KV), ACT.Copy)
            act.activation(VC[0:NCMP, :, :], MISC[0:NCMP, 64:64 + B_KV * DH].rearrange("p (g d) -> p g d", g=B_KV),
                           ACT.Copy).then_inc(*raised("compressed_copied", ("kc",)))
            last = None
            for g in range(B_KV):
                tag = ("cmp_att", g)
                act.wait_ge(*done((tag, "less_max")))
                act.activation(SMc, SMc, ACT.Exp).then_inc(*raised("exps_ready", (tag, "exps")))
                act.wait_ge(*done((tag, "turned")))
                if last is not None:
                    act.wait_ge(*done((last, "out")))
                act.activation(PT[0:NCMP, :, 0:T], ACC[0:NCMP, :, 0:T], ACT.Copy)\
                    .then_inc(*raised("psum_copied", (tag, "copied")))
                attend_act(act, ("sel_att", g), busy=(tag, "out"))
                attend_act(act, ("win_att", g), busy=(("sel_att", g), "out"))
                last = ("win_att", g)
            split_o_act(act, m, [(last, "heads")])
            out_act(act, ("mix_out", m), c0 + EV_IN + CMP)

        def ev_dve(dve, m, c0):
            dve.memset(SM[:, :, :], 0.0).then_inc(*raised("shift_zero_k", ("shift_zero_k",)))
            dve.memset(PT[:, :, :], 0.0).then_inc(*raised("shift_zero", ("shift_zero",)))
            in_dve(dve, m, c0, EV_IN, True)
            for n, x in enumerate("kv"):
                dve.wait_ge(*done(("shift", x)))
                s, pos = SHIFT[x], prm(f"pos_{x}")
                for g in range(B_KV):
                    dst = BLOCKS[x].rearrange("p (l g n) -> p g l n", l=CMP_STRIDE, g=B_KV)[:, g]
                    src = s[:, g, 0:T].rearrange("p (n l) -> p l n", l=CMP_STRIDE)
                    ins = dve.tensor_tensor(dst, src, pos.rearrange("p (l n) -> p l n", n=1)
                                            .broadcast_to([P, CMP_STRIDE, NCMP]), ALU.add)
                ins.then_inc(*raised("blocks_full", ("blocks_full", x)))
                dve.wait_ge(*done(("blocks_high", x)))
                dve.tensor_tensor(OLf[:, 768 * n:768 * (n + 1)], BLOCKS[x],
                                  OHf[:, 768 * n:768 * (n + 1)].bitcast(F32), ALU.subtract)\
                    .then_inc(*raised("blocks", ("blocks", x)))
            for j in range(CMP):
                dve_ahead(dve, c0 + EV_IN + j)
            dve.wait_ge(*done(("v_mean",)))
            dve.tensor_scalar(RV, MISC[:, 0:T], RMS_EPS, None, ALU.add).then_inc(*raised("v_var", ("v_var",)))
            dve.wait_ge(*done(("v_root",)))
            dve.reciprocal(RV, RV).then_inc(*raised("v_rstd", ("v_rstd",)))
            dve.wait_ge(*done(("v_rstd",)))
            for t in range(2):
                ins = dve.scalar_tensor_tensor(out=W[:, 4 + t, :], in0=FEAT[:, 2 + t, :],
                                               scalar=prm("sgu_norm")[:, t:t + 1], in1=RV, op0=ALU.mult, op1=ALU.mult)
            ins.then_inc(*raised("v_scaled", ("v_scaled",)))
            dve.wait_ge(*done(("sgu",)))
            for t in range(2):
                ins = dve.tensor_tensor(W[:, t, :].rearrange("p (c s) -> p c s", c=QT),
                                        misc[:, t, :].rearrange("p (c s) -> p c s", c=QT),
                                        over(prm("sgu_b")[:, t * P:(t + 1) * P], QT), ALU.add)
            ins.then_inc(*raised("sgu_bias", ("sgu_bias",)))
            dve.wait_ge(*done(("sgu_bias",)))
            dve.tensor_tensor(W[:, 0:2, :], W[:, 0:2, :], FEAT[:, 0:2, :], ALU.mult)\
                .then_inc(*raised("gmlp", ("gmlp",)))
            rope_dve(dve, ("rope_q", m), FEAT[:, 4:10, :], QR[:, :, :], ("in", m, 9, "read"), 0, G2[:, 0])
            dve.wait_ge(*done((("rope_q", m), 4, "done")))
            rope_dve(dve, ("rope_k", m), FEAT[:, 13:16, :], FEAT[:, 13:16, :], ("in", m, 9, "read"), 0, G2[:, 0])
            last = None
            dve.wait_ge(*done((("v2",), "gates")))
            for g in range(B_KV):
                tag = ("cmp_att", g)
                if last is not None:
                    dve.wait_ge(*done((last, "heads")))
                zero_out_dve(dve, ("sel_att", g))
                dve.wait_ge(*done((tag, "scores")))
                if last is not None:
                    dve.wait_ge(*done((last, "turned")))
                S = SMc.rearrange("p (h x) -> p h x", h=4)
                S8 = SMc.rearrange("p (e n) -> p e n", n=NCMP)
                dve.scalar_tensor_tensor(out=S, in0=ACC[:, :, 0:QT * NCMP], scalar=SCALE,
                                         in1=over(prm("cmp_mask"), 4), op0=ALU.mult, op1=ALU.add)\
                    .then_inc(*raised("scores_masked", (tag, "masked")))
                dve.wait_ge(*done((tag, "masked")))
                dve.tensor_reduce(MX, S8, AX.X, ALU.max).then_inc(*raised("row_max", (tag, "mx")))
                dve.wait_ge(*done((tag, "mx")))
                dve.tensor_tensor(S8, S8, MX.rearrange("p (e n) -> p e n", n=1).broadcast_to([P, 8, NCMP]),
                                  ALU.subtract).then_inc(*raised("less_max", (tag, "less_max")))
                dve.wait_ge(*done((tag, "exps")))
                dve.tensor_reduce(SU, S8, AX.X, ALU.add).then_inc(*raised("row_sum", (tag, "sum")))
                dve.wait_ge(*done((tag, "sum")))
                any_r = over(prm("cmp_any"), 4)
                RCr = RC.rearrange("p (h r) -> p h r", r=QT)
                dve.reciprocal(RC, SU).then_inc(*raised("sum_inverted", (tag, "rc")))
                dve.wait_ge(*done((tag, "rc")))
                dve.tensor_tensor(RCr, RCr, any_r, ALU.mult).then_inc(*raised("empty_rows_cleared", (tag, "rc_any")))
                dve.wait_ge(*done((tag, "rc_any")))
                dve.tensor_tensor(RCr, RCr, GTh[:, 0, 4 * g:4 * g + 4, :], ALU.mult)\
                    .then_inc(*raised("gate_applied", (tag, "gated")))
                dve.wait_ge(*done((tag, "gated")))
                dve.tensor_tensor(S8, S8, RC.rearrange("p (e n) -> p e n", n=1).broadcast_to([P, 8, NCMP]),
                                  ALU.mult).then_inc(*raised("probs_ready", (tag, "probs")))
                for n, name in enumerate(("sel_att", "win_att")):
                    attend_dve(dve, (name, g), prm("causal"), gate=GTh[:, 1 + n, 4 * g:4 * g + 4, :],
                               busy=(tag, "turned") if n == 0 else (("sel_att", g), "turned"))
                last = ("win_att", g)
                heads_out_dve(dve, last, 2 + 2 * g)
            split_o_dve(dve, m, ("o_split", ("mix_out", m)))
            out_dve(dve, ("mix_out", m), c0 + EV_IN + CMP, False)

        VW = SIL
        SC, WK = PT[:, 0, :], PT[:, 1, :]
        M8 = [small[:, 40:48], small[:, 48:56]]
        DMASK = A[:, :, :].rearrange("p a t -> p (a t)")[:, 0:SEQ_K]
        KEYS = ((0, P), (P, SEQ_K))

        def od_heads(n, m):
            first = 4 * (n % 2)
            base = 0 if n < 2 else 8
            ps = [((h % 2) * DH, (first + h) // 2) for h in range(4)]
            q = [FEAT[p:p + DH, base + t, :] for p, t in ps]
            k = [FEAT[p:p + DH, 4 if n < 2 else 12 + t, :] for p, t in ps]
            v = (lambda h, r: VW[:, r, 0:DH]) if n < 2 else \
                (lambda h, r: VT[:, r, (first + h) * DH:(first + h + 1) * DH])
            return q, k, v

        def od_pe(pe, m, c0):
            in_pe(pe, m, c0, OD_IN)
            after = ("in", m, 9, "read")
            rope_pe(pe, ("rope_i", m), FEAT[:, 6:8, :], after, "rotate_i")
            turn_pe(pe, ("vw",), [FEAT[:, 5, :]], after)
            pe.wait_ge(*done((("rope_i", m), 0, "done")))
            for h in range(IDX_HEADS):
                for r, (lo, hi) in enumerate(KEYS):
                    p = slice(h * IDX_DIM, (h + 1) * IDX_DIM)
                    mm = pe.matmul(ACC[:, h, lo:hi], FEAT[p, 6, r * P:(r + 1) * P], FEAT[p, 7, 0:hi - lo],
                                   start=True, stop=True)
            mm.then_inc(*raised("scores_done", ("index",)))
            Misc.accs = ("index_relu",)
            rope_pe(pe, ("rope_c", m), FEAT[:, 0:5, :], after, "rotate")
            rope_pe(pe, ("rope_d", m), FEAT[:, 8:16, :], after, "rotate")
            for n in range(2):
                turn_pe(pe, ("vd", n), [FEAT[:, 16 + 2 * n, :], FEAT[:, 17 + 2 * n, :]], after)
            for n in range(4):
                q, k, v = od_heads(n, m)
                attend_pe(pe, ("od", n), q, k, v,
                          [(("rope_c", m), 4, "done"), (("rope_d", m), 6, "done"), (("vd", 1), "copied")],
                          (("od", n), "zero"))
            out_pe(pe, ("mix_out", m), c0 + OD_IN)

        def od_act(act, m, c0):
            in_act(act, m, c0, OD_IN, False)
            turn_act(act, ("vw",), 1, VW[:, :, 0:P])
            act.wait_ge(*done(("index",)))
            act.activation(SM[:, :, :], ACC[:, :, 0:SEQ_K], ACT.Relu, scale=IDX_DIM ** -0.5)\
                .then_inc(*raised("index_relu", ("index_relu",)))
            for n in range(2):
                turn_act(act, ("vd", n), 2, VT[:, :, 2 * n * P:2 * (n + 1) * P])
            for n in range(4):
                attend_act(act, ("od", n), busy=(("od", n - 1), "out") if n else ("selected",))
            split_o_act(act, m, [(("od", 3), "heads")])
            out_act(act, ("mix_out", m), c0 + OD_IN)

        def od_dve(dve, m, c0):
            in_dve(dve, m, c0, OD_IN, True)
            after = ("in", m, 9, "read")
            rope_dve(dve, ("rope_i", m), FEAT[:, 6:8, :], FEAT[:, 6:8, :], after, 2, G2[:, 0])
            dve.wait_ge(*done((("rope_i", m), 0, "done")))
            rope_dve(dve, ("rope_c", m), FEAT[:, 0:5, :], FEAT[:, 0:5, :], after, 0, G2[:, 1])
            dve.wait_ge(*done((("rope_c", m), 4, "done")))
            rope_dve(dve, ("rope_d", m), FEAT[:, 8:16, :], FEAT[:, 8:16, :], after, 0, G2[:, 0])
            dve.wait_ge(*done((("vw",), "copied")))
            dve.wait_ge(*done(("index_relu",)))
            for h in range(IDX_HEADS):
                if h:
                    dve.wait_ge(*done(("index_sum", h - 1)))
                for r, (lo, hi) in enumerate(KEYS):
                    w = VW[:, r, DH + h:DH + h + 1]
                    if h == 0:
                        ins = dve.tensor_scalar(SC[:, lo:hi], SM[:, h, lo:hi], w, None, ALU.mult)
                    else:
                        ins = dve.scalar_tensor_tensor(out=SC[:, lo:hi], in0=SM[:, h, lo:hi], scalar=w,
                                                       in1=SC[:, lo:hi], op0=ALU.mult, op1=ALU.add)
                ins.then_inc(*raised("index_sum", ("index_sum", h)))
            dve.wait_ge(*done(("index_sum", IDX_HEADS - 1)))
            dve.scalar_tensor_tensor(out=WK, in0=SC, scalar=IDX_HEADS ** -0.5, in1=prm("causal"),
                                     op0=ALU.mult, op1=ALU.add)\
                .then_inc(*raised("index_score", ("index_score",)))
            dve.wait_ge(*done(("index_score",)))
            for n in range(TOPK // 8):
                for r, (lo, hi) in enumerate(KEYS):
                    if n:
                        dve.wait_ge(*done(("taken", n - 1, r)))
                    dve.max(M8[r], WK[:, lo:hi]).then_inc(*raised("top_8_found", ("top8", n, r)))
                for r, (lo, hi) in enumerate(KEYS):
                    dve.wait_ge(*done(("top8", n, r)))
                    dve.match_replace(WK[:, lo:hi], M8[r], WK[:, lo:hi], TAKEN)\
                        .then_inc(*raised("top_8_taken", ("taken", n, r)))
            dve.wait_ge(*done(("taken", TOPK // 8 - 1, 1)))
            dve.tensor_scalar(DMASK, WK, TAKEN / 2, NEG, ALU.is_gt, ALU.mult)\
                .then_inc(*raised("not_taken", ("not_taken",)))
            dve.wait_ge(*done(("not_taken",)))
            dve.tensor_tensor(DMASK, DMASK, prm("causal"), ALU.add).then_inc(*raised("selected", ("selected",)))
            dve.wait_ge(*done(("selected",)))
            for n in range(4):
                tag = ("od", n)
                if n:
                    dve.wait_ge(*done((("od", n - 1), "heads")))
                zero_out_dve(dve, tag)
                attend_dve(dve, tag, DMASK if n < 2 else prm("causal"), busy=(("od", n - 1), "turned") if n else None)
                heads_out_dve(dve, tag, 2 * n)
            split_o_dve(dve, m, ("o_split", ("mix_out", m)))
            out_dve(dve, ("mix_out", m), c0 + OD_IN, False)

        HID = sb("HID", [P, 4, NB])
        KC = sb("KC", [P, B_KV, NCMP])
        VC = sb("VC", [P, B_KV, DH])
        c = 0
        stages = []
        for l in range(DEPTH):
            stages.append(("mix1", l, c))
            c += IN1 + GATE1 + OUT
            stages.append(("ffn1", l, c))
            c += FFN_CHUNKS
        for l in range(DEPTH):
            stages.append(("ffn2", 2 + 2 * l, c))
            c += FFN_CHUNKS
            stages.append(("ev" if l % 2 == 0 else "od", l, c))
            c += (EV_IN + CMP if l % 2 == 0 else OD_IN) + OUT
            stages.append(("ffn2", 3 + 2 * l, c))
            c += FFN_CHUNKS
        assert c == n_chunks, (c, n_chunks)

        M2 = {l: ("mix2", l) for l in range(DEPTH)}

        @block.sync
        def _(sp):
            sp.dma_start(X[:, :, :], x_in).then_inc(*raised("x_loaded", "x_loaded", 16))
            sp.dma_start(PRM[:, :], params).then_inc(*raised("params_loaded", "params_loaded", 16))
            sp.dma_start(posi[:, 0, :], pos1.partition_broadcast(P)).then_inc(K.sem("positions_loaded"), 16)
            sp.dma_start(posi[:, 1, :], pos2.partition_broadcast(P)).then_inc(K.sem("positions_loaded"), 16)
            for s in range(RING):
                sp.dma_start(raw[:, s, :], weights[s]).then_inc(K.sem(f"chunk_loaded{s}"), 16)
            turns = n_chunks // RING
            with sp.Fori(1, turns) as i:
                for s in range(RING):
                    sp.wait_ge(K.sem("w_low_ready"), i * RING + (s + 1 - RING))
                    sp.dma_start(raw[:, s, :], weights[bass.ds(i * RING + s, 1)]
                                 .rearrange("a p c -> (a p) c")).then_inc(K.sem(f"chunk_loaded{s}"), 16)
            for cc in range(turns * RING, n_chunks):
                sp.wait_ge(K.sem("w_low_ready"), cc + 1 - RING)
                sp.dma_start(raw[:, cc % RING, :], weights[cc]).then_inc(K.sem(f"chunk_loaded{cc % RING}"), 16)
            sp.wait_ge(*done("result"))
            sp.dma_start(out, W[:, :, :]).then_inc(K.sem("out_stored"), 16)
            sp.wait_ge(K.sem("out_stored"), 16)

        @block.gpsimd
        def _(pool):
            pool.memset(ones_d[:, :], 1.0 / D).then_inc(*raised("constants_set", "ones_d"))
            pool.memset(ones_v[:, :], 1.0 / 256).then_inc(*raised("constants_set", "ones_v"))
            pool.memset(UP[:, :, :, 0:2], 0.0).then_inc(*raised("constants_set", "up_zero"))
            pool.wait_ge(*done("params_loaded"))
            w = prm("sgu_w").rearrange("p (g t) -> p g t", g=4)
            pool.affine_select(out=w, in_=w, compare_op=ALU.is_ge, fill=0.0, base=0,
                               pattern=[[0, 4], [1, P]], channel_multiplier=-1)\
                .then_inc(*raised("constants_set", "sgu_masked"))

        def rope_tables_dve(dve, stack):
            two_pi = 2 * np.pi
            c1 = 6.28125
            c2 = float(np.float32(np.round((two_pi - c1) * 2 ** 22) / 2 ** 22))
            c3 = two_pi - c1 - c2
            dve.wait_ge(K.sem("positions_loaded"), 32)
            tag = ("tables", stack)
            n = [0]

            def step(ins):
                ins.then_inc(*raised("table_step", (tag, n[0])))
                dve.wait_ge(*done((tag, n[0])))
                n[0] += 1

            step(dve.tensor_copy(posf, posi[:, stack, :]))
            for which, f in enumerate(("freq", "freq_i")[:1 + stack]):
                ang, turn = W[:, 4, :], W[:, 5, :]
                step(dve.tensor_scalar(ang, posf, prm(f), None, ALU.mult))
                step(dve.tensor_scalar(turn, ang, 1 / two_pi, 12582912.0, ALU.mult, ALU.add))
                step(dve.tensor_scalar(turn, turn, -12582912.0, None, ALU.add))
                for part in (c1, c2, c3):
                    step(dve.scalar_tensor_tensor(out=ang, in0=turn, scalar=-part, in1=ang, op0=ALU.mult, op1=ALU.add))
                step(dve.tensor_scalar(turn, ang, np.pi / 2, -two_pi, ALU.is_gt, ALU.mult))
                step(dve.scalar_tensor_tensor(out=turn, in0=ang, scalar=np.pi / 2, in1=turn, op0=ALU.add, op1=ALU.add))
                lim = 3.1415925
                step(dve.tensor_scalar(W[:, 2 * which, :], turn, lim, -lim, ALU.min, ALU.max))
                dve.tensor_scalar(W[:, 2 * which + 1, :], ang, lim, -lim, ALU.min, ALU.max)\
                    .then_inc(*raised("angles", (tag, "angles", which)))
                dve.wait_ge(*done((tag, "angles", which)))

        def rope_tables_act(act, stack):
            for which in range(1 + stack):
                act.wait_ge(*done((("tables", stack), "angles", which)))
                ins = act.activation(ropes[:, 2 * which:2 * which + 2, :], W[:, 2 * which:2 * which + 2, :], ACT.Sin)
            ins.then_inc(*raised("tables_done", ("tables", stack, "done")))

        @block.tensor
        def _(pe):
            pe.wait_ge(*done("params_loaded"))
            pe.wait_ge(*done("ones_v"))
            for kind, n, c0 in stages:
                if kind == "mix1":
                    mix1_pe(pe, n, c0)
                    ln_pe(pe, ("mix_out", n))
                elif kind == "ffn1":
                    ffn_pe(pe, n, c0)
                    ln_pe(pe, n)
                    if n == DEPTH - 1:
                        rms_pe(pe, "stack2")
                elif kind == "ffn2":
                    ffn_pe(pe, n, c0)
                    rms_pe(pe, n)
                elif kind == "ev":
                    pe.wait_ge(*done("sgu_masked"))
                    ev_pe(pe, M2[n], c0)
                    rms_pe(pe, ("mix_out", M2[n]))
                else:
                    od_pe(pe, M2[n], c0)
                    rms_pe(pe, ("mix_out", M2[n]))

        def norms(kind, n):
            if kind == "ffn2":
                if n == 5:
                    return n, None, "final_norm"
                return (n, M2[0], "mix_norm0") if n == 2 else (n, 4, "ffn1_norm1") if n == 3 else (n, M2[1], "mix_norm1")
            return ("mix_out", M2[n]), 3 + 2 * n, f"ffn2_norm{n}"

        @block.scalar
        def _(act):
            act.wait_ge(*done("x_loaded"))
            act.activation(XH[:, :, :], X[:, :, :], ACT.Copy).then_inc(*raised("x_high", ("x_high", ("mix", 0))))
            split_high(act, 0)
            split_high(act, 1)
            act.wait_ge(*done("params_loaded"))
            rope_tables_act(act, 0)
            act.wait_ge(*done("up_zero"))
            for kind, n, c0 in stages:
                if kind == "mix1":
                    mix1_act(act, n, c0)
                    ln_act(act, ("mix_out", n), n, f"ln1_g{n}", f"ln1_b{n}")
                elif kind == "ffn1":
                    ffn_act(act, n, c0, n)
                    last = n == DEPTH - 1
                    ln_act(act, n, None if last else ("mix", n + 1), f"ln2_g{n}", f"ln2_b{n}")
                    if last:
                        rms_act(act, "stack2", 2, "ffn1_norm0")
                        rope_tables_act(act, 1)
                else:
                    if kind == "ffn2":
                        ffn_act(act, n, c0, None)
                    elif kind == "ev":
                        ev_act(act, M2[n], c0)
                    else:
                        od_act(act, M2[n], c0)
                    rms_act(act, *norms(kind, n))

        @block.vector
        def _(dve):
            dve.wait_ge(*done(("x_high", ("mix", 0))))
            dve.tensor_tensor(XL[:, :, :], X[:, :, :], XH[:, :, :].bitcast(F32), ALU.subtract)\
                .then_inc(*raised("x_split", ("x_split", ("mix", 0))))
            split_low(dve, 0)
            split_low(dve, 1)
            dve.wait_ge(*done("params_loaded"))
            rope_tables_dve(dve, 0)
            dve.wait_ge(*done(("tables", 0, "done")))
            for kind, n, c0 in stages:
                if kind == "mix1":
                    mix1_dve(dve, n, c0)
                    ln_dve(dve, ("mix_out", n), n, f"ln1_g{n}", f"ln1_b{n}")
                elif kind == "ffn1":
                    ffn_dve(dve, n, c0, n)
                    residual_from_acc(dve, n, True)
                    last = n == DEPTH - 1
                    ln_dve(dve, n, None if last else ("mix", n + 1), f"ln2_g{n}", f"ln2_b{n}")
                    if last:
                        rms_dve(dve, "stack2", 2, "ffn1_norm0")
                        dve.wait_ge(*done(("sums", "stack2")))
                        rope_tables_dve(dve, 1)
                        dve.wait_ge(*done(("tables", 1, "done")))
                else:
                    if kind == "ffn2":
                        ffn_dve(dve, n, c0, None)
                        residual_from_acc(dve, n, False)
                    elif kind == "ev":
                        ev_dve(dve, M2[n], c0)
                    else:
                        od_dve(dve, M2[n], c0)
                    rms_dve(dve, *norms(kind, n))
            for k in range(KT):
                ins = dve.scalar_tensor_tensor(out=W[:, k, :], in0=X[:, k, :], scalar=prm("final_norm")[:, k:k + 1],
                                               in1=RS[:, :], op0=ALU.mult, op1=ALU.mult)
            ins.then_inc(*raised("result_ready", "result"))
        return K.now


def kernel(**inputs):
    import concourse.bacc as bacc
    from concourse.bass_utils import run_bass_kernel_spmd

    a = {k: np.asarray(v) for k, v in inputs.items()}
    params, at = small_parameters(a)
    arrays = {
        "weights": weight_stream(a),
        "params": params,
        "x_in": np.ascontiguousarray(a["x"][0].T.reshape(KT, P, T).transpose(1, 0, 2)),
        "pos1": np.ascontiguousarray(a["positions"].reshape(T)),
        "pos2": np.ascontiguousarray(a["positions_2"].reshape(T)),
    }
    seen = None
    for _ in range(2):
        nc = bacc.Bacc("TRN2", target_bir_lowering=False, num_devices=1)
        aps = {n: nc.dram_tensor(n, v.shape, mybir.dt.from_np(v.dtype), kind="ExternalInput").ap()
               for n, v in arrays.items()}
        out = nc.dram_tensor("out", (P, KT, T), F32, kind="ExternalOutput").ap()
        seen = build(nc, at=at, out=out, seen=seen, **aps)
    r = run_bass_kernel_spmd(nc, [arrays], core_ids=[0])
    got = r.results[0]["out"]
    return np.ascontiguousarray(got.transpose(2, 1, 0)).reshape(1, T, D)
```

```python
from contextlib import ExitStack, contextmanager

import numpy as np

import concourse.bass as bass
from concourse import mybir

F32 = mybir.dt.float32
F32R = mybir.dt.float32r
I32 = mybir.dt.int32
ALU = mybir.AluOpType
ACT = mybir.ActivationFunctionType
AX = mybir.AxisListType

P = 128
D = 1024
KT = D // P
T = 256
QT = T // P
DEPTH = 2
DH = 64
D_FF = 2816
FT = D_FF // P
CH = 2048
RING = 3
PAIRS = FT // 2
FFN_CHUNKS = FT + PAIRS
ALPHA = (2 * DEPTH) ** 0.25
LN_EPS = 1e-5
RMS_EPS = 1e-6
NEG = -1e30
TAKEN = -3e38
TOPK = min(256, T // 4)
SCALE = DH ** -0.5
IDX_HEADS, IDX_DIM = 4, 32
B_HEADS, B_KV = 12, 3
CMP_LEN, CMP_STRIDE = 32, 16
NCMP = T // CMP_STRIDE
SEQ_K = T + P
POOL_PAD = 16
ROPE_THETA = 500000.0

IN1, GATE1, OUT = 7, 16, 4
EV_IN, CMP, OD_IN = 10, 4, 10
EV_ORDER, EV_EARLY = (1, 0, 5, 6, 7, 8, 9, 2, 3, 4), 7
OD_ORDER = (3, 2, 0, 1, 4, 6, 5, 7, 8, 9)


def panel(w):
    return w.reshape(KT, P, 2 * P).transpose(1, 0, 2).reshape(P, CH)


def down_pair(w):
    return w.reshape(2, P, D).transpose(1, 0, 2).reshape(P, CH)


def per_partition(v):
    return v.reshape(-1, P).T


def ffn_chunks(a, b, down):
    u = [panel(np.concatenate([a[:, j * P:(j + 1) * P], b[:, j * P:(j + 1) * P]], 1)) for j in range(FT)]
    d = [down_pair(down[2 * P * m:2 * P * (m + 1)]) for m in range(PAIRS)]
    out = u[:2]
    for m in range(PAIRS - 1):
        out += [u[2 * m + 2], d[m], u[2 * m + 3]]
    return out + [d[-1]]


def panels(w):
    return [panel(w[:, c:c + 2 * P]) for c in range(0, w.shape[1], 2 * P)]


def weight_stream(a):
    s = []
    for l in range(DEPTH):
        w = a["w_in"][l]
        pool, q, k, v, xc, gb, gc, gates = np.split(w, np.cumsum([256, 512, 128, 128, 256, 256, 256]), 1)
        s += panels(np.concatenate([q, k, v, pool, xc, gc, gb], 1))
        branch = np.concatenate([a["w_branch_a"][l], a["w_branch_b"][l], a["w_branch_c"][l]], 0)
        for j in range(KT // 2):
            cols = slice(2 * P * j, 2 * P * (j + 1))
            s += [panel(gates[:, b * D:(b + 1) * D][:, cols]) for b in range(3)] + [panel(branch[:, cols])]
        s += panels(a["w_o"][l])
        s += ffn_chunks(a["w_up"][l][:, :D_FF], a["w_up"][l][:, D_FF:], a["w_down"][l])
    for l in range(DEPTH):
        for n in (1, 2):
            if n == 2:
                if l % 2 == 0:
                    z, q, kc, vc, ks, vs, kw, vw, gl = np.split(
                        a["ev_w_in_2"][0], np.cumsum([512, 768] + [192] * 6), 1)
                    fill = np.zeros((D, P - gl.shape[1]), np.float32)
                    into = panels(np.concatenate([z, q, kc, vc, ks, kw, vs, vw, gl, fill], 1))
                    s += [into[j] for j in EV_ORDER[:EV_EARLY]]
                    for x in "kv":
                        w1 = a[f"ev_cmp_w1_{x}_2"][0].reshape(2, CMP_STRIDE, DH, 256)
                        w1 = w1.transpose(1, 0, 2, 3).reshape(2 * D, 256)
                        s += [panel(w1[:D]), panel(w1[D:])]
                    s += [into[j] for j in EV_ORDER[EV_EARLY:]]
                    s += panels(a["ev_w_out_2"][0])
                else:
                    q, kc, vc, qi, ki, wi, qd, kd, vd = np.split(
                        a["od_w_in_2"][0], np.cumsum([512, 64, 64, 128, 32, 4, 512, 512]), 1)
                    fill = np.zeros((D, P - 68), np.float32)
                    into = panels(np.concatenate([q, kc, kc, vc, wi, fill, qi, ki, ki, ki, ki, qd, kd, vd], 1))
                    s += [into[j] for j in OD_ORDER]
                    s += panels(a["od_w_out_2"][0])
            s += ffn_chunks(a[f"ffn{n}_w_gate_2"][l], a[f"ffn{n}_w_up_2"][l], a[f"ffn{n}_w_down_2"][l])
    return np.stack(s)


def small_parameters(a):
    p = np.arange(P)
    t = np.arange(T)
    c = {"ident": np.eye(P)}
    for name, dim, half in (("rotate", DH, 8), ("rotate_i", IDX_DIM, 4)):
        r = np.zeros((P, P))
        for i in p:
            if i % dim < half:
                r[i, i + half] = -1
            elif i % dim < 2 * half:
                r[i, i - half] = 1
        c[name] = r.T
        freq = np.float32(ROPE_THETA) ** (-np.arange(0, 2 * half, 2, dtype=np.float32) / np.float32(2 * half))
        c["freq" + name[6:]] = np.where(p % dim < 2 * half, freq[(p % dim) % half], 0)[:, None]
    causal = np.where(t[None] <= p[:, None], 0, NEG)
    later = np.where(t[None] <= p[:, None] + P, 0, NEG)
    window = np.where((t[None] <= p[:, None] + P) & (t[None] > p[:, None]), 0, NEG)
    c["causal"] = np.concatenate([causal[:, :P], later], 1)
    c["window"] = np.concatenate([causal[:, :P], window], 1)
    n = np.arange(NCMP)
    tok = p[:, None, None] + P * np.arange(QT)[None, :, None]
    ok = (n * CMP_STRIDE + CMP_LEN - 1 <= tok) & (n * CMP_STRIDE + CMP_LEN <= T)
    c["cmp_mask"] = np.where(ok, 0, NEG).reshape(P, QT * NCMP)
    c["cmp_any"] = ok.any(-1)
    win = np.array([[2, 8], [4, 16]])[p // DH]
    c["per_count"] = (1 / np.minimum(t + 1, win[..., None])).reshape(P, 2 * T)
    for l in range(DEPTH):
        wp = np.zeros((P, 2, P), np.float32)
        for g in range(4):
            b = DH * (g % 2)
            wp[b:b + DH, g // 2, b:b + DH] = a["w_pool"][l, g]
        c[f"w_pool{l}"] = wp.reshape(P, 2 * P)
        c[f"pool_scale{l}"] = per_partition(a["pool_scale"][l])
        c[f"sinks{l}"] = np.broadcast_to(a["attn_sinks"][l], (P, 8))
        c[f"conv_w{l}"] = a["conv_w"][l].reshape(3, 2, P).transpose(2, 1, 0).reshape(P, 6)
        c[f"ffn_conv{l}"] = a["ffn_conv_w"][l].reshape(3, 2, FT, P).transpose(3, 2, 1, 0).reshape(P, FT * 6)
        for x in ("ln1_g", "ln1_b", "ln2_g", "ln2_b"):
            c[f"{x}{l}"] = per_partition(a[x][l])
        for x in ("ffn1_norm", "mix_norm", "ffn2_norm"):
            c[f"{x}{l}"] = per_partition(a[x + "_2"][l])
    c["final_norm"] = per_partition(a["final_norm_2"])
    c["sgu_norm"] = per_partition(a["ev_sgu_norm_2"][0])
    c["sgu_w"] = a["ev_sgu_w_2"][0].transpose(2, 0, 1).reshape(P, 4 * P)
    c["sgu_b"] = np.repeat(a["ev_sgu_b_2"][0].reshape(2, 2, P), DH, 1).transpose(1, 0, 2).reshape(P, 2 * P)
    for x in "kv":
        c[f"pos_{x}"] = a[f"ev_cmp_pos_{x}_2"][0].reshape(2, CMP_STRIDE, DH).transpose(0, 2, 1).reshape(P, CMP_STRIDE)
    w2 = a["ev_cmp_w2_k_2"][0].reshape(2, P, DH).transpose(1, 0, 2)
    c["cmp_w2_k"] = np.concatenate([w2, w2], 2).reshape(P, 2 * P)
    c["cmp_w2_v"] = a["ev_cmp_w2_v_2"][0].reshape(2, P, DH).transpose(1, 0, 2).reshape(P, 2 * DH)
    at, off = {}, 0
    for name, v in c.items():
        at[name] = (off, v.shape[1])
        off += v.shape[1]
    return np.concatenate([np.asarray(v, np.float32) for v in c.values()], 1), at


class Counts:

    def __init__(self, nc, ctx, seen):
        self.nc, self.ctx, self.seen = nc, ctx, seen
        self.sems, self.total, self.now, self.loop = {}, {}, {}, None

    def sem(self, name):
        if name not in self.sems:
            self.sems[name] = self.ctx.enter_context(self.nc.semaphore(name))
        return self.sems[name]

    def raised(self, name, event, by=1):
        assert event not in self.now, event
        self.total[name] = self.total.get(name, 0) + by
        self.now[event] = (name, self.total[name], 0, 1)
        if self.loop is not None:
            self.loop.append(event)
        return self.sem(name), by

    def alias(self, event, other):
        self.now[event] = self.now[other]
        if self.loop is not None:
            self.loop.append(event)

    @contextmanager
    def fori(self, eng, n):
        start = dict(self.total)
        self.loop = []
        with eng.Fori(0, n) as i:
            yield i
        for event in self.loop:
            name, count, _, _ = self.now[event]
            self.now[event] = (name, count, self.total[name] - start.get(name, 0), n)
        for name, count in self.total.items():
            self.total[name] = start.get(name, 0) + n * (count - start.get(name, 0))
        self.loop = None

    def done(self, event, i=None, lag=0):
        if self.seen is None:
            return self.sem("first_build"), 1
        name, count, slope, n = self.seen[event]
        if i is None or not slope:
            return self.sem(name), count + slope * (n - 1)
        assert count - lag * slope > 0, event
        return self.sem(name), i * slope + (count - lag * slope)


def build(nc, weights, params, at, x_in, pos1, pos2, out, seen):
    n_chunks = weights.shape[0]
    with ExitStack() as ctx:
        def sb(name, shape, dt=F32):
            return ctx.enter_context(nc.sbuf_tensor(name, shape, dt))

        K = Counts(nc, ctx, seen)
        done, raised = K.done, K.raised

        raw = sb("raw", [P, RING, CH])
        w_high = sb("w_high", [P, RING, CH], F32R)
        w_low = sb("w_low", [P, RING, CH], F32R)
        X = sb("X", [P, KT, T])
        XH = sb("XH", [P, KT, T], F32R)
        XL = sb("XL", [P, KT, T], F32R)
        OH = sb("OH", [P, KT, T], F32R)
        OL = sb("OL", [P, KT, T], F32R)
        W = sb("W", [P, KT, T])
        RS = sb("RS", [P, T])
        FEAT = sb("FEAT", [P, 20, T])
        QR = sb("QR", [P, 6, T])
        KD = sb("KD", [P, 6, T])
        VT = sb("VT", [P, QT, 512])
        PRM = sb("PRM", [P, params.shape[1]])
        ropes = sb("ropes", [P, 4, T])
        ones_d = sb("ones_d", [P, P])
        ones_v = sb("ones_v", [P, P])
        posi = QR[:, 0:2, :].bitcast(I32)
        posf = W[:, 7, :]
        ROT = W[:, 2:4, :]
        small = sb("small", [P, 144])
        SM = sb("SM", [P, 4, SEQ_K])
        PT = sb("PT", [P, 4, SEQ_K])
        UP = sb("UP", [P, 2, 2, T + 2])
        G2 = sb("G2", [P, 2, 2, T])
        SIL = sb("SIL", [P, 2, T])
        A = sb("A", [P, 2, T])
        AH = sb("AH", [P, 2, T], F32R)
        AL = sb("AL", [P, 2, T], F32R)

        PAN = ctx.enter_context(nc.psum_tensor("PAN", [P, 2, 512], F32))
        ACC = ctx.enter_context(nc.psum_tensor("ACC", [P, 4, 512], F32))
        OUTP = ctx.enter_context(nc.psum_tensor("OUTP", [P, 512], F32))
        MISC = ctx.enter_context(nc.psum_tensor("MISC", [P, 512], F32))

        def prm(name):
            off, n = at[name]
            return PRM[:, off:off + n]

        def two(ap):
            return ap.rearrange("p (a t) -> p a t", a=2)

        def over(ap, n):
            return ap.rearrange("p (a t) -> p a t", a=1).broadcast_to([P, n, ap.shape[1]])

        ident = prm("ident")
        banks = [two(PAN[:, b, :]) for b in range(2)]
        acc = [two(ACC[:, b, :]) for b in range(4)]
        misc = two(MISC[:, :])
        outp = two(OUTP[:, :])
        Wr = W[:, :, :].rearrange("p k t -> p t k")

        def split_high(act, c, i=None):
            s = c % RING
            act.wait_ge(K.sem(f"chunk_loaded{s}"), 16 * (c // RING + 1) if i is None else i * 16 + 16 * (c // RING + 1))
            act.activation(w_high[:, s, :], raw[:, s, :], ACT.Copy).then_inc(K.sem("w_high_ready"), 1)

        def split_low(dve, c, i=None):
            s = c % RING
            dve.wait_ge(K.sem("w_high_ready"), c + 1 if i is None else i * RING + (c + 1))
            dve.tensor_tensor(w_low[:, s, :], raw[:, s, :], w_high[:, s, :].bitcast(F32),
                              ALU.subtract).then_inc(K.sem("w_low_ready"), 1)

        def act_ahead(act, c):
            if c + 2 < n_chunks:
                if c >= 1:
                    act.wait_ge(*done(("used", c - 1)))
                split_high(act, c + 2)

        def dve_ahead(dve, c):
            if c + 2 < n_chunks:
                split_low(dve, c + 2)

        def weights_ready(pe, c, i=None):
            pe.wait_ge(K.sem("w_low_ready"), c + 1 if i is None else i * RING + (c + 1))

        def multiply(pe, bank, s, XH=XH, XL=XL, ks=range(KT)):
            ks = list(ks)
            for n in range(2):
                for k in ks:
                    w = slice(k * 2 * P + n * P, k * 2 * P + (n + 1) * P)
                    pe.matmul(bank[:, n, :], w_high[:, s, w], XH[:, k, :], start=k == ks[0], stop=False)
                    pe.matmul(bank[:, n, :], w_high[:, s, w], XL[:, k, :], start=False, stop=False)
                    mm = pe.matmul(bank[:, n, :], w_low[:, s, w], XH[:, k, :], start=False, stop=k == ks[-1])
            return mm

        def multiply_down(pe, s, half, buf):
            for n in range(KT):
                w = slice(half * D + n * P, half * D + (n + 1) * P)
                for a, b in ((w_high, AH), (w_high, AL), (w_low, AH)):
                    mm = pe.matmul(acc[n // 2][:, n % 2, :], a[:, s, w], b[:, buf, :], start=False,
                                   stop=False, skip_group_check=True)
            return mm

        class Bank:
            read = [None, None]
            used = {}

        def in_pe(pe, m, c, step, j):
            Bank.used[m, j] = step % 2
            pe_panel(pe, c, step % 2, ("in", m, j))

        def pe_panel(pe, c, b, event):
            weights_ready(pe, c)
            if Bank.read[b] is not None:
                pe.wait_ge(*done(Bank.read[b]))
            mm = multiply(pe, banks[b], c % RING)
            mm.then_inc(*raised("panel_done", event))
            K.alias(("used", c), event)
            Bank.read[b] = event + ("read",)

        block = ctx.enter_context(nc.Block())


        def ffn_pe(pe, f, c0):
            def up(c, i, ev, lag_ev):
                b = ev in ("p1", "b")
                weights_ready(pe, c, i)
                if i is not None:
                    pe.wait_ge(*done(("ffn_read", f, ev), i, 1))
                elif Bank.read[b] is not None:
                    pe.wait_ge(*done(Bank.read[b]))
                multiply(pe, banks[b], c % RING).then_inc(*raised("panel_done", ("up", f, ev)))

            def down(c, i, half, ev, act_ev, lag):
                if i is None:
                    pe.wait_ge(*done(act_ev))
                else:
                    pe.wait_ge(*done(act_ev, i, lag))
                weights_ready(pe, c, i)
                multiply_down(pe, c % RING, half, half).then_inc(*raised("acc_done", ev))

            pe.wait_ge(*done(("x_split", f)))
            up(c0, None, "p0", None)
            up(c0 + 1, None, "p1", None)
            pe.wait_ge(*done(("acc_zero", f)))
            with K.fori(pe, PAIRS - 1) as i:
                up(c0 + 2, i, "a", None)
                down(c0 + 3, i, 0, ("down", f, "a"), ("act", f, "a"), 1)
                up(c0 + 4, i, "b", None)
                down(c0 + 3, i, 1, ("down", f, "b"), ("act", f, "b"), 1)
            down(c0 + FFN_CHUNKS - 1, None, 0, ("down", f, "last0"), ("act", f, "a"), 0)
            down(c0 + FFN_CHUNKS - 1, None, 1, ("down", f, "last1"), ("act", f, "b"), 0)
            Bank.read[0], Bank.read[1] = ("ffn_read", f, "a"), ("ffn_read", f, "b")
            last = c0 + FFN_CHUNKS
            K.alias(("used", last - 3), ("down", f, "b"))
            K.alias(("used", last - 2), ("up", f, "b"))
            K.alias(("used", last - 1), ("down", f, "last1"))

        def ffn_act(act, f, c0, conv):
            def take(b, i, ev):
                if conv is not None:
                    act.wait_ge(*done(("up", f, ev), i))
                    if i is not None:
                        act.wait_ge(*done(("conv", f, ev), i, 1))
                    act.activation(UP[:, b, :, 2:], banks[b], ACT.Copy)\
                        .then_inc(*raised("panel_read", ("ffn_read", f, ev)))

            def silu(b, i, ev):
                act.wait_ge(*done(("gated_in", f, ev), i))
                act.activation(SIL[:, b, :], G2[:, b, 0, :], ACT.Silu)\
                    .then_inc(*raised("silu_ready", ("silu", f, ev)))

            act_ahead(act, c0)
            take(0, None, "p0")
            silu(0, None, "p0")
            take(1, None, "p1")
            silu(1, None, "p1")
            act.wait_ge(*done(("up", f, "p1")))
            with K.fori(act, PAIRS - 1) as i:
                act.wait_ge(*done(("down", f, "b"), i, 1))
                split_high(act, c0 + 3, i)
                act.wait_ge(*done(("up", f, "b"), i, 1))
                split_high(act, c0 + 4, i)
                take(0, i, "a")
                silu(0, i, "a")
                act.wait_ge(*done(("up", f, "a"), i))
                split_high(act, c0 + 5, i)
                take(1, i, "b")
                silu(1, i, "b")
            last = c0 + FFN_CHUNKS
            for c in (last - 2, last - 1):
                act_ahead(act, c)

        def ffn_dve(dve, f, c0, conv):
            def enter(b, i, ev):
                if conv is None:
                    dve.wait_ge(*done(("up", f, ev), i))
                    if ev == "p0":
                        dve.wait_ge(*done(("rms", f)))
                    dve.tensor_tensor(G2[:, b], banks[b], over(RS[:, :], 2), ALU.mult)\
                        .then_inc(*raised("panel_read" if conv is not None else "panel_scaled", ("ffn_read", f, ev)))
                    K.alias(("gated_in", f, ev), ("ffn_read", f, ev))
                    return
                w = prm(f"ffn_conv{conv}").rearrange("p (j x) -> p j x", x=6)
                j = {"p0": 0, "p1": 1}[ev] if i is None else i * 2 + (2 + b)
                dve.wait_ge(*done(("ffn_read", f, ev), i))
                for tap in range(3):
                    if tap:
                        dve.wait_ge(*done(("conv", f, ev, tap - 1), i))
                    for ab in range(2):
                        k = w[:, j:j + 1, ab * 3 + tap] if i is None else w[:, bass.ds(j, 1), ab * 3 + tap]
                        src = UP[:, b, ab, tap:tap + T]
                        if tap == 0:
                            ins = dve.tensor_scalar(G2[:, b, ab, :], src, k, None, ALU.mult)
                        else:
                            ins = dve.scalar_tensor_tensor(out=G2[:, b, ab, :], in0=src, scalar=k,
                                                           in1=G2[:, b, ab, :], op0=ALU.mult, op1=ALU.add)
                    ins.then_inc(*raised("conv_ready", ("conv", f, ev, tap)))
                K.alias(("conv", f, ev), ("conv", f, ev, 2))
                K.alias(("gated_in", f, ev), ("conv", f, ev, 2))

            def leave(b, i, ev):
                dve.wait_ge(*done(("silu", f, ev), i))
                dve.tensor_tensor(A[:, b, :], SIL[:, b, :], G2[:, b, 1, :], ALU.mult)\
                    .then_inc(*raised("product_ready", ("product", f, ev)))
                if i is not None:
                    dve.wait_ge(*done(("down", f, ev), i))
                dve.wait_ge(*done(("product", f, ev), i))
                dve.tensor_copy(AH[:, b, :], A[:, b, :]).then_inc(*raised("product_ready", ("act_high", f, ev)))
                dve.wait_ge(*done(("act_high", f, ev), i))
                dve.tensor_tensor(AL[:, b, :], A[:, b, :], AH[:, b, :].bitcast(F32), ALU.subtract)\
                    .then_inc(*raised("act_split", ("act", f, ev)))

            dve_ahead(dve, c0)
            dve.memset(ACC[:, :, :], 0.0).then_inc(*raised("acc_zeroed", ("acc_zero", f)))
            enter(0, None, "p0")
            leave(0, None, "p0")
            enter(1, None, "p1")
            leave(1, None, "p1")
            with K.fori(dve, PAIRS - 1) as i:
                split_low(dve, c0 + 3, i)
                split_low(dve, c0 + 4, i)
                enter(0, i, "a")
                split_low(dve, c0 + 5, i)
                leave(0, i, "a")
                enter(1, i, "b")
                leave(1, i, "b")
            last = c0 + FFN_CHUNKS
            for c in (last - 2, last - 1):
                dve_ahead(dve, c)

        def residual_from_acc(dve, f, first):
            dve.wait_ge(*done(("down", f, "last1")))
            for b in range(4):
                x = X[:, 2 * b:2 * b + 2, :]
                if first:
                    ins = dve.scalar_tensor_tensor(out=x, in0=x, scalar=ALPHA, in1=acc[b], op0=ALU.mult, op1=ALU.add)
                else:
                    ins = dve.scalar_tensor_tensor(out=x, in0=acc[b], scalar=0.5, in1=x, op0=ALU.mult, op1=ALU.add)
                ins.then_inc(*raised("residual_added", ("resid", f, b)))

        def out_pe(pe, m, c0, high, low, after):
            for e in after:
                pe.wait_ge(*done(e))
            for j in range(OUT):
                weights_ready(pe, c0 + j)
                pe.wait_ge(*done(Bank.read[j % 2]))
                multiply(pe, banks[j % 2], (c0 + j) % RING, high, low).then_inc(*raised("panel_done", ("out", m, j)))
                K.alias(("used", c0 + j), ("out", m, j))
                Bank.read[j % 2] = ("resid", m, j)

        def out_dve(dve, m, c0, first):
            for j in range(OUT):
                dve_ahead(dve, c0 + j)
                dve.wait_ge(*done(("out", m, j)))
                x = X[:, 2 * j:2 * j + 2, :]
                dve.scalar_tensor_tensor(out=x, in0=x, scalar=ALPHA if first else 1.0, in1=banks[j % 2],
                                         op0=ALU.mult, op1=ALU.add).then_inc(*raised("residual_added", ("resid", m, j)))

        def out_act(act, m, c0):
            for j in range(OUT):
                act_ahead(act, c0 + j)

        def ln_pe(pe, m):
            pe.wait_ge(*done(("sums", m)))
            pe.matmul(MISC[:, 0:T], ones_d[:, :], RS[:, :], start=True, stop=True)\
                .then_inc(*raised("mean_ready", ("mean", m)))
            pe.wait_ge(*done(("sums2", m)))
            pe.matmul(MISC[:, 0:T], ones_d[:, :], RS[:, :], start=True, stop=True)\
                .then_inc(*raised("second_mean", ("mean2", m)))

        def ln_dve(dve, m, n, g, b):
            dve.wait_ge(*done(("resid", m, 3)))
            dve.tensor_reduce(RS[:, :], X[:, :, :].rearrange("p k t -> p t k"), AX.X, ALU.add)\
                .then_inc(*raised("feature_sums", ("sums", m)))
            dve.wait_ge(*done(("mean", m)))
            dve.tensor_tensor(X[:, :, :], X[:, :, :], over(MISC[:, 0:T], KT), ALU.subtract)\
                .then_inc(*raised("centered", ("centered", m)))
            dve.wait_ge(*done(("squares", m)))
            dve.tensor_reduce(RS[:, :], Wr, AX.X, ALU.add).then_inc(*raised("square_sums", ("sums2", m)))
            dve.wait_ge(*done(("mean2", m)))
            dve.tensor_scalar(RS[:, :], MISC[:, 0:T], LN_EPS, None, ALU.add).then_inc(*raised("variance", ("var", m)))
            dve.wait_ge(*done(("root", m)))
            dve.reciprocal(RS[:, :], RS[:, :]).then_inc(*raised("ln_factor", ("rstd", m)))
            dve.wait_ge(*done(("rstd", m)))
            dve.tensor_tensor(W[:, :, :], X[:, :, :], over(RS[:, :], KT), ALU.mult)\
                .then_inc(*raised("normed", ("normed", m)))
            dve.wait_ge(*done(("normed", m)))
            for k in range(KT):
                ins = dve.tensor_scalar(X[:, k, :], W[:, k, :], prm(g)[:, k:k + 1], prm(b)[:, k:k + 1],
                                        ALU.mult, ALU.add)
            ins.then_inc(*raised("ln_out", ("ln_out", m)))
            dve.wait_ge(*done(("ln_out", m)))
            if n is None:
                for q in range(4):
                    K.alias(("resid", "stack2", q), ("ln_out", m))
                return
            dve.wait_ge(*done(("x_high", n)))
            dve.tensor_tensor(XL[:, :, :], X[:, :, :], XH[:, :, :].bitcast(F32), ALU.subtract)\
                .then_inc(*raised("x_split", ("x_split", n)))

        def ln_act(act, m, n, g, b):
            act.wait_ge(*done(("centered", m)))
            act.activation(W[:, :, :], X[:, :, :], ACT.Square).then_inc(*raised("squares_ready", ("squares", m)))
            act.wait_ge(*done(("var", m)))
            act.activation(RS[:, :], RS[:, :], ACT.Sqrt).then_inc(*raised("deviation", ("root", m)))
            if n is None:
                return
            act.wait_ge(*done(("normed", m)))
            for k in range(KT):
                ins = act.activation(XH[:, k, :], W[:, k, :], ACT.Identity, scale=prm(g)[:, k:k + 1],
                                     bias=prm(b)[:, k:k + 1])
            ins.then_inc(*raised("x_high", ("x_high", n)))

        def rms_act(act, m, n, g):
            for b in range(4):
                act.wait_ge(*done(("resid", m, b)))
                if n is None:
                    continue
                for k in (2 * b, 2 * b + 1):
                    ins = act.activation(XH[:, k, :], X[:, k, :], ACT.Identity, scale=prm(g)[:, k:k + 1])
                ins.then_inc(*raised("x_tile_high", ("xh", n, b)))
            act.activation(W[:, :, :], X[:, :, :], ACT.Square).then_inc(*raised("squares_ready", ("squares", m)))
            act.wait_ge(*done(("var", m)))
            act.activation(RS[:, :], RS[:, :], ACT.Sqrt).then_inc(*raised("deviation", ("root", m)))

        def rms_pe(pe, m):
            pe.wait_ge(*done(("sums", m)))
            pe.matmul(MISC[:, 0:T], ones_d[:, :], RS[:, :], start=True, stop=True)\
                .then_inc(*raised("mean_ready", ("mean", m)))

        def rms_dve(dve, m, n, g):
            for b in range(4 if n is not None else 0):
                dve.wait_ge(*done(("xh", n, b)))
                for k in (2 * b, 2 * b + 1):
                    ins = dve.scalar_tensor_tensor(out=XL[:, k, :], in0=X[:, k, :], scalar=prm(g)[:, k:k + 1],
                                                   in1=XH[:, k, :].bitcast(F32), op0=ALU.mult, op1=ALU.subtract)
                ins.then_inc(*raised("x_split", ("x_split", n) if b == 3 else ("xl", n, b)))
            dve.wait_ge(*done(("squares", m)))
            dve.tensor_reduce(RS[:, :], Wr, AX.X, ALU.add).then_inc(*raised("feature_sums", ("sums", m)))
            dve.wait_ge(*done(("mean", m)))
            dve.tensor_scalar(RS[:, :], MISC[:, 0:T], RMS_EPS, None, ALU.add).then_inc(*raised("variance", ("var", m)))
            dve.wait_ge(*done(("root", m)))
            dve.reciprocal(RS[:, :], RS[:, :]).then_inc(*raised("rms_factor", ("rms", n)))
            dve.wait_ge(*done(("rms", n)))

        def in_act(act, m, j):
            act.wait_ge(*done(("in", m, j)))
            act.activation(FEAT[:, 2 * j:2 * j + 2, :], banks[Bank.used[m, j]], ACT.Copy)\
                .then_inc(*raised("panel_read", ("in", m, j, "read")))

        def in_dve(dve, m, j):
            dve.wait_ge(*done(("in", m, j)))
            dve.tensor_tensor(FEAT[:, 2 * j:2 * j + 2, :], banks[Bank.used[m, j]], over(RS[:, :], 2), ALU.mult)\
                .then_inc(*raised("panel_scaled", ("in", m, j, "read")))

        def rope_pe(pe, tag, src, after, matrix):
            pe.wait_ge(*done(after))
            misc_free(pe)
            for t in range(src.shape[1]):
                mm = pe.matmul(misc[:, t, :], prm(matrix), src[:, t, :], start=True, stop=True)
            mm.then_inc(*raised("rotated", (tag, "rotated")))
            Misc.read = (tag, "sin")

        def rope_dve(dve, tag, src, dst, cs):
            w = src.shape[1]
            dve.wait_ge(*done((tag, "rotated")))
            if Misc.rope is not None:
                dve.wait_ge(*done(Misc.rope))
            dve.tensor_tensor(ROT[:, 0:w, :], misc[:, 0:w, :], over(ropes[:, cs + 1, :], w), ALU.mult)\
                .then_inc(*raised("sin_part", (tag, "sin")))
            dve.tensor_tensor(dst, src, over(ropes[:, cs, :], w), ALU.mult)\
                .then_inc(*raised("cos_part", (tag, "cos")))
            dve.wait_ge(*done((tag, "sin")))
            dve.wait_ge(*done((tag, "cos")))
            dve.tensor_tensor(dst, dst, ROT[:, 0:w, :], ALU.add).then_inc(*raised("rotation_added", (tag, "done")))
            Misc.rope = (tag, "done")

        class Misc:
            read = None
            outp = None
            accs = None
            rope = None

        def misc_free(pe):
            if Misc.read is not None:
                pe.wait_ge(*done(Misc.read))

        def turn_pe(pe, tag, tiles, after):
            pe.wait_ge(*done(after))
            misc_free(pe)
            for r in range(QT):
                for n, t in enumerate(tiles):
                    mm = pe.transpose(MISC[:, (r * len(tiles) + n) * P:(r * len(tiles) + n + 1) * P],
                                      t[:, r * P:(r + 1) * P], ident)
            mm.then_inc(*raised("turned", (tag, "turned")))
            Misc.read = (tag, "copied")

        def turn_act(act, tag, n, dst, func=ACT.Copy):
            act.wait_ge(*done((tag, "turned")))
            act.activation(dst, MISC[:, 0:QT * n * P].rearrange("p (r c) -> p r c", r=QT)[:, :, 0:dst.shape[2]],
                           func).then_inc(*raised("psum_copied", (tag, "copied")))

        FULL = ((0, P), (P, SEQ_K))
        BLOCKWISE = ((0, NCMP), (NCMP, QT * NCMP))

        class Item:
            def __init__(self, tag, q, k, v, keys, mask, after=(), sink=None, gate=None, any_key=None):
                self.tag, self.q, self.k, self.v, self.keys, self.mask = tag, q, k, v, keys, mask
                self.after, self.sink, self.gate, self.any_key = after, sink, gate, any_key

        def in_pairs(m, pairs):
            items = []
            for n, (tile, its) in enumerate(pairs):
                for it in its:
                    it.pair, it.tile, it.m, it.slot = n, tile, m, len(items) % 2
                    it.prob = PROBS[len(items) % 3]
                    it.stats = [small[:, 20 * (len(items) % 3) + 4 * i:20 * (len(items) % 3) + 4 * i + 4]
                                for i in range(5)]
                    it.first, it.last = it is its[0], it is its[-1]
                    it.out = (outp if n % 2 == 0 else misc)[:, 0, :]
                    items.append(it)
            return items

        PROBS = [SM[:, 0:2, :], SM[:, 2:4, :],
                 W[:, 2:5, :].rearrange("p a t -> p (a t)").rearrange("p (h k) -> p h k", h=2)]

        def hr(ap):
            return ap.rearrange("p (h r) -> p h r", r=QT)

        def attention_pe(pe, items):
            def scores(n):
                it = items[n]
                for e in it.after:
                    pe.wait_ge(*done(e))
                if n >= 2:
                    pe.wait_ge(*done((items[n - 2].tag, "masked")))
                elif Misc.accs is not None:
                    pe.wait_ge(*done(Misc.accs))
                for h in range(2):
                    for r, (lo, hi) in enumerate(it.keys):
                        mm = pe.matmul(ACC[:, 2 * it.slot + h, lo:hi], it.q[h][:, r * P:(r + 1) * P],
                                       it.k[h][:, 0:hi - lo], start=True, stop=True)
                mm.then_inc(*raised("scores_done", (it.tag, "scores")))

            for n in range(min(3, len(items))):
                scores(n)
            for n, it in enumerate(items):
                pe.wait_ge(*done((it.tag, "probs")))
                if n:
                    pe.wait_ge(*done((items[n - 1].tag, "copied")))
                else:
                    for b in range(2):
                        pe.wait_ge(*done(Bank.read[b]))
                for h in range(2):
                    if it.keys is FULL:
                        for b in range(3):
                            mm = pe.transpose(PAN[:, h, b * P:(b + 1) * P],
                                              it.prob[:, h, b * P:(b + 1) * P], ident)
                    else:
                        for r, (lo, hi) in enumerate(it.keys):
                            mm = pe.transpose(PAN[0:NCMP, h, r * P:(r + 1) * P],
                                              it.prob[:, h, lo:hi], ident)
                mm.then_inc(*raised("turned", (it.tag, "turned")))
                if n + 3 < len(items):
                    scores(n + 3)
                pe.wait_ge(*done((it.tag, "copied")))
                if it.first:
                    pe.wait_ge(*done(("zero", it.m, it.pair)))
                for h in range(2):
                    o = it.out[h * DH:(h + 1) * DH, :]
                    pt = PT[:, 2 * it.slot + h, :]
                    if it.keys is FULL:
                        pe.matmul(o, it.v(h, 0), pt[:, 0:T], start=False, stop=False, skip_group_check=True)
                        mm = pe.matmul(o[:, P:T], it.v(h, 1), pt[:, T:SEQ_K], start=False, stop=False,
                                       skip_group_check=True)
                    else:
                        mm = pe.matmul(o, it.v(h, 0), pt[0:NCMP, 0:T], start=False, stop=False,
                                       skip_group_check=True)
                mm.then_inc(*raised("attended", (it.tag, "out")))
            Misc.accs = (items[-1].tag, "masked")
            Bank.read = [(items[-1].tag, "copied")] * 2
            Misc.read = ("o_split", items[-1].m, [it.tile for it in items if it.pair % 2][-1])

        def attention_act(act, items, pt_free=None):
            def exps(n):
                it = items[n]
                _, minus_max, total, _, sink_part = it.stats
                if it.sink is not None:
                    act.wait_ge(*done((it.tag, "sink_less")))
                    act.activation(sink_part, sink_part, ACT.Exp).then_inc(*raised("sink_exp", (it.tag, "sink_exp")))
                act.wait_ge(*done((it.tag, "max")))
                for h in range(2):
                    for r, (lo, hi) in enumerate(it.keys):
                        x = it.prob[:, h, lo:hi]
                        j = 2 * h + r
                        ins = act.activation(x, x, ACT.Exp, bias=minus_max[:, j:j + 1], accum_out=total[:, j:j + 1])
                ins.then_inc(*raised("exps_ready", (it.tag, "exps")))

            def high(it):
                act.wait_ge(*done((it.tag, "out")))
                act.activation(OH[:, it.tile, :], it.out, ACT.Copy)\
                    .then_inc(*raised("o_high_ready", ("oh", it.m, it.tile)))

            for n in range(min(2, len(items))):
                exps(n)
            for n, it in enumerate(items):
                act.wait_ge(*done((it.tag, "turned")))
                if n >= 2:
                    act.wait_ge(*done((items[n - 2].tag, "out")))
                elif pt_free is not None:
                    act.wait_ge(*done(pt_free))
                s = slice(2 * it.slot, 2 * it.slot + 2)
                if it.keys is FULL:
                    ins = act.activation(PT[:, s, :], PAN[:, :, 0:SEQ_K], ACT.Copy)
                else:
                    ins = act.activation(PT[0:NCMP, s, 0:T], PAN[0:NCMP, :, 0:T], ACT.Copy)
                ins.then_inc(*raised("psum_copied", (it.tag, "copied")))
                if n and items[n - 1].last:
                    high(items[n - 1])
                if n + 2 < len(items):
                    exps(n + 2)
            high(items[-1])

        def attention_dve(dve, items, sm_free=(), misc_last=None):
            def masked_max(n):
                it = items[n]
                top, minus_max, _, _, sink_part = it.stats
                s, w = slice(2 * it.slot, 2 * it.slot + 2), it.keys[1][1]
                dve.wait_ge(*done((it.tag, "scores")))
                if n >= 3:
                    dve.wait_ge(*done((items[n - 3].tag, "turned")))
                dve.scalar_tensor_tensor(out=it.prob[:, :, 0:w], in0=ACC[:, s, 0:w], scalar=SCALE,
                                         in1=over(it.mask, 2), op0=ALU.mult, op1=ALU.add)\
                    .then_inc(*raised("scores_masked", (it.tag, "masked")))
                dve.wait_ge(*done((it.tag, "masked")))
                for r, (lo, hi) in enumerate(it.keys):
                    ins = dve.tensor_reduce(hr(top)[:, :, r], it.prob[:, :, lo:hi], AX.X, ALU.max)
                ins.then_inc(*raised("row_max", (it.tag, "mx")))
                dve.wait_ge(*done((it.tag, "mx")))
                if it.sink is not None:
                    sink = it.sink.rearrange("p (h r) -> p h r", r=1).broadcast_to([P, 2, QT])
                    dve.tensor_tensor(hr(top), hr(top), sink, ALU.max)\
                        .then_inc(*raised("row_max_with_sink", (it.tag, "mxs")))
                    dve.wait_ge(*done((it.tag, "mxs")))
                    dve.tensor_tensor(hr(sink_part), sink, hr(top), ALU.subtract)\
                        .then_inc(*raised("sink_less", (it.tag, "sink_less")))
                dve.tensor_scalar(minus_max, top, -1.0, None, ALU.mult).then_inc(*raised("negated_max", (it.tag, "max")))

            def normalise(it):
                _, _, total, factor, sink_part = it.stats
                dve.wait_ge(*done((it.tag, "exps")))
                if it.sink is not None:
                    dve.wait_ge(*done((it.tag, "sink_exp")))
                    dve.tensor_tensor(total, total, sink_part, ALU.add).then_inc(*raised("row_sum", (it.tag, "sum")))
                    dve.wait_ge(*done((it.tag, "sum")))
                dve.reciprocal(factor, total).then_inc(*raised("sum_inverted", (it.tag, "rc")))
                dve.wait_ge(*done((it.tag, "rc")))
                if it.any_key is not None:
                    dve.tensor_tensor(hr(factor), hr(factor), over(it.any_key, 2), ALU.mult)\
                        .then_inc(*raised("empty_rows_cleared", (it.tag, "rc_any")))
                    dve.wait_ge(*done((it.tag, "rc_any")))
                if it.gate is not None:
                    dve.tensor_tensor(hr(factor), hr(factor), it.gate, ALU.mult)\
                        .then_inc(*raised("gate_applied", (it.tag, "gated")))
                    dve.wait_ge(*done((it.tag, "gated")))
                for r, (lo, hi) in enumerate(it.keys):
                    ins = dve.tensor_tensor(it.prob[:, :, lo:hi], it.prob[:, :, lo:hi],
                                            hr(factor)[:, :, r:r + 1].broadcast_to([P, 2, hi - lo]), ALU.mult)
                ins.then_inc(*raised("probs_ready", (it.tag, "probs")))

            def zero(it):
                dve.memset(it.out, 0.0).then_inc(*raised("out_zeroed", ("zero", it.m, it.pair)))

            def low(it):
                dve.wait_ge(*done(("oh", it.m, it.tile)))
                dve.tensor_tensor(OL[:, it.tile, :], it.out, OH[:, it.tile, :].bitcast(F32), ALU.subtract)\
                    .then_inc(*raised("o_low_ready", ("o_split", it.m, it.tile)))

            firsts = [it for it in items if it.first]
            for e in sm_free + ([Misc.rope] if Misc.rope else []):
                dve.wait_ge(*done(e))
            for n in range(min(2, len(items))):
                masked_max(n)
            zero(firsts[0])
            if misc_last is not None:
                dve.wait_ge(*done(misc_last))
            zero(firsts[1])
            for n, it in enumerate(items):
                normalise(it)
                if n + 2 < len(items):
                    masked_max(n + 2)
                if n and items[n - 1].last:
                    low(items[n - 1])
                    if items[n - 1].pair + 2 < len(firsts):
                        dve.wait_ge(*done(("o_split", items[n - 1].m, items[n - 1].tile)))
                        zero(firsts[items[n - 1].pair + 2])
            low(items[-1])

        def split_w_act(act, m, tiles, after):
            for e in after:
                act.wait_ge(*done(e))
            act.activation(OH[:, tiles, :], W[:, tiles, :], ACT.Copy)\
                .then_inc(*raised("o_high_ready", ("oh", m, tiles.start)))

        def split_w_dve(dve, m, tiles):
            dve.wait_ge(*done(("oh", m, tiles.start)))
            dve.tensor_tensor(OL[:, tiles, :], W[:, tiles, :], OH[:, tiles, :].bitcast(F32), ALU.subtract)\
                .then_inc(*raised("o_low_ready", ("o_split", m, tiles.start)))
            K.alias(("o_split", m, tiles.start + 1), ("o_split", m, tiles.start))

        POOL0 = 6
        PU = [PT[:, :, :].rearrange("p a b -> p (a b)")[:, n * 2 * (T + POOL_PAD):(n + 1) * 2 * (T + POOL_PAD)]
              .rearrange("p (a t) -> p a t", a=2) for n in range(2)]
        SMf = SM[:, :, :].rearrange("p a b -> p (a b)")
        SUMS = SMf[:, 0:2 * T].rearrange("p (a t) -> p a t", a=2)
        CV = SMf[:, 2 * T:2 * T + 2 * (T + 2)].rearrange("p (a t) -> p a t", a=2)

        def mix1_items(l):
            pairs = []
            for n in range(4):
                q = [FEAT[h * DH:(h + 1) * DH, n, :] for h in range(2)]
                k = [KD[h * DH:(h + 1) * DH, n // 2, :] for h in range(2)]
                pairs.append((2 + n, [Item(("att", l, n), q, k, lambda h, r, g=n // 2: VT[:, r, g * DH:(g + 1) * DH],
                                           FULL, prm("window"), after=[("kd", l), (("v", l), "copied")],
                                           sink=prm(f"sinks{l}")[:, 2 * n:2 * n + 2])]))
            return in_pairs(("mix", l), pairs)

        def merge_pe(pe, l, c1):
            for j in range(KT // 2):
                for g in range(3):
                    pe_panel(pe, c1 + 4 * j + g, (j + g) % 2, ("gate", l, j, g))
                c = c1 + 4 * j + 3
                weights_ready(pe, c)
                if j == 0:
                    for t in range(KT):
                        pe.wait_ge(*done(("o_split", ("mix", l), t)))
                else:
                    pe.wait_ge(*done(("merge", l, j - 1, 2)))
                for b, ks in enumerate((range(0, 2), range(2, 6), range(6, 8))):
                    mm = multiply(pe, acc[b], c % RING, OH, OL, ks)
                mm.then_inc(*raised("acc_done", ("branch", l, j)))
                K.alias(("used", c), ("branch", l, j))
            Misc.accs = ("merge", l, KT // 2 - 1, 2)

        GS = FEAT

        def merge_act(act, l, c1):
            for j in range(KT // 2):
                for g in range(3):
                    act_ahead(act, c1 + 4 * j + g)
                    act.wait_ge(*done(("gate", l, j, g)))
                    if j:
                        act.wait_ge(*done(("merge", l, j - 1, g)))
                    act.activation(GS[:, 14 + 2 * g:16 + 2 * g, :], banks[(j + g) % 2], ACT.Sigmoid)\
                        .then_inc(*raised("panel_read", ("gate", l, j, g, "read")))
                act_ahead(act, c1 + 4 * j + 3)
            for j in range(KT // 2):
                act.wait_ge(*done(("merge_sum", l, j, 1)))
                act.activation(XH[:, 2 * j:2 * j + 2, :], W[:, 2 * j:2 * j + 2, :], ACT.Copy)\
                    .then_inc(*raised("merged_high", ("merged_high", l, j)))

        def merge_dve(dve, l, c1):
            def low(j):
                dve.wait_ge(*done(("merged_high", l, j)))
                dve.tensor_tensor(XL[:, 2 * j:2 * j + 2, :], W[:, 2 * j:2 * j + 2, :],
                                  XH[:, 2 * j:2 * j + 2, :].bitcast(F32), ALU.subtract)\
                    .then_inc(*raised("merged_low", ("merged_split", l, j)))

            for j in range(KT // 2):
                for g in range(4):
                    dve_ahead(dve, c1 + 4 * j + g)
                if j == KT // 2 - 1:
                    for i in range(j):
                        low(i)
                dve.wait_ge(*done(("branch", l, j)))
                w = W[:, 2 * j:2 * j + 2, :]
                for g in range(3):
                    dve.wait_ge(*done(("gate", l, j, g, "read")))
                    t = GS[:, 14 + 2 * g:16 + 2 * g, :]
                    dst = w if g == 0 else (G2[:, g - 1])
                    if g and j:
                        dve.wait_ge(*done(("merge_sum", l, j - 1, g - 1)))
                    dve.tensor_tensor(dst, t, acc[g], ALU.mult).then_inc(*raised("gate_times_branch", ("merge", l, j, g)))
                for g in range(2):
                    dve.wait_ge(*done(("merge", l, j, g + 1)))
                    if g:
                        dve.wait_ge(*done(("merge_sum", l, j, 0)))
                    dve.tensor_tensor(w, w, G2[:, g], ALU.add).then_inc(*raised("merged", ("merge_sum", l, j, g)))
            low(KT // 2 - 1)

        def mix1_pe(pe, l, c0):
            m = ("mix", l)
            read = [("in", m, j, "read") for j in range(IN1)]
            pe.wait_ge(*done(("x_split", m)))
            for j in range(IN1):
                in_pe(pe, m, c0 + j, j, j)
                if 1 <= j <= 2:
                    rope_pe(pe, ("rope", l, j - 1), FEAT[:, 2 * j - 2:2 * j, :], read[j - 1], "rotate")
                if j == 3:
                    rope_pe(pe, ("rope", l, 2), FEAT[:, 4:5, :], read[2], "rotate")
                    turn_pe(pe, ("v", l), [FEAT[:, 5, :]], read[2])
                if j == 5:
                    pe.wait_ge(*done(("pooled", l)))
                    misc_free(pe)
                    for t in range(2):
                        mm = pe.matmul(misc[:, t, :], prm(f"w_pool{l}")[:, t * P:(t + 1) * P], SUMS[:, t, :],
                                       start=True, stop=True)
                    mm.then_inc(*raised("pool_mixed", ("pool_mixed", l)))
                    Misc.read = ("pool_out", l)
            attention_pe(pe, mix1_items(l))
            merge_pe(pe, l, c0 + IN1)
            out_pe(pe, ("mix_out", l), c0 + IN1 + GATE1, XH, XL, [("merged_split", l, j) for j in range(4)])

        def mix1_act(act, l, c0):
            m = ("mix", l)
            for j in range(IN1):
                act_ahead(act, c0 + j)
                in_act(act, m, j)
                if j == 4:
                    act.wait_ge(*done((("rope", l, 2), "done")))
                    for g in range(2):
                        for h in range(2):
                            ins = act.activation(KD[h * DH:(h + 1) * DH, g, :], FEAT[g * DH:(g + 1) * DH, 4, :],
                                                 ACT.Copy)
                    ins.then_inc(*raised("keys_doubled", ("kd", l)))
                    turn_act(act, ("v", l), 1, VT[:, :, 0:P])
                if j == 6:
                    act.wait_ge(*done(("pool_mixed", l)))
                    for t in range(2):
                        ins = act.activation(W[:, t, :], misc[:, t, :], ACT.Copy,
                                             scale=prm(f"pool_scale{l}")[:, t:t + 1])
                    ins.then_inc(*raised("pool_out", ("pool_out", l)))
                    split_w_act(act, m, slice(0, 2), [("pool_out", l)])
            attention_act(act, mix1_items(l))
            split_w_act(act, m, slice(6, 8), [("conv_out", l)])
            merge_act(act, l, c0 + IN1)
            out_act(act, ("mix_out", l), c0 + IN1 + GATE1)

        def mix1_dve(dve, l, c0):
            m = ("mix", l)
            for j in range(IN1):
                dve_ahead(dve, c0 + j)
                if 1 <= j <= 2:
                    rope_dve(dve, ("rope", l, j - 1), FEAT[:, 2 * j - 2:2 * j, :], FEAT[:, 2 * j - 2:2 * j, :], 0)
                if j == 3:
                    rope_dve(dve, ("rope", l, 2), FEAT[:, 4:5, :], FEAT[:, 4:5, :], 0)
                if j == 4:
                    pool_dve(dve, l, ("in", m, 3, "read"))
                if j == 6:
                    conv_dve(dve, l, m)
            attention_dve(dve, mix1_items(l), [("pool_mixed", l), ("cv_tap", l, 2)], ("pool_out", l))
            dve.wait_ge(*done(("in", m, 6, "read")))
            dve.tensor_tensor(W[:, 6:8, :], W[:, 6:8, :], FEAT[:, 12:14, :], ALU.mult)\
                .then_inc(*raised("conv_out", ("conv_out", l)))
            split_w_dve(dve, m, slice(0, 2))
            split_w_dve(dve, m, slice(6, 8))
            merge_dve(dve, l, c0 + IN1)
            out_dve(dve, ("mix_out", l), c0 + IN1 + GATE1, True)

        def pool_dve(dve, l, after):
            dve.memset(PT[:, :, :], 0.0).then_inc(*raised("pool_zero", ("pool_zero", l)))
            dve.wait_ge(*done(after))
            dve.wait_ge(*done(("pool_zero", l)))
            u = FEAT[:, POOL0:POOL0 + 2, :]
            dve.tensor_copy(PU[0][:, :, POOL_PAD:], u).then_inc(*raised("pool_sum", ("pool_sum", l, 0)))
            for n in range(4):
                src, dst, shift = PU[n % 2], PU[(n + 1) % 2], 1 << n
                dve.wait_ge(*done(("pool_sum", l, n)))
                if n:
                    dve.wait_ge(*done(("pool_pick", l, n - 1)))
                dve.tensor_tensor(dst[:, :, POOL_PAD:], src[:, :, POOL_PAD:],
                                  src[:, :, POOL_PAD - shift:POOL_PAD - shift + T], ALU.add)\
                    .then_inc(*raised("pool_sum", ("pool_sum", l, n + 1)))
                dve.wait_ge(*done(("pool_sum", l, n + 1)))
                half = slice((n % 2) * DH, (n % 2 + 1) * DH)
                cnt = prm("per_count").rearrange("p (a t) -> p a t", a=2)
                dve.tensor_tensor(SUMS[half, n // 2, :], dst[half, n // 2, POOL_PAD:], cnt[half, n // 2, :],
                                  ALU.mult).then_inc(*raised("pool_pick", ("pool_pick", l, n)))
            dve.wait_ge(*done(("pool_pick", l, 3)))
            dve.tensor_tensor(SUMS, SUMS, u, ALU.subtract).then_inc(*raised("pooled", ("pooled", l)))

        def conv_dve(dve, l, m):
            dve.wait_ge(*done(("in", m, 5, "read")))
            dve.memset(CV[:, :, 0:2], 0.0).then_inc(*raised("conv_pad_zeroed", ("cv_zero", l)))
            dve.tensor_tensor(CV[:, :, 2:], FEAT[:, 10:12, :], FEAT[:, 8:10, :], ALU.mult)\
                .then_inc(*raised("conv_input", ("cv_in", l)))
            dve.wait_ge(*done(("cv_zero", l)))
            dve.wait_ge(*done(("cv_in", l)))
            cw = prm(f"conv_w{l}")
            for tap in range(3):
                if tap:
                    dve.wait_ge(*done(("cv_tap", l, tap - 1)))
                for t in range(2):
                    k = cw[:, 3 * t + tap:3 * t + tap + 1]
                    src = CV[:, t, tap:tap + T]
                    dst = W[:, 6 + t, :]
                    if tap == 0:
                        ins = dve.tensor_scalar(dst, src, k, None, ALU.mult)
                    else:
                        ins = dve.scalar_tensor_tensor(out=dst, in0=src, scalar=k, in1=dst, op0=ALU.mult, op1=ALU.add)
                ins.then_inc(*raised("conv_tap", ("cv_tap", l, tap)))

        def half(col):
            return FEAT[(col % 2) * DH:(col % 2 + 1) * DH, col // 2, :]

        PTf = PT[:, :, :].rearrange("p a b -> p (a b)")
        UPf = UP[:, :, :, :].rearrange("p a b c -> p (a b c)")
        G2f = G2[:, :, :, :].rearrange("p a b c -> p (a b c)")
        SHW = T + CMP_STRIDE
        NB = B_KV * NCMP
        SHIFT = {x: t[:, 0:B_KV * SHW].rearrange("p (g t) -> p g t", g=B_KV) for x, t in (("k", SMf), ("v", PTf))}
        BLOCKS = {x: t[:, 0:CMP_STRIDE * NB] for x, t in (("k", G2f), ("v", UPf))}
        OHf = OH[:, :, :].rearrange("p k t -> p (k t)")
        OLf = OL[:, :, :].rearrange("p k t -> p (k t)")
        HIDDEN = W[0:NB, 4:6, :]
        VG = A
        RV = SIL[:, 0, :]
        GT = small[:, 64:64 + QT * 36].rearrange("p (r c) -> p r c", r=QT)
        GTh = small[:, 64:64 + QT * 36].rearrange("p (r h b) -> p b h r", r=QT, b=3)

        def ev_items(m):
            pairs = []
            for n in range(B_HEADS // 2):
                g = n // 2
                hs = [slice(h * DH, (h + 1) * DH) for h in range(2)]
                q_raw, q_rot = [[t[h, tile, :] for h in hs] for t, tile in ((FEAT, 4 + n), (QR, n))]
                gate = [GTh[:, b, 2 * n:2 * n + 2, :] for b in range(3)]
                items = [Item(("cmp_att", n), q_raw, [KC[h, g, :] for h in hs], lambda h, r, g=g: VC[0:NCMP, g, :],
                              BLOCKWISE, prm("cmp_mask"), after=[("kc",), ("in", m, 2 + n // 2, "read")],
                              gate=gate[0], any_key=prm("cmp_any"))]
                for b, name in enumerate(("sel_att", "win_att")):
                    items.append(Item((name, n), q_rot, [KD[h, 3 * b + g, :] for h in hs],
                                      lambda h, r, at=(3 * b + g) * DH: VT[:, r, at:at + DH], FULL, prm("causal"),
                                      after=[("kd", m), (("v1",), "copied"), (("v2",), "gates"),
                                             (("rope_q", m, n // 2), "done")], gate=gate[1 + b]))
                pairs.append((2 + n, items))
            return in_pairs(m, pairs)

        EV_STEPS = EV_ORDER[:EV_EARLY] + ("k0", "k1", "v0", "v1") + EV_ORDER[EV_EARLY:]

        def compress_pe(pe, c, x, j):
            n = "kv".index(x)
            if j == 0:
                pe.wait_ge(*done(("blocks", x)))
            weights_ready(pe, c)
            for k in range(KT):
                w = slice(k * 2 * P, (k + 1) * 2 * P)
                at0 = n * 768 + (j * KT + k) * NB
                hi, lo = OHf[:, at0:at0 + NB], OLf[:, at0:at0 + NB]
                dst = ACC[0:NB, n, 0:2 * P]
                s = c % RING
                pe.matmul(dst, hi, w_high[:, s, w], start=j == 0 and k == 0, stop=False)
                pe.matmul(dst, lo, w_high[:, s, w], start=False, stop=False)
                mm = pe.matmul(dst, hi, w_low[:, s, w], start=False, stop=j == 1 and k == KT - 1)
            mm.then_inc(*raised("panel_done", ("cmp", x, j)))
            K.alias(("used", c), ("cmp", x, j))

        def ev_pe(pe, m, c0):
            pe.wait_ge(*done(("x_split", m)))
            for step, j in enumerate(EV_STEPS):
                if j in ("k0", "k1", "v0", "v1"):
                    compress_pe(pe, c0 + step, j[0], int(j[1]))
                else:
                    in_pe(pe, m, c0 + step, step, j)
                if step == 2:
                    pe.wait_ge(*done(("v_squares",)))
                    misc_free(pe)
                    for t in range(2):
                        mm = pe.matmul(MISC[:, 0:T], ones_v[:, :], W[:, 6 + t, :], start=t == 0, stop=t == 1)
                    mm.then_inc(*raised("v_mean", ("v_mean",)))
                    Misc.read = ("v_var",)
                if step == 4:
                    turn_pe(pe, ("vg",), [W[:, 4, :], W[:, 5, :]], ("v_scaled",))
                    rope_pe(pe, ("rope_k", m, 0), FEAT[:, 13:14, :], ("in", m, 6, "read"), "rotate")
                if step == 5:
                    pe.wait_ge(*done((("vg",), "copied")))
                    misc_free(pe)
                    for c in range(QT):
                        for g in range(4):
                            mm = pe.matmul(misc[(g % 2) * DH:(g % 2 + 1) * DH, g // 2, c * P:(c + 1) * P],
                                           VG[:, c, g * DH:(g + 1) * DH], prm("sgu_w")[:, g * P:(g + 1) * P],
                                           start=True, stop=True)
                    mm.then_inc(*raised("tokens_mixed", ("sgu",)))
                    Misc.read = ("sgu_bias",)
                if step == 6:
                    rope_pe(pe, ("rope_k", m, 1), FEAT[:, 14:16, :], ("in", m, 7, "read"), "rotate")
                if step == 7:
                    turn_pe(pe, ("v1",), [FEAT[:, 16, :], FEAT[:, 17, :]], ("in", m, 8, "read"))
                if step == 8:
                    turn_pe(pe, ("v2",), [FEAT[:, 18, :], FEAT[:, 19, :]], ("in", m, 9, "read"))
                if step == 11:
                    pe.wait_ge(*done(("hidden",)))
                    misc_free(pe)
                    for o in range(4):
                        mm = pe.transpose(MISC[:, o * NB:(o + 1) * NB], HIDDEN[:, o // 2, o % 2 * P:(o % 2 + 1) * P],
                                          ident[0:NB, 0:NB])
                    mm.then_inc(*raised("turned", ("hid", "turned")))
                    Misc.read = ("hid", "copied")
                if step == 12:
                    compressed_pe(pe)
                    rope_pe(pe, ("rope_q", m, 0), FEAT[:, 4:6, :], ("in", m, 2, "read"), "rotate")
                if step == 13:
                    rope_pe(pe, ("rope_q", m, 1), FEAT[:, 6:8, :], ("in", m, 3, "read"), "rotate")
            rope_pe(pe, ("rope_q", m, 2), FEAT[:, 8:10, :], ("in", m, 4, "read"), "rotate")
            attention_pe(pe, ev_items(m))
            out_pe(pe, ("mix_out", m), c0 + EV_IN + CMP, OH, OL, [("o_split", m, t) for t in range(KT)])

        def compressed_pe(pe):
            pe.wait_ge(*done(("hid", "copied")))
            misc_free(pe)
            w2k = prm("cmp_w2_k").rearrange("p (k c) -> p k c", k=2)
            w2v = prm("cmp_w2_v").rearrange("p (k c) -> p k c", k=2)
            for k in range(2):
                pe.matmul(MISC[:, 0:NB], w2k[:, k, :], HID[:, k, :], start=k == 0, stop=k == 1)
            for g in range(B_KV):
                for k in range(2):
                    mm = pe.matmul(MISC[0:NCMP, 64 + g * DH:64 + (g + 1) * DH],
                                   HID[:, 2 + k, g * NCMP:(g + 1) * NCMP], w2v[:, k, :], start=k == 0, stop=k == 1)
            mm.then_inc(*raised("compressed", ("compressed",)))
            Misc.read = ("kc",)

        def ev_act(act, m, c0):
            def shift(x):
                n = "kv".index(x)
                act.wait_ge(*done(("shift_zero",)))
                for g in range(B_KV):
                    src = half(20 + 3 * n + g)
                    act.activation(SHIFT[x][0:DH, g, 0:T], src, ACT.Copy)
                    ins = act.activation(SHIFT[x][DH:P, g, 0:T - CMP_STRIDE], src[:, CMP_STRIDE:], ACT.Copy)
                ins.then_inc(*raised("tokens_shifted", ("shift", x)))
                act.wait_ge(*done(("blocks_full", x)))
                act.activation(OHf[:, 768 * n:768 * (n + 1)], BLOCKS[x], ACT.Copy)\
                    .then_inc(*raised("blocks_high", ("blocks_high", x)))

            for step, j in enumerate(EV_STEPS):
                act_ahead(act, c0 + step)
                if step == 2:
                    act.wait_ge(*done(("in", m, 0, "read")))
                    act.wait_ge(*done(("in", m, 1, "read")))
                    act.activation(FEAT[:, 0:4, :], FEAT[:, 0:4, :], ACT.Gelu_apprx_tanh)\
                        .then_inc(*raised("gelu", ("gelu",)))
                    act.wait_ge(*done(("gelu",)))
                    act.activation(W[:, 6:8, :], FEAT[:, 2:4, :], ACT.Square)\
                        .then_inc(*raised("v_squares", ("v_squares",)))
                if step == 3:
                    act.wait_ge(*done(("v_var",)))
                    act.activation(RV, RV, ACT.Sqrt).then_inc(*raised("v_root", ("v_root",)))
                if step == 4:
                    turn_act(act, ("vg",), 2, VG[:, :, :])
                    act.wait_ge(*done(("in", m, 6, "read")))
                    shift("k")
                if step == 5:
                    shift("v")
                if step == 8:
                    act.wait_ge(*done((("rope_k", m, 1), "done")))
                    for h in range(2):
                        for p in range(2):
                            ins = act.activation(KD[h * DH:(h + 1) * DH, p::2, :], FEAT[p * DH:(p + 1) * DH, 13:16, :],
                                                 ACT.Copy)
                    ins.then_inc(*raised("keys_doubled", ("kd", m)))
                    turn_act(act, ("v1",), 2, VT[:, :, 0:2 * P])
                if step == 9:
                    act.wait_ge(*done((("v2",), "turned")))
                    mr = MISC[:, 0:512].rearrange("p (r c) -> p r c", r=QT)
                    act.activation(VT[:, :, 2 * P:3 * P], mr[:, :, 0:P], ACT.Copy)
                    act.activation(GT, mr[:, :, P:P + 36], ACT.Sigmoid).then_inc(*raised("v2_gates", (("v2",), "gates")))
                    K.alias((("v2",), "copied"), (("v2",), "gates"))
                if step == 11:
                    act.wait_ge(*done(("cmp", "v", 1)))
                    act.activation(HIDDEN, ACC[0:NB, 0:2, 0:2 * P], ACT.Gelu_apprx_tanh)\
                        .then_inc(*raised("hidden", ("hidden",)))
                if step == 12:
                    act.wait_ge(*done(("hid", "turned")))
                    act.activation(HID[:, :, :], MISC[:, 0:4 * NB].rearrange("p (o n) -> p o n", o=4), ACT.Copy)\
                        .then_inc(*raised("psum_copied", ("hid", "copied")))
                if step == 13:
                    act.wait_ge(*done(("compressed",)))
                    act.activation(KC[:, :, :], MISC[:, 0:NB].rearrange("p (g n) -> p g n", g=B_KV), ACT.Copy)
                    act.activation(VC[0:NCMP, :, :],
                                   MISC[0:NCMP, 64:64 + B_KV * DH].rearrange("p (g d) -> p g d", g=B_KV),
                                   ACT.Copy).then_inc(*raised("compressed_copied", ("kc",)))
                    split_w_act(act, m, slice(0, 2), [("gmlp",)])
            attention_act(act, ev_items(m))
            out_act(act, ("mix_out", m), c0 + EV_IN + CMP)

        def ev_dve(dve, m, c0):
            def blocks(x):
                n = "kv".index(x)
                dve.wait_ge(*done(("shift", x)))
                s, pos = SHIFT[x], prm(f"pos_{x}")
                for g in range(B_KV):
                    dst = BLOCKS[x].rearrange("p (l g n) -> p g l n", l=CMP_STRIDE, g=B_KV)[:, g]
                    src = s[:, g, 0:T].rearrange("p (n l) -> p l n", l=CMP_STRIDE)
                    ins = dve.tensor_tensor(dst, src, pos.rearrange("p (l n) -> p l n", n=1)
                                            .broadcast_to([P, CMP_STRIDE, NCMP]), ALU.add)
                ins.then_inc(*raised("blocks_full", ("blocks_full", x)))
                dve.wait_ge(*done(("blocks_high", x)))
                dve.tensor_tensor(OLf[:, 768 * n:768 * (n + 1)], BLOCKS[x],
                                  OHf[:, 768 * n:768 * (n + 1)].bitcast(F32), ALU.subtract)\
                    .then_inc(*raised("blocks", ("blocks", x)))

            dve.memset(SM[:, :, :], 0.0).then_inc(*raised("shift_zero_k", ("shift_zero_k",)))
            dve.memset(PT[:, :, :], 0.0).then_inc(*raised("shift_zero", ("shift_zero",)))
            for step, j in enumerate(EV_STEPS):
                dve_ahead(dve, c0 + step)
                if j not in ("k0", "k1", "v0", "v1"):
                    in_dve(dve, m, j)
                if step == 3:
                    dve.wait_ge(*done(("v_mean",)))
                    dve.tensor_scalar(RV, MISC[:, 0:T], RMS_EPS, None, ALU.add).then_inc(*raised("v_var", ("v_var",)))
                    dve.wait_ge(*done(("v_root",)))
                    dve.reciprocal(RV, RV).then_inc(*raised("v_rstd", ("v_rstd",)))
                    dve.wait_ge(*done(("v_rstd",)))
                    for t in range(2):
                        ins = dve.scalar_tensor_tensor(out=W[:, 4 + t, :], in0=FEAT[:, 2 + t, :],
                                                       scalar=prm("sgu_norm")[:, t:t + 1], in1=RV,
                                                       op0=ALU.mult, op1=ALU.mult)
                    ins.then_inc(*raised("v_scaled", ("v_scaled",)))
                if step == 4:
                    rope_dve(dve, ("rope_k", m, 0), FEAT[:, 13:14, :], FEAT[:, 13:14, :], 0)
                    blocks("k")
                if step == 5:
                    blocks("v")
                if step == 6:
                    dve.wait_ge(*done(("sgu",)))
                    for t in range(2):
                        ins = dve.tensor_tensor(W[:, t, :].rearrange("p (c s) -> p c s", c=QT),
                                                misc[:, t, :].rearrange("p (c s) -> p c s", c=QT),
                                                over(prm("sgu_b")[:, t * P:(t + 1) * P], QT), ALU.add)
                    ins.then_inc(*raised("sgu_bias", ("sgu_bias",)))
                    dve.wait_ge(*done(("sgu_bias",)))
                    dve.tensor_tensor(W[:, 0:2, :], W[:, 0:2, :], FEAT[:, 0:2, :], ALU.mult)\
                        .then_inc(*raised("gmlp", ("gmlp",)))
                if step == 7:
                    rope_dve(dve, ("rope_k", m, 1), FEAT[:, 14:16, :], FEAT[:, 14:16, :], 0)
                if step == 13:
                    rope_dve(dve, ("rope_q", m, 0), FEAT[:, 4:6, :], QR[:, 0:2, :], 0)
            for n in (1, 2):
                rope_dve(dve, ("rope_q", m, n), FEAT[:, 4 + 2 * n:6 + 2 * n, :], QR[:, 2 * n:2 * n + 2, :], 0)
            split_w_dve(dve, m, slice(0, 2))
            attention_dve(dve, ev_items(m), [("blocks_full", "k")], (("rope_q", m, 2), "sin"))
            out_dve(dve, ("mix_out", m), c0 + EV_IN + CMP, False)

        VW = SIL
        SC, WK = UPf[:, 0:SEQ_K], UPf[:, SEQ_K:2 * SEQ_K]
        M8 = [small[:, 40:48], small[:, 48:56]]
        DMASK = A[:, :, :].rearrange("p a t -> p (a t)")[:, 0:SEQ_K]

        def od_items(m):
            pairs = []
            for n in range(KT):
                hs = [slice(h * DH, (h + 1) * DH) for h in range(2)]
                if n < 4:
                    q, k = [FEAT[h, n, :] for h in hs], [FEAT[h, 4, :] for h in hs]
                    it = Item(("od", n), q, k, lambda h, r: VW[:, r, 0:DH], FULL, DMASK)
                else:
                    q, k = [FEAT[h, 4 + n, :] for h in hs], [FEAT[h, 8 + n, :] for h in hs]
                    it = Item(("od", n), q, k, lambda h, r, at=2 * (n - 4) * DH: VT[:, r, at + h * DH:at + (h + 1) * DH],
                              FULL, prm("causal"), after=[(("vd", 1), "copied")])
                it.after = list(it.after) + [od_roped(m, t) for t in ((n, 4) if n < 4 else (4 + n, 8 + n))]
                pairs.append((n, [it]))
            return in_pairs(m, pairs)

        def od_roped(m, tile):
            return ("rope_o", m, tile // 2), "done"

        def od_rope(m, step):
            j = OD_ORDER[step - 1] if step else None
            if j in (0, 1, 4, 5, 6, 7):
                return ("rope_o", m, j), FEAT[:, 2 * j:2 * j + 2, :]
            if j == 2:
                return ("rope_o", m, j), FEAT[:, 4:5, :]
            return None

        def od_pe(pe, m, c0):
            pe.wait_ge(*done(("x_split", m)))
            for step, j in enumerate(OD_ORDER):
                in_pe(pe, m, c0 + step, step, j)
                if step == 1:
                    rope_pe(pe, ("rope_i", m), FEAT[:, 6:8, :], ("in", m, 3, "read"), "rotate_i")
                if step == 2:
                    turn_pe(pe, ("vw",), [FEAT[:, 5, :]], ("in", m, 2, "read"))
                    pe.wait_ge(*done((("rope_i", m), "done")))
                    for h in range(IDX_HEADS):
                        for r, (lo, hi) in enumerate(FULL):
                            p = slice(h * IDX_DIM, (h + 1) * IDX_DIM)
                            mm = pe.matmul(ACC[:, h, lo:hi], FEAT[p, 6, r * P:(r + 1) * P], FEAT[p, 7, 0:hi - lo],
                                           start=True, stop=True)
                    mm.then_inc(*raised("scores_done", ("index",)))
                    Misc.accs = ("index_relu",)
                if od_rope(m, step):
                    tag, tiles = od_rope(m, step)
                    rope_pe(pe, tag, tiles, ("in", m, OD_ORDER[step - 1], "read"), "rotate")
                if step == 9:
                    turn_pe(pe, ("vd", 0), [FEAT[:, 16, :], FEAT[:, 17, :]], ("in", m, 8, "read"))
            turn_pe(pe, ("vd", 1), [FEAT[:, 18, :], FEAT[:, 19, :]], ("in", m, 9, "read"))
            attention_pe(pe, od_items(m))
            out_pe(pe, ("mix_out", m), c0 + OD_IN, OH, OL, [("o_split", m, t) for t in range(KT)])

        def od_act(act, m, c0):
            for step in range(OD_IN):
                act_ahead(act, c0 + step)
                if step == 3:
                    turn_act(act, ("vw",), 1, VW[:, :, 0:P])
                    act.wait_ge(*done(("index",)))
                    act.activation(SM[:, :, :], ACC[:, :, 0:SEQ_K], ACT.Relu, scale=IDX_DIM ** -0.5)\
                        .then_inc(*raised("index_relu", ("index_relu",)))
            for n in range(2):
                turn_act(act, ("vd", n), 2, VT[:, :, 2 * n * P:2 * (n + 1) * P])
            attention_act(act, od_items(m))
            out_act(act, ("mix_out", m), c0 + OD_IN)

        def od_dve(dve, m, c0):
            rounds = TOPK // 8
            for step, j in enumerate(OD_ORDER):
                dve_ahead(dve, c0 + step)
                in_dve(dve, m, j)
                if step == 1:
                    rope_dve(dve, ("rope_i", m), FEAT[:, 6:8, :], FEAT[:, 6:8, :], 2)
                if od_rope(m, step):
                    tag, tiles = od_rope(m, step)
                    rope_dve(dve, tag, tiles, tiles, 0)
                if step == 3:
                    index_dve(dve)
                if step >= 4:
                    for n in range(rounds * (step - 4) // 6, rounds * (step - 3) // 6):
                        top_round_dve(dve, n)
            dve.wait_ge(*done(("taken", rounds - 1, 1)))
            dve.tensor_scalar(DMASK, WK, TAKEN / 2, NEG, ALU.is_gt, ALU.mult)\
                .then_inc(*raised("not_taken", ("not_taken",)))
            dve.wait_ge(*done(("not_taken",)))
            dve.tensor_tensor(DMASK, DMASK, prm("causal"), ALU.add).then_inc(*raised("selected", ("selected",)))
            dve.wait_ge(*done(("selected",)))
            attention_dve(dve, od_items(m), [], (("vd", 1), "copied"))
            out_dve(dve, ("mix_out", m), c0 + OD_IN, False)

        def index_dve(dve):
            dve.wait_ge(*done((("vw",), "copied")))
            dve.wait_ge(*done(("index_relu",)))
            for h in range(IDX_HEADS):
                if h:
                    dve.wait_ge(*done(("index_sum", h - 1)))
                for r, (lo, hi) in enumerate(FULL):
                    w = VW[:, r, DH + h:DH + h + 1]
                    if h == 0:
                        ins = dve.tensor_scalar(SC[:, lo:hi], SM[:, h, lo:hi], w, None, ALU.mult)
                    else:
                        ins = dve.scalar_tensor_tensor(out=SC[:, lo:hi], in0=SM[:, h, lo:hi], scalar=w,
                                                       in1=SC[:, lo:hi], op0=ALU.mult, op1=ALU.add)
                ins.then_inc(*raised("index_sum", ("index_sum", h)))
            dve.wait_ge(*done(("index_sum", IDX_HEADS - 1)))
            dve.scalar_tensor_tensor(out=WK, in0=SC, scalar=IDX_HEADS ** -0.5, in1=prm("causal"),
                                     op0=ALU.mult, op1=ALU.add)\
                .then_inc(*raised("index_score", ("index_score",)))
            dve.wait_ge(*done(("index_score",)))

        def top_round_dve(dve, n):
            for r, (lo, hi) in enumerate(FULL):
                if n:
                    dve.wait_ge(*done(("taken", n - 1, r)))
                dve.max(M8[r], WK[:, lo:hi]).then_inc(*raised("top_8_found", ("top8", n, r)))
            for r, (lo, hi) in enumerate(FULL):
                dve.wait_ge(*done(("top8", n, r)))
                dve.match_replace(WK[:, lo:hi], M8[r], WK[:, lo:hi], TAKEN)\
                    .then_inc(*raised("top_8_taken", ("taken", n, r)))

        HID = sb("HID", [P, 4, NB])
        KC = sb("KC", [P, B_KV, NCMP])
        VC = sb("VC", [P, B_KV, DH])
        c = 0
        stages = []
        for l in range(DEPTH):
            stages.append(("mix1", l, c))
            c += IN1 + GATE1 + OUT
            stages.append(("ffn1", l, c))
            c += FFN_CHUNKS
        for l in range(DEPTH):
            stages.append(("ffn2", 2 + 2 * l, c))
            c += FFN_CHUNKS
            stages.append(("ev" if l % 2 == 0 else "od", l, c))
            c += (EV_IN + CMP if l % 2 == 0 else OD_IN) + OUT
            stages.append(("ffn2", 3 + 2 * l, c))
            c += FFN_CHUNKS
        assert c == n_chunks, (c, n_chunks)

        M2 = {l: ("mix2", l) for l in range(DEPTH)}

        @block.sync
        def _(sp):
            sp.dma_start(X[:, :, :], x_in).then_inc(*raised("x_loaded", "x_loaded", 16))
            sp.dma_start(PRM[:, :], params).then_inc(*raised("params_loaded", "params_loaded", 16))
            sp.dma_start(posi[:, 0, :], pos1.partition_broadcast(P)).then_inc(K.sem("positions_loaded"), 16)
            sp.dma_start(posi[:, 1, :], pos2.partition_broadcast(P)).then_inc(K.sem("positions_loaded"), 16)
            for s in range(RING):
                sp.dma_start(raw[:, s, :], weights[s]).then_inc(K.sem(f"chunk_loaded{s}"), 16)
            turns = n_chunks // RING
            with sp.Fori(1, turns) as i:
                for s in range(RING):
                    sp.wait_ge(K.sem("w_low_ready"), i * RING + (s + 1 - RING))
                    sp.dma_start(raw[:, s, :], weights[bass.ds(i * RING + s, 1)]
                                 .rearrange("a p c -> (a p) c")).then_inc(K.sem(f"chunk_loaded{s}"), 16)
            for cc in range(turns * RING, n_chunks):
                sp.wait_ge(K.sem("w_low_ready"), cc + 1 - RING)
                sp.dma_start(raw[:, cc % RING, :], weights[cc]).then_inc(K.sem(f"chunk_loaded{cc % RING}"), 16)
            sp.wait_ge(*done("result"))
            sp.dma_start(out, W[:, :, :]).then_inc(K.sem("out_stored"), 16)
            sp.wait_ge(K.sem("out_stored"), 16)

        @block.gpsimd
        def _(pool):
            pool.memset(ones_d[:, :], 1.0 / D).then_inc(*raised("constants_set", "ones_d"))
            pool.memset(ones_v[:, :], 1.0 / 256).then_inc(*raised("constants_set", "ones_v"))
            pool.memset(UP[:, :, :, 0:2], 0.0).then_inc(*raised("constants_set", "up_zero"))
            pool.wait_ge(*done("params_loaded"))
            w = prm("sgu_w").rearrange("p (g t) -> p g t", g=4)
            pool.affine_select(out=w, in_=w, compare_op=ALU.is_ge, fill=0.0, base=0,
                               pattern=[[0, 4], [1, P]], channel_multiplier=-1)\
                .then_inc(*raised("constants_set", "sgu_masked"))

        def rope_tables_dve(dve, stack):
            two_pi = 2 * np.pi
            c1 = 6.28125
            c2 = float(np.float32(np.round((two_pi - c1) * 2 ** 22) / 2 ** 22))
            c3 = two_pi - c1 - c2
            dve.wait_ge(K.sem("positions_loaded"), 32)
            tag = ("tables", stack)
            n = [0]

            def step(ins):
                ins.then_inc(*raised("table_step", (tag, n[0])))
                dve.wait_ge(*done((tag, n[0])))
                n[0] += 1

            step(dve.tensor_copy(posf, posi[:, stack, :]))
            for which, f in enumerate(("freq", "freq_i")[:1 + stack]):
                ang, turn = W[:, 4, :], W[:, 5, :]
                step(dve.tensor_scalar(ang, posf, prm(f), None, ALU.mult))
                step(dve.tensor_scalar(turn, ang, 1 / two_pi, 12582912.0, ALU.mult, ALU.add))
                step(dve.tensor_scalar(turn, turn, -12582912.0, None, ALU.add))
                for part in (c1, c2, c3):
                    step(dve.scalar_tensor_tensor(out=ang, in0=turn, scalar=-part, in1=ang, op0=ALU.mult, op1=ALU.add))
                step(dve.tensor_scalar(turn, ang, np.pi / 2, -two_pi, ALU.is_gt, ALU.mult))
                step(dve.scalar_tensor_tensor(out=turn, in0=ang, scalar=np.pi / 2, in1=turn, op0=ALU.add, op1=ALU.add))
                lim = 3.1415925
                step(dve.tensor_scalar(W[:, 2 * which, :], turn, lim, -lim, ALU.min, ALU.max))
                dve.tensor_scalar(W[:, 2 * which + 1, :], ang, lim, -lim, ALU.min, ALU.max)\
                    .then_inc(*raised("angles", (tag, "angles", which)))
                dve.wait_ge(*done((tag, "angles", which)))

        def rope_tables_act(act, stack):
            for which in range(1 + stack):
                act.wait_ge(*done((("tables", stack), "angles", which)))
                ins = act.activation(ropes[:, 2 * which:2 * which + 2, :], W[:, 2 * which:2 * which + 2, :], ACT.Sin)
            ins.then_inc(*raised("tables_done", ("tables", stack, "done")))

        @block.tensor
        def _(pe):
            pe.wait_ge(*done("params_loaded"))
            pe.wait_ge(*done("ones_v"))
            for kind, n, c0 in stages:
                if kind == "mix1":
                    mix1_pe(pe, n, c0)
                    ln_pe(pe, ("mix_out", n))
                elif kind == "ffn1":
                    ffn_pe(pe, n, c0)
                    ln_pe(pe, n)
                    if n == DEPTH - 1:
                        rms_pe(pe, "stack2")
                elif kind == "ffn2":
                    ffn_pe(pe, n, c0)
                    rms_pe(pe, n)
                elif kind == "ev":
                    pe.wait_ge(*done("sgu_masked"))
                    ev_pe(pe, M2[n], c0)
                    rms_pe(pe, ("mix_out", M2[n]))
                else:
                    od_pe(pe, M2[n], c0)
                    rms_pe(pe, ("mix_out", M2[n]))

        def norms(kind, n):
            if kind == "ffn2":
                if n == 5:
                    return n, None, "final_norm"
                return (n, M2[0], "mix_norm0") if n == 2 else (n, 4, "ffn1_norm1") if n == 3 else (n, M2[1], "mix_norm1")
            return ("mix_out", M2[n]), 3 + 2 * n, f"ffn2_norm{n}"

        @block.scalar
        def _(act):
            act.wait_ge(*done("x_loaded"))
            act.activation(XH[:, :, :], X[:, :, :], ACT.Copy).then_inc(*raised("x_high", ("x_high", ("mix", 0))))
            split_high(act, 0)
            split_high(act, 1)
            act.wait_ge(*done("params_loaded"))
            rope_tables_act(act, 0)
            act.wait_ge(*done("up_zero"))
            for kind, n, c0 in stages:
                if kind == "mix1":
                    mix1_act(act, n, c0)
                    ln_act(act, ("mix_out", n), n, f"ln1_g{n}", f"ln1_b{n}")
                elif kind == "ffn1":
                    ffn_act(act, n, c0, n)
                    last = n == DEPTH - 1
                    ln_act(act, n, None if last else ("mix", n + 1), f"ln2_g{n}", f"ln2_b{n}")
                    if last:
                        rms_act(act, "stack2", 2, "ffn1_norm0")
                        rope_tables_act(act, 1)
                else:
                    if kind == "ffn2":
                        ffn_act(act, n, c0, None)
                    elif kind == "ev":
                        ev_act(act, M2[n], c0)
                    else:
                        od_act(act, M2[n], c0)
                    rms_act(act, *norms(kind, n))

        @block.vector
        def _(dve):
            dve.wait_ge(*done(("x_high", ("mix", 0))))
            dve.tensor_tensor(XL[:, :, :], X[:, :, :], XH[:, :, :].bitcast(F32), ALU.subtract)\
                .then_inc(*raised("x_split", ("x_split", ("mix", 0))))
            split_low(dve, 0)
            split_low(dve, 1)
            dve.wait_ge(*done("params_loaded"))
            rope_tables_dve(dve, 0)
            dve.wait_ge(*done(("tables", 0, "done")))
            for kind, n, c0 in stages:
                if kind == "mix1":
                    mix1_dve(dve, n, c0)
                    ln_dve(dve, ("mix_out", n), n, f"ln1_g{n}", f"ln1_b{n}")
                elif kind == "ffn1":
                    ffn_dve(dve, n, c0, n)
                    residual_from_acc(dve, n, True)
                    last = n == DEPTH - 1
                    ln_dve(dve, n, None if last else ("mix", n + 1), f"ln2_g{n}", f"ln2_b{n}")
                    if last:
                        rms_dve(dve, "stack2", 2, "ffn1_norm0")
                        dve.wait_ge(*done(("sums", "stack2")))
                        rope_tables_dve(dve, 1)
                        dve.wait_ge(*done(("tables", 1, "done")))
                else:
                    if kind == "ffn2":
                        ffn_dve(dve, n, c0, None)
                        residual_from_acc(dve, n, False)
                    elif kind == "ev":
                        ev_dve(dve, M2[n], c0)
                    else:
                        od_dve(dve, M2[n], c0)
                    rms_dve(dve, *norms(kind, n))
            for k in range(KT):
                ins = dve.scalar_tensor_tensor(out=W[:, k, :], in0=X[:, k, :], scalar=prm("final_norm")[:, k:k + 1],
                                               in1=RS[:, :], op0=ALU.mult, op1=ALU.mult)
            ins.then_inc(*raised("result_ready", "result"))
        return K.now


def kernel(**inputs):
    import concourse.bacc as bacc
    from concourse.bass_utils import run_bass_kernel_spmd

    a = {k: np.asarray(v) for k, v in inputs.items()}
    params, at = small_parameters(a)
    arrays = {
        "weights": weight_stream(a),
        "params": params,
        "x_in": np.ascontiguousarray(a["x"][0].T.reshape(KT, P, T).transpose(1, 0, 2)),
        "pos1": np.ascontiguousarray(a["positions"].reshape(T)),
        "pos2": np.ascontiguousarray(a["positions_2"].reshape(T)),
    }
    seen = None
    for _ in range(2):
        nc = bacc.Bacc("TRN2", target_bir_lowering=False, num_devices=1)
        aps = {n: nc.dram_tensor(n, v.shape, mybir.dt.from_np(v.dtype), kind="ExternalInput").ap()
               for n, v in arrays.items()}
        out = nc.dram_tensor("out", (P, KT, T), F32, kind="ExternalOutput").ap()
        seen = build(nc, at=at, out=out, seen=seen, **aps)
    r = run_bass_kernel_spmd(nc, [arrays], core_ids=[0])
    got = r.results[0]["out"]
    return np.ascontiguousarray(got.transpose(2, 1, 0)).reshape(1, T, D)
```

```python
from contextlib import ExitStack, contextmanager

import numpy as np

import concourse.bass as bass
from concourse import mybir

F32 = mybir.dt.float32
F32R = mybir.dt.float32r
I32 = mybir.dt.int32
ALU = mybir.AluOpType
ACT = mybir.ActivationFunctionType
AX = mybir.AxisListType

P = 128
D = 1024
KT = D // P
T = 256
QT = T // P
DEPTH = 2
DH = 64
D_FF = 2816
FT = D_FF // P
CH = 2048
RING = 3
PAIRS = FT // 2
FFN_CHUNKS = FT + PAIRS
ALPHA = (2 * DEPTH) ** 0.25
LN_EPS = 1e-5
RMS_EPS = 1e-6
NEG = -1e30
TAKEN = -3e38
TOPK = min(256, T // 4)
SCALE = DH ** -0.5
IDX_HEADS, IDX_DIM = 4, 32
B_HEADS, B_KV = 12, 3
CMP_LEN, CMP_STRIDE = 32, 16
NCMP = T // CMP_STRIDE
SEQ_K = T + P
POOL_PAD = 16
ROPE_THETA = 500000.0

IN1, GATE1, OUT = 7, 16, 4
EV_IN, CMP, OD_IN = 10, 4, 10
EV_ORDER, EV_EARLY = (1, 0, 5, 6, 7, 8, 2, 9, 3, 4), 6
OD_ORDER = (3, 2, 0, 1, 4, 6, 5, 7, 8, 9)


def panel(w):
    return w.reshape(KT, P, 2 * P).transpose(1, 0, 2).reshape(P, CH)


def down_pair(w):
    return w.reshape(2, P, D).transpose(1, 0, 2).reshape(P, CH)


def per_partition(v):
    return v.reshape(-1, P).T


def ffn_chunks(a, b, down):
    u = [panel(np.concatenate([a[:, j * P:(j + 1) * P], b[:, j * P:(j + 1) * P]], 1)) for j in range(FT)]
    d = [down_pair(down[2 * P * m:2 * P * (m + 1)]) for m in range(PAIRS)]
    out = u[:2]
    for m in range(PAIRS - 1):
        out += [u[2 * m + 2], u[2 * m + 3], d[m]]
    return out + [d[-1]]


def panels(w):
    return [panel(w[:, c:c + 2 * P]) for c in range(0, w.shape[1], 2 * P)]


def weight_stream(a):
    s = []
    for l in range(DEPTH):
        w = a["w_in"][l]
        pool, q, k, v, xc, gb, gc, gates = np.split(w, np.cumsum([256, 512, 128, 128, 256, 256, 256]), 1)
        s += panels(np.concatenate([q, k, v, pool, xc, gc, gb], 1))
        branch = np.concatenate([a["w_branch_a"][l], a["w_branch_b"][l], a["w_branch_c"][l]], 0)
        for j in range(KT // 2):
            cols = slice(2 * P * j, 2 * P * (j + 1))
            s += [panel(gates[:, b * D:(b + 1) * D][:, cols]) for b in range(3)] + [panel(branch[:, cols])]
        s += panels(a["w_o"][l])
        s += ffn_chunks(a["w_up"][l][:, :D_FF], a["w_up"][l][:, D_FF:], a["w_down"][l])
    for l in range(DEPTH):
        for n in (1, 2):
            if n == 2:
                if l % 2 == 0:
                    z, q, kc, vc, ks, vs, kw, vw, gl = np.split(
                        a["ev_w_in_2"][0], np.cumsum([512, 768] + [192] * 6), 1)
                    fill = np.zeros((D, P - gl.shape[1]), np.float32)
                    into = panels(np.concatenate([z, q, kc, vc, ks, kw, vs, vw, gl, fill], 1))
                    s += [into[j] for j in EV_ORDER[:EV_EARLY]]
                    for x in "kv":
                        w1 = a[f"ev_cmp_w1_{x}_2"][0].reshape(2, CMP_STRIDE, DH, 256)
                        w1 = w1.transpose(1, 0, 2, 3).reshape(2 * D, 256)
                        s += [panel(w1[:D]), panel(w1[D:])]
                    s += [into[j] for j in EV_ORDER[EV_EARLY:]]
                    s += panels(a["ev_w_out_2"][0])
                else:
                    q, kc, vc, qi, ki, wi, qd, kd, vd = np.split(
                        a["od_w_in_2"][0], np.cumsum([512, 64, 64, 128, 32, 4, 512, 512]), 1)
                    fill = np.zeros((D, P - 68), np.float32)
                    into = panels(np.concatenate([q, kc, kc, vc, wi, fill, qi, ki, ki, ki, ki, qd, kd, vd], 1))
                    s += [into[j] for j in OD_ORDER]
                    s += panels(a["od_w_out_2"][0])
            s += ffn_chunks(a[f"ffn{n}_w_gate_2"][l], a[f"ffn{n}_w_up_2"][l], a[f"ffn{n}_w_down_2"][l])
    return np.stack(s)


def small_parameters(a):
    p = np.arange(P)
    t = np.arange(T)
    c = {"ident": np.eye(P)}
    for name, dim, half in (("rotate", DH, 8), ("rotate_i", IDX_DIM, 4)):
        r = np.zeros((P, P))
        for i in p:
            if i % dim < half:
                r[i, i + half] = -1
            elif i % dim < 2 * half:
                r[i, i - half] = 1
        c[name] = r.T
        freq = np.float32(ROPE_THETA) ** (-np.arange(0, 2 * half, 2, dtype=np.float32) / np.float32(2 * half))
        c["freq" + name[6:]] = np.where(p % dim < 2 * half, freq[(p % dim) % half], 0)[:, None]
    causal = np.where(t[None] <= p[:, None], 0, NEG)
    later = np.where(t[None] <= p[:, None] + P, 0, NEG)
    window = np.where((t[None] <= p[:, None] + P) & (t[None] > p[:, None]), 0, NEG)
    c["causal"] = np.concatenate([causal[:, :P], later], 1)
    c["window"] = np.concatenate([causal[:, :P], window], 1)
    n = np.arange(NCMP)
    tok = p[:, None, None] + P * np.arange(QT)[None, :, None]
    ok = (n * CMP_STRIDE + CMP_LEN - 1 <= tok) & (n * CMP_STRIDE + CMP_LEN <= T)
    c["cmp_mask"] = np.where(ok, 0, NEG).reshape(P, QT * NCMP)
    c["cmp_any"] = ok.any(-1)
    win = np.array([[2, 8], [4, 16]])[p // DH]
    c["per_count"] = (1 / np.minimum(t + 1, win[..., None])).reshape(P, 2 * T)
    for l in range(DEPTH):
        wp = np.zeros((P, 2, P), np.float32)
        for g in range(4):
            b = DH * (g % 2)
            wp[b:b + DH, g // 2, b:b + DH] = a["w_pool"][l, g]
        c[f"w_pool{l}"] = wp.reshape(P, 2 * P)
        c[f"pool_scale{l}"] = per_partition(a["pool_scale"][l])
        c[f"sinks{l}"] = np.broadcast_to(a["attn_sinks"][l], (P, 8))
        c[f"conv_w{l}"] = a["conv_w"][l].reshape(3, 2, P).transpose(2, 1, 0).reshape(P, 6)
        c[f"ffn_conv{l}"] = a["ffn_conv_w"][l].reshape(3, 2, FT, P).transpose(3, 2, 1, 0).reshape(P, FT * 6)
        for x in ("ln1_g", "ln1_b", "ln2_g", "ln2_b"):
            c[f"{x}{l}"] = per_partition(a[x][l])
        for x in ("ffn1_norm", "mix_norm", "ffn2_norm"):
            c[f"{x}{l}"] = per_partition(a[x + "_2"][l])
    c["final_norm"] = per_partition(a["final_norm_2"])
    c["sgu_norm"] = per_partition(a["ev_sgu_norm_2"][0])
    c["sgu_w"] = a["ev_sgu_w_2"][0].transpose(2, 0, 1).reshape(P, 4 * P)
    c["sgu_b"] = np.repeat(a["ev_sgu_b_2"][0].reshape(2, 2, P), DH, 1).transpose(1, 0, 2).reshape(P, 2 * P)
    for x in "kv":
        c[f"pos_{x}"] = a[f"ev_cmp_pos_{x}_2"][0].reshape(2, CMP_STRIDE, DH).transpose(0, 2, 1).reshape(P, CMP_STRIDE)
    w2 = a["ev_cmp_w2_k_2"][0].reshape(2, P, DH).transpose(1, 0, 2)
    c["cmp_w2_k"] = np.concatenate([w2, w2], 2).reshape(P, 2 * P)
    c["cmp_w2_v"] = a["ev_cmp_w2_v_2"][0].reshape(2, P, DH).transpose(1, 0, 2).reshape(P, 2 * DH)
    at, off = {}, 0
    for name, v in c.items():
        at[name] = (off, v.shape[1])
        off += v.shape[1]
    return np.concatenate([np.asarray(v, np.float32) for v in c.values()], 1), at


class Counts:

    def __init__(self, nc, ctx, seen):
        self.nc, self.ctx, self.seen = nc, ctx, seen
        self.sems, self.total, self.now, self.loop = {}, {}, {}, None

    def sem(self, name):
        if name not in self.sems:
            self.sems[name] = self.ctx.enter_context(self.nc.semaphore(name))
        return self.sems[name]

    def raised(self, name, event, by=1):
        assert event not in self.now, event
        self.total[name] = self.total.get(name, 0) + by
        self.now[event] = (name, self.total[name], 0, 1)
        if self.loop is not None:
            self.loop.append(event)
        return self.sem(name), by

    def alias(self, event, other):
        self.now[event] = self.now[other]
        if self.loop is not None:
            self.loop.append(event)

    @contextmanager
    def fori(self, eng, n):
        start = dict(self.total)
        self.loop = []
        with eng.Fori(0, n) as i:
            yield i
        for event in self.loop:
            name, count, _, _ = self.now[event]
            self.now[event] = (name, count, self.total[name] - start.get(name, 0), n)
        for name, count in self.total.items():
            self.total[name] = start.get(name, 0) + n * (count - start.get(name, 0))
        self.loop = None

    def done(self, event, i=None, lag=0):
        if self.seen is None:
            return self.sem("first_build"), 1
        name, count, slope, n = self.seen[event]
        if i is None or not slope:
            return self.sem(name), count + slope * (n - 1)
        assert count - lag * slope > 0, event
        return self.sem(name), i * slope + (count - lag * slope)


def build(nc, weights, params, at, x_in, pos1, pos2, out, seen):
    n_chunks = weights.shape[0]
    with ExitStack() as ctx:
        def sb(name, shape, dt=F32):
            return ctx.enter_context(nc.sbuf_tensor(name, shape, dt))

        K = Counts(nc, ctx, seen)
        done, raised = K.done, K.raised

        raw = sb("raw", [P, RING, CH])
        w_high = sb("w_high", [P, RING, CH], F32R)
        w_low = sb("w_low", [P, RING, CH], F32R)
        X = sb("X", [P, KT, T])
        XH = sb("XH", [P, KT, T], F32R)
        XL = sb("XL", [P, KT, T], F32R)
        OH = sb("OH", [P, KT, T], F32R)
        OL = sb("OL", [P, KT, T], F32R)
        W = sb("W", [P, KT, T])
        RS = sb("RS", [P, T])
        FEAT = sb("FEAT", [P, 20, T])
        QR = sb("QR", [P, 6, T])
        KD = sb("KD", [P, 6, T])
        VT = sb("VT", [P, QT, 512])
        PRM = sb("PRM", [P, params.shape[1]])
        ropes = sb("ropes", [P, 4, T])
        ones_d = sb("ones_d", [P, P])
        ones_v = sb("ones_v", [P, P])
        ones_1 = sb("ones_1", [P, P])
        posi = QR[:, 0:2, :].bitcast(I32)
        posf = FEAT[:, 18, :]
        ROT = W[:, 2:4, :]
        small = sb("small", [P, 144])
        SM = sb("SM", [P, 4, SEQ_K])
        PT = sb("PT", [P, 4, SEQ_K])
        UP = sb("UP", [P, 2, 2, T + 2])
        G2 = sb("G2", [P, 2, 2, T])
        SIL = sb("SIL", [P, 2, T])
        A = sb("A", [P, 2, T])
        AH = sb("AH", [P, 2, T], F32R)
        AL = sb("AL", [P, 2, T], F32R)

        PAN = ctx.enter_context(nc.psum_tensor("PAN", [P, 2, 512], F32))
        ACC = ctx.enter_context(nc.psum_tensor("ACC", [P, 4, 512], F32))
        OUTP = ctx.enter_context(nc.psum_tensor("OUTP", [P, 512], F32))
        MISC = ctx.enter_context(nc.psum_tensor("MISC", [P, 512], F32))

        def prm(name):
            off, n = at[name]
            return PRM[:, off:off + n]

        def two(ap):
            return ap.rearrange("p (a t) -> p a t", a=2)

        def over(ap, n):
            return ap.rearrange("p (a t) -> p a t", a=1).broadcast_to([P, n, ap.shape[1]])

        ident = prm("ident")
        banks = [two(PAN[:, b, :]) for b in range(2)]
        acc = [two(ACC[:, b, :]) for b in range(4)]
        misc = two(MISC[:, :])
        outp = two(OUTP[:, :])
        SQ = FEAT[:, 0:KT, :]
        DIAG = FEAT[:, KT, :].rearrange("p (r c) -> p r c", r=QT)

        def split_high(act, c, i=None):
            s = c % RING
            act.wait_ge(K.sem(f"chunk_loaded{s}"), 16 * (c // RING + 1) if i is None else i * 16 + 16 * (c // RING + 1))
            act.activation(w_high[:, s, :], raw[:, s, :], ACT.Copy).then_inc(K.sem("w_high_ready"), 1)

        def split_low(dve, c, i=None):
            s = c % RING
            dve.wait_ge(K.sem("w_high_ready"), c + 1 if i is None else i * RING + (c + 1))
            dve.tensor_tensor(w_low[:, s, :], raw[:, s, :], w_high[:, s, :].bitcast(F32),
                              ALU.subtract).then_inc(K.sem("w_low_ready"), 1)

        def act_ahead(act, c):
            if c + 2 < n_chunks:
                if c >= 1:
                    act.wait_ge(*done(("used", c - 1)))
                split_high(act, c + 2)

        def dve_ahead(dve, c):
            if c + 2 < n_chunks:
                split_low(dve, c + 2)

        def weights_ready(pe, c, i=None):
            pe.wait_ge(K.sem("w_low_ready"), c + 1 if i is None else i * RING + (c + 1))

        def multiply(pe, bank, s, XH=XH, XL=XL, ks=range(KT)):
            ks = list(ks)
            for n in range(2):
                for k in ks:
                    w = slice(k * 2 * P + n * P, k * 2 * P + (n + 1) * P)
                    pe.matmul(bank[:, n, :], w_high[:, s, w], XH[:, k, :], start=k == ks[0], stop=False)
                    pe.matmul(bank[:, n, :], w_high[:, s, w], XL[:, k, :], start=False, stop=False)
                    mm = pe.matmul(bank[:, n, :], w_low[:, s, w], XH[:, k, :], start=False, stop=k == ks[-1])
            return mm

        def multiply_as_ready(pe, bank, s, ready, XH=XH, XL=XL):
            for k in range(KT):
                if k == 0 or ready[k] != ready[k - 1]:
                    pe.wait_ge(*done(ready[k]))
                for n in range(2):
                    w = slice(k * 2 * P + n * P, k * 2 * P + (n + 1) * P)
                    for i, (a, b) in enumerate(((w_high, XH), (w_high, XL), (w_low, XH))):
                        mm = pe.matmul(bank[:, n, :], a[:, s, w], b[:, k, :], start=k + n + i == 0, stop=False,
                                       skip_group_check=True)
            return mm

        AFTER_LN = (0, 1, ("mix", 1))

        def x_split(n):
            ready = [("x_split", n, k // 2) for k in range(KT)]
            if n in AFTER_LN:
                ready[0] = ("x_split", n, "tile 0")
            return ready

        def multiply_down(pe, s, half, buf, ns=range(KT)):
            for n in ns:
                w = slice(half * D + n * P, half * D + (n + 1) * P)
                for a, b in ((w_high, AH), (w_high, AL), (w_low, AH)):
                    mm = pe.matmul(acc[n // 2][:, n % 2, :], a[:, s, w], b[:, buf, :], start=False,
                                   stop=False, skip_group_check=True)
            return mm

        class Bank:
            read = [None, None]
            used = {}

        def in_pe(pe, m, c, step, j):
            Bank.used[m, j] = step % 2
            pe_panel(pe, c, step % 2, ("in", m, j), x_split(m) if step == 0 else None)

        def pe_panel(pe, c, b, event, ready=None):
            weights_ready(pe, c)
            if Bank.read[b] is not None:
                pe.wait_ge(*done(Bank.read[b]))
            if ready is None:
                mm = multiply(pe, banks[b], c % RING)
            else:
                mm = multiply_as_ready(pe, banks[b], c % RING, ready)
            mm.then_inc(*raised("panel_done", event))
            K.alias(("used", c), event)
            Bank.read[b] = event + ("read",)

        block = ctx.enter_context(nc.Block())


        def ffn_pe(pe, f, c0, norm):
            def up(c, i, ev, lag_ev):
                b = ev in ("p1", "b")
                weights_ready(pe, c, i)
                if ev == "a":
                    pe.wait_ge(*done(("ffn_read", f, "a"), i, 1))
                elif ev == "b":
                    pe.wait_ge(*done(("ffn_read", f, "last b"), i))
                elif Bank.read[b] is not None:
                    pe.wait_ge(*done(Bank.read[b]))
                if ev == "p0":
                    mm = multiply_as_ready(pe, banks[b], c % RING, x_split(f))
                else:
                    mm = multiply(pe, banks[b], c % RING)
                mm.then_inc(*raised("panel_done", ("up", f, ev)))

            def down(c, i, half, ev, act_ev, lag):
                if i is None:
                    pe.wait_ge(*done(act_ev))
                else:
                    pe.wait_ge(*done(act_ev, i, lag))
                weights_ready(pe, c, i)
                multiply_down(pe, c % RING, half, half).then_inc(*raised("acc_done", ev))

            up(c0, None, "p0", None)
            if norm is not None:
                rms_pe(pe, norm)
            up(c0 + 1, None, "p1", None)
            with K.fori(pe, PAIRS - 1) as i:
                up(c0 + 2, i, "a", None)
                pe.wait_ge(*done(("acc_zero", f)))
                down(c0 + 4, i, 0, ("down", f, "a"), ("act", f, "a"), 1)
                up(c0 + 3, i, "b", None)
                down(c0 + 4, i, 1, ("down", f, "b"), ("act", f, "last b"), 0)
            down(c0 + FFN_CHUNKS - 1, None, 0, ("down", f, "last0"), ("act", f, "a"), 0)
            pe.wait_ge(*done(("act", f, "end")))
            for b in range(4):
                multiply_down(pe, (c0 + FFN_CHUNKS - 1) % RING, 1, 1, (2 * b, 2 * b + 1))\
                    .then_inc(*raised("acc_done", ("down", f, "last1", b)))
            Bank.read[0], Bank.read[1] = ("ffn_read", f, "a"), ("ffn_read", f, "end")
            last = c0 + FFN_CHUNKS
            K.alias(("used", last - 3), ("up", f, "b"))
            K.alias(("used", last - 2), ("down", f, "b"))
            K.alias(("used", last - 1), ("down", f, "last1", 3))

        def ffn_act(act, f, c0, conv, norm):
            def take(b, i, ev, up, lag=0):
                if conv is not None:
                    act.wait_ge(*done(("up", f, up), i, lag))
                    if i is not None:
                        act.wait_ge(*done(("conv", f, "a"), i, 1))
                    elif ev == "end":
                        act.wait_ge(*done(("conv", f, "last b")))
                    act.activation(UP[:, b, :, 2:], banks[b], ACT.Copy)\
                        .then_inc(*raised("panel_read", ("ffn_read", f, ev)))

            def zero_acc():
                ones = ones_v[:, 0:1].rearrange("p (a t) -> p a t", a=1).broadcast_to([P, 4, 2 * T])
                act.activation(ACC[:, :, :], ones, ACT.Copy, scale=0.0)\
                    .then_inc(*raised("acc_zeroed", ("acc_zero", f)))

            def silu(b, i, ev):
                act.wait_ge(*done(("gated_in", f, ev), i))
                act.activation(SIL[:, b, :], G2[:, b, 0, :], ACT.Silu)\
                    .then_inc(*raised("silu_ready", ("silu", f, ev)))

            act_ahead(act, c0)
            if norm is not None:
                zero_acc()
                rms_act(act, norm)
                warm(act, ACT.Silu)
            else:
                take(0, None, "p0", "p0")
                zero_acc()
            silu(0, None, "p0")
            with K.fori(act, PAIRS - 1) as i:
                act.wait_ge(*done(("up", f, "b"), i, 1))
                split_high(act, c0 + 3, i)
                take(1, i, "last b", "b", 1)
                act.wait_ge(*done(("down", f, "b"), i, 1))
                split_high(act, c0 + 4, i)
                take(0, i, "a", "a")
                act.wait_ge(*done(("up", f, "a"), i))
                split_high(act, c0 + 5, i)
                silu(1, i, "last b")
                silu(0, i, "a")
            last = c0 + FFN_CHUNKS
            take(1, None, "end", "b")
            act_ahead(act, last - 2)
            silu(1, None, "end")
            act_ahead(act, last - 1)

        def ffn_dve(dve, f, c0, conv, norm):
            def enter(b, i, ev):
                if conv is None:
                    up, lag = {"last b": ("b", 1), "end": ("b", 0)}.get(ev, (ev, 0))
                    dve.wait_ge(*done(("up", f, up), i, lag))
                    dve.tensor_tensor(G2[:, b], banks[b], over(RS[:, :], 2), ALU.mult)\
                        .then_inc(*raised("panel_read" if conv is not None else "panel_scaled", ("ffn_read", f, ev)))
                    K.alias(("gated_in", f, ev), ("ffn_read", f, ev))
                    return
                w = prm(f"ffn_conv{conv}").rearrange("p (j x) -> p j x", x=6)
                j = {"p0": 0, "end": FT - 1}[ev] if i is None else i * 2 + (1 if ev == "last b" else 2)
                dve.wait_ge(*done(("ffn_read", f, ev), i))
                for tap in range(3):
                    if tap:
                        dve.wait_ge(*done(("conv", f, ev, tap - 1), i))
                    for ab in range(2):
                        k = w[:, j:j + 1, ab * 3 + tap] if i is None else w[:, bass.ds(j, 1), ab * 3 + tap]
                        src = UP[:, b, ab, tap:tap + T]
                        if tap == 0:
                            ins = dve.tensor_scalar(G2[:, b, ab, :], src, k, None, ALU.mult)
                        else:
                            ins = dve.scalar_tensor_tensor(out=G2[:, b, ab, :], in0=src, scalar=k,
                                                           in1=G2[:, b, ab, :], op0=ALU.mult, op1=ALU.add)
                    ins.then_inc(*raised("conv_ready", ("conv", f, ev, tap)))
                K.alias(("conv", f, ev), ("conv", f, ev, 2))
                K.alias(("gated_in", f, ev), ("conv", f, ev, 2))

            def leave(b, i, ev):
                dve.wait_ge(*done(("silu", f, ev), i))
                dve.tensor_tensor(A[:, b, :], SIL[:, b, :], G2[:, b, 1, :], ALU.mult)\
                    .then_inc(*raised("product_ready", ("product", f, ev)))
                if ev == "a":
                    dve.wait_ge(*done(("down", f, "a"), i))
                elif ev == "last b":
                    dve.wait_ge(*done(("down", f, "b"), i, 1))
                elif ev == "end":
                    dve.wait_ge(*done(("down", f, "b")))
                dve.wait_ge(*done(("product", f, ev), i))
                dve.tensor_copy(AH[:, b, :], A[:, b, :]).then_inc(*raised("product_ready", ("act_high", f, ev)))
                dve.wait_ge(*done(("act_high", f, ev), i))
                dve.tensor_tensor(AL[:, b, :], A[:, b, :], AH[:, b, :].bitcast(F32), ALU.subtract)\
                    .then_inc(*raised("act_split", ("act", f, ev)))

            dve_ahead(dve, c0)
            if norm is not None:
                rms_dve(dve, norm)
            enter(0, None, "p0")
            leave(0, None, "p0")
            with K.fori(dve, PAIRS - 1) as i:
                split_low(dve, c0 + 3, i)
                split_low(dve, c0 + 4, i)
                enter(1, i, "last b")
                enter(0, i, "a")
                leave(1, i, "last b")
                split_low(dve, c0 + 5, i)
                leave(0, i, "a")
            last = c0 + FFN_CHUNKS
            enter(1, None, "end")
            leave(1, None, "end")
            dve_ahead(dve, last - 2)

        def residual_pair(dve, m, j, src, first):
            x = X[:, 2 * j:2 * j + 2, :]
            if first:
                ins = dve.scalar_tensor_tensor(out=x, in0=x, scalar=ALPHA, in1=src, op0=ALU.mult, op1=ALU.add)
            elif src is acc[j]:
                ins = dve.scalar_tensor_tensor(out=x, in0=src, scalar=0.5, in1=x, op0=ALU.mult, op1=ALU.add)
            else:
                ins = dve.tensor_tensor(x, x, src, ALU.add)
            ins.then_inc(*raised("residual_added", ("resid", m, j)))
            if not first:
                return
            if j == 1:
                dve.wait_ge(*done(("resid", m, 1)))
                dve.tensor_tensor(W[:, 0:2, :], X[:, 0:2, :], X[:, 2:4, :], ALU.add)\
                    .then_inc(*raised("feature_sums", ("sum", m)))

        def ffn_residual_dve(dve, f, c0, first, n, g):
            for b in range(4):
                dve.wait_ge(*done(("down", f, "last1", b)))
                residual_pair(dve, f, b, acc[b], first)
                if b and not first and n is not None:
                    rms_low_dve(dve, n, g, b - 1)
            if not first:
                if n is not None:
                    rms_low_dve(dve, n, g, 3)
                rms_sums_dve(dve, f)
                dve_ahead(dve, c0 + FFN_CHUNKS - 1)

        def out_pe(pe, m, c0, high, low, ready):
            for j in range(OUT):
                weights_ready(pe, c0 + j)
                pe.wait_ge(*done(Bank.read[j % 2]))
                if j == 0:
                    mm = multiply_as_ready(pe, banks[j % 2], (c0 + j) % RING, ready, high, low)
                else:
                    mm = multiply(pe, banks[j % 2], (c0 + j) % RING, high, low)
                mm.then_inc(*raised("panel_done", ("out", m, j)))
                K.alias(("used", c0 + j), ("out", m, j))
                Bank.read[j % 2] = ("resid", m, j)

        def out_dve(dve, m, c0, first, n=None, g=None):
            for j in range(OUT):
                dve_ahead(dve, c0 + j)
                if j and not first:
                    rms_low_dve(dve, n, g, j - 1)
                dve.wait_ge(*done(("out", m, j)))
                residual_pair(dve, m, j, banks[j % 2], first)
            if not first:
                rms_low_dve(dve, n, g, 3)

        def out_act(act, m, c0, n=None, g=None):
            for j in range(OUT):
                act_ahead(act, c0 + j)
                if j and n is not None:
                    rms_high_act(act, m, n, g, j - 1)
            if n is not None:
                rms_high_act(act, m, n, g, 3)

        def ln_pe(pe, m):
            misc_free(pe)
            outp_free(pe)
            pe.wait_ge(*done(("sum", m)))
            for t in range(2):
                pe.matmul(MISC[:, 0:T], ones_d[:, :], W[:, t, :], start=t == 0, stop=False)
            for k in range(4, KT):
                if k % 2 == 0:
                    pe.wait_ge(*done(("resid", m, k // 2)))
                mm = pe.matmul(MISC[:, 0:T], ones_d[:, :], X[:, k, :], start=False, stop=k == KT - 1)
            mm.then_inc(*raised("mean_ready", ("mean", m)))
            for k in range(6):
                if k % 2 == 0:
                    pe.wait_ge(*done(("squares", m, k // 2) if k < 4 else ("upper_squares", m)))
                for r in range(QT):
                    mm = pe.matmul(OUTP[:, r:r + 1], SQ[:, k, r * P:(r + 1) * P], ones_d[:, 0:1],
                                   start=k + r == 0, stop=k == 5, skip_group_check=True)
            mm.then_inc(*raised("second_mean", ("mean2", m)))
            pe.wait_ge(*done(("diagonal", m)))
            for r in range(QT):
                mm = pe.matmul(OUTP[:, T + r * P:T + (r + 1) * P], ones_1[:, :], DIAG[:, r, :], start=True, stop=True)
            mm.then_inc(*raised("factor_spread", ("rstd", m)))
            Misc.read = ("centered", m, 3)
            Misc.outp = ("normed", m, 3)

        LN_PARTS = [("tile 0", slice(0, 1)), (0, slice(1, 2))] + [(j, slice(2 * j, 2 * j + 2)) for j in range(1, 4)]

        def ln_dve(dve, m, n, g, b, ahead=None):
            dve.wait_ge(*done(("mean", m)))
            pairs = [slice(2 * j, 2 * j + 2) for j in range(4)]
            for j, p in enumerate(pairs):
                dve.tensor_tensor(X[:, p, :], X[:, p, :], over(MISC[:, 0:T], 2), ALU.subtract)\
                    .then_inc(*raised("centered", ("centered", m, j)))
            dve.wait_ge(*done(("squares", m, 3)))
            dve.tensor_tensor(SQ[:, 4:6, :], SQ[:, 4:6, :], SQ[:, 6:8, :], ALU.add)\
                .then_inc(*raised("upper_squares", ("upper_squares", m)))
            if ahead is not None:
                dve_ahead(dve, ahead)
            dve.wait_ge(*done(("mean2", m)))
            var = small[:, 140:142]
            dve.tensor_scalar(var, OUTP[:, 0:QT], LN_EPS, None, ALU.add).then_inc(*raised("variance", ("var", m)))
            dve.wait_ge(*done(("root", m)))
            dve.reciprocal(var, var).then_inc(*raised("ln_factor", ("inverse_root", m)))
            dve.wait_ge(*done(("inverse_root", m)))
            for r in range(QT):
                ins = dve.tensor_scalar(DIAG[:, r, :], ident, var[:, r:r + 1], None, ALU.mult)
            ins.then_inc(*raised("diagonal", ("diagonal", m)))
            dve.wait_ge(*done(("rstd", m)))

            def scale(u):
                name, p = LN_PARTS[u]
                dve.tensor_tensor(W[:, p, :], X[:, p, :], over(OUTP[:, T:2 * T], p.stop - p.start), ALU.mult)\
                    .then_inc(*raised("normed", ("normed", m, name)))

            scale(0)
            for u, (name, p) in enumerate(LN_PARTS):
                dve.wait_ge(*done(("normed", m, name)))
                for k in range(p.start, p.stop):
                    ins = dve.tensor_scalar(X[:, k, :], W[:, k, :], prm(g)[:, k:k + 1], prm(b)[:, k:k + 1],
                                            ALU.mult, ALU.add)
                ins.then_inc(*raised("ln_out", ("ln_out", m, name)))
                if u + 1 < len(LN_PARTS):
                    scale(u + 1)
                if n is None:
                    K.alias(("resid", "stack2", name), ("ln_out", m, name))
                    if u >= 2:
                        rms_low_dve(dve, 2, "ffn1_norm0", name - 1)
                    continue
                dve.wait_ge(*done(("ln_out", m, name)))
                dve.wait_ge(*done(("x_high", n, name)))
                dve.tensor_tensor(XL[:, p, :], X[:, p, :], XH[:, p, :].bitcast(F32), ALU.subtract)\
                    .then_inc(*raised("x_split", ("x_split", n, name)))

        def warm(act, func):
            act.activation(small[:, 143:144], ones_v[:, 0:1], func)

        def ln_act(act, m, n, g, b):
            warm(act, ACT.Sqrt)
            for j in range(4):
                act.wait_ge(*done(("centered", m, j)))
                act.activation(SQ[:, 2 * j:2 * j + 2, :], X[:, 2 * j:2 * j + 2, :], ACT.Square)\
                    .then_inc(*raised("squares_ready", ("squares", m, j)))
            act.wait_ge(*done(("var", m)))
            act.activation(small[:, 140:142], small[:, 140:142], ACT.Sqrt).then_inc(*raised("deviation", ("root", m)))
            if n is None:
                return
            for name, p in LN_PARTS:
                act.wait_ge(*done(("normed", m, name)))
                for k in range(p.start, p.stop):
                    ins = act.activation(XH[:, k, :], W[:, k, :], ACT.Identity, scale=prm(g)[:, k:k + 1],
                                         bias=prm(b)[:, k:k + 1])
                ins.then_inc(*raised("x_high", ("x_high", n, name)))

        def rms_high_act(act, m, n, g, b):
            act.wait_ge(*done(("resid", m, b)))
            for k in (2 * b, 2 * b + 1):
                ins = act.activation(XH[:, k, :], X[:, k, :], ACT.Identity, scale=prm(g)[:, k:k + 1])
            ins.then_inc(*raised("x_tile_high", ("xh", n, b)))

        def rms_low_dve(dve, n, g, b):
            dve.wait_ge(*done(("xh", n, b)))
            for k in (2 * b, 2 * b + 1):
                ins = dve.scalar_tensor_tensor(out=XL[:, k, :], in0=X[:, k, :], scalar=prm(g)[:, k:k + 1],
                                               in1=XH[:, k, :].bitcast(F32), op0=ALU.mult, op1=ALU.subtract)
            ins.then_inc(*raised("x_split", ("x_split", n, b)))

        def rms_squares_act(act, m):
            for b in (2, 3):
                act.wait_ge(*done(("resid", m, b)))
            act.activation(SQ[:, 4:8, :], X[:, 4:8, :], ACT.Square).then_inc(*raised("squares_ready", ("squares", m)))

        def rms_squares_pool(pool, m):
            for b in range(2):
                p = slice(2 * b, 2 * b + 2)
                pool.wait_ge(*done(("resid", m, b)))
                pool.tensor_tensor(SQ[:, p, :], X[:, p, :], X[:, p, :], ALU.mult)\
                    .then_inc(*raised("pool_squares", ("pool_squares", m, b)))
            pool.wait_ge(*done(("pool_squares", m, 1)))
            pool.tensor_tensor(SQ[:, 0:2, :], SQ[:, 0:2, :], SQ[:, 2:4, :], ALU.add)\
                .then_inc(*raised("pool_squares", ("pool_squares", m, "sum")))

        def rms_sums_dve(dve, m):
            dve.wait_ge(*done(("squares", m)))
            dve.tensor_tensor(SQ[:, 4:6, :], SQ[:, 4:6, :], SQ[:, 6:8, :], ALU.add)\
                .then_inc(*raised("square_sums", ("upper_sum", m)))
            dve.wait_ge(*done(("pool_squares", m, "sum")))
            dve.wait_ge(*done(("upper_sum", m)))
            dve.tensor_tensor(SQ[:, 0:2, :], SQ[:, 0:2, :], SQ[:, 4:6, :], ALU.add)\
                .then_inc(*raised("square_sums", ("sums", m)))

        def rms_pe(pe, m):
            misc_free(pe)
            pe.wait_ge(*done(("sums", m)))
            for t in range(2):
                mm = pe.matmul(MISC[:, 0:T], ones_d[:, :], SQ[:, t, :], start=t == 0, stop=t == 1)
            mm.then_inc(*raised("mean_ready", ("mean", m)))
            Misc.read = ("var", m)

        def rms_act(act, m):
            act.wait_ge(*done(("var", m)))
            act.activation(RS[:, :], RS[:, :], ACT.Sqrt).then_inc(*raised("deviation", ("root", m)))

        def rms_dve(dve, m):
            dve.wait_ge(*done(("mean", m)))
            dve.tensor_scalar(RS[:, :], MISC[:, 0:T], RMS_EPS, None, ALU.add).then_inc(*raised("variance", ("var", m)))
            dve.wait_ge(*done(("root", m)))
            dve.reciprocal(RS[:, :], RS[:, :]).then_inc(*raised("rms_factor", ("rms", m)))
            dve.wait_ge(*done(("rms", m)))

        def in_act(act, m, j):
            act.wait_ge(*done(("in", m, j)))
            act.activation(FEAT[:, 2 * j:2 * j + 2, :], banks[Bank.used[m, j]], ACT.Copy)\
                .then_inc(*raised("panel_read", ("in", m, j, "read")))

        def in_dve(dve, m, j):
            dve.wait_ge(*done(("in", m, j)))
            dve.tensor_tensor(FEAT[:, 2 * j:2 * j + 2, :], banks[Bank.used[m, j]], over(RS[:, :], 2), ALU.mult)\
                .then_inc(*raised("panel_scaled", ("in", m, j, "read")))

        def rope_pe(pe, tag, src, after, matrix):
            pe.wait_ge(*done(after))
            misc_free(pe)
            for t in range(src.shape[1]):
                mm = pe.matmul(misc[:, t, :], prm(matrix), src[:, t, :], start=True, stop=True)
            mm.then_inc(*raised("rotated", (tag, "rotated")))
            Misc.read = (tag, "sin")

        def rope_dve(dve, tag, cs, w):
            dve.wait_ge(*done((tag, "rotated")))
            if Misc.rope is not None:
                dve.wait_ge(*done(Misc.rope))
            dve.tensor_tensor(ROT[:, 0:w, :], misc[:, 0:w, :], over(ropes[:, cs + 1, :], w), ALU.mult)\
                .then_inc(*raised("sin_part", (tag, "sin")))
            Misc.rope = (tag, "done")

        def rope_pool(pool, tag, src, dst, cs):
            w = src.shape[1]
            pool.wait_ge(*done((tag, "rotated")))
            pool.tensor_tensor(dst, src, over(ropes[:, cs, :], w), ALU.mult)\
                .then_inc(*raised("cos_part", (tag, "cos")))
            pool.wait_ge(*done((tag, "sin")))
            pool.wait_ge(*done((tag, "cos")))
            pool.tensor_tensor(dst, dst, ROT[:, 0:w, :], ALU.add).then_inc(*raised("rotation_added", (tag, "done")))

        class Misc:
            read = None
            outp = None
            accs = None
            rope = None

        def misc_free(pe):
            if Misc.read is not None:
                pe.wait_ge(*done(Misc.read))

        def outp_free(pe):
            if Misc.outp is not None:
                pe.wait_ge(*done(Misc.outp))

        def turn_pe(pe, tag, tiles, after):
            pe.wait_ge(*done(after))
            outp_free(pe)
            for r in range(QT):
                for n, t in enumerate(tiles):
                    mm = pe.transpose(OUTP[:, (r * len(tiles) + n) * P:(r * len(tiles) + n + 1) * P],
                                      t[:, r * P:(r + 1) * P], ident)
            mm.then_inc(*raised("turned", (tag, "turned")))
            Misc.outp = (tag, "copied")

        def turn_act(act, tag, n, dst, func=ACT.Copy):
            act.wait_ge(*done((tag, "turned")))
            act.activation(dst, OUTP[:, 0:QT * n * P].rearrange("p (r c) -> p r c", r=QT)[:, :, 0:dst.shape[2]],
                           func).then_inc(*raised("psum_copied", (tag, "copied")))

        FULL = ((0, P), (P, SEQ_K))
        BLOCKWISE = ((0, NCMP), (NCMP, QT * NCMP))

        class Item:
            def __init__(self, tag, q, k, v, keys, mask, after=(), sink=None, gate=None, any_key=None):
                self.tag, self.q, self.k, self.v, self.keys, self.mask = tag, q, k, v, keys, mask
                self.after, self.sink, self.gate, self.any_key = after, sink, gate, any_key

        def in_pairs(m, pairs):
            items = []
            for n, (tile, its) in enumerate(pairs):
                for it in its:
                    it.pair, it.tile, it.m, it.slot = n, tile, m, len(items) % 2
                    it.prob = PROBS[len(items) % 3]
                    it.stats = [small[:, 20 * (len(items) % 3) + 4 * i:20 * (len(items) % 3) + 4 * i + 4]
                                for i in range(5)]
                    it.first, it.last = it is its[0], it is its[-1]
                    it.out = (outp if n % 2 == 0 else misc)[:, 0, :]
                    items.append(it)
            return items

        PROBS = [SM[:, 0:2, :], SM[:, 2:4, :],
                 W[:, 2:5, :].rearrange("p a t -> p (a t)").rearrange("p (h k) -> p h k", h=2)]

        def hr(ap):
            return ap.rearrange("p (h r) -> p h r", r=QT)

        def scores_pe(pe, items, n):
            it = items[n]
            for e in it.after:
                pe.wait_ge(*done(e))
            if n >= 2:
                pe.wait_ge(*done((items[n - 2].tag, "masked")))
            elif Misc.accs is not None:
                pe.wait_ge(*done(Misc.accs))
            for h in range(2):
                for r, (lo, hi) in enumerate(it.keys):
                    mm = pe.matmul(ACC[:, 2 * it.slot + h, lo:hi], it.q[h][:, r * P:(r + 1) * P],
                                   it.k[h][:, 0:hi - lo], start=True, stop=True)
            mm.then_inc(*raised("scores_done", (it.tag, "scores")))

        def start_attention_pe(pe, items):
            for n in range(2):
                scores_pe(pe, items, n)

        def turn_into(items, n):
            s = 2 * items[n].slot
            return ACC[:, s:s + 2, :] if n >= len(items) - 2 else PAN[:, :, :]

        def turn_probs_pe(pe, items, n):
            it, to = items[n], turn_into(items, n)
            pe.wait_ge(*done((it.tag, "probs")))
            if n == 0:
                for b in range(2):
                    pe.wait_ge(*done(Bank.read[b]))
            elif n < len(items) - 2:
                pe.wait_ge(*done((items[n - 1].tag, "copied")))
            for h in range(2):
                if it.keys is FULL:
                    for b in range(3):
                        mm = pe.transpose(to[:, h, b * P:(b + 1) * P], it.prob[:, h, b * P:(b + 1) * P], ident)
                else:
                    for r, (lo, hi) in enumerate(it.keys):
                        mm = pe.transpose(to[0:NCMP, h, r * P:(r + 1) * P], it.prob[:, h, lo:hi], ident)
            mm.then_inc(*raised("turned", (it.tag, "turned")))

        def apply_pe(pe, items, n):
            it = items[n]
            pe.wait_ge(*done((it.tag, "copied")))
            if it.first:
                pe.wait_ge(*done(("zero", it.m, it.pair)))
            for h in range(2):
                o = it.out[h * DH:(h + 1) * DH, :]
                pt = PT[:, 2 * it.slot + h, :]
                if it.keys is FULL:
                    pe.matmul(o, it.v(h, 0), pt[:, 0:T], start=False, stop=False, skip_group_check=True)
                    mm = pe.matmul(o[:, P:T], it.v(h, 1), pt[:, T:SEQ_K], start=False, stop=False,
                                   skip_group_check=True)
                else:
                    mm = pe.matmul(o, it.v(h, 0), pt[0:NCMP, 0:T], start=False, stop=False,
                                   skip_group_check=True)
            mm.then_inc(*raised("attended", (it.tag, "out")))

        def attention_pe(pe, items):
            last = len(items) - 1
            for n in range(last - 1):
                turn_probs_pe(pe, items, n)
                if n + 3 <= last:
                    scores_pe(pe, items, n + 3)
                else:
                    turn_probs_pe(pe, items, n + 1)
                apply_pe(pe, items, n)
            Misc.accs = (items[-1].tag, "copied")
            Bank.read = [(items[-3].tag, "copied")] * 2
            Misc.read = ("o_split", items[-1].m, [it.tile for it in items if it.pair % 2][-1])
            Misc.outp = ("o_split", items[-1].m, [it.tile for it in items if it.pair % 2 == 0][-1])

        def exps_act(act, items, n):
            it = items[n]
            _, minus_max, total, _, sink_part = it.stats
            if it.sink is not None:
                act.wait_ge(*done((it.tag, "sink_less")))
                act.activation(sink_part, sink_part, ACT.Exp).then_inc(*raised("sink_exp", (it.tag, "sink_exp")))
            act.wait_ge(*done((it.tag, "max")))
            for h in range(2):
                for r, (lo, hi) in enumerate(it.keys):
                    x = it.prob[:, h, lo:hi]
                    j = 2 * h + r
                    ins = act.activation(x, x, ACT.Exp, bias=minus_max[:, j:j + 1], accum_out=total[:, j:j + 1])
            ins.then_inc(*raised("exps_ready", (it.tag, "exps")))

        def masked_max_dve(dve, items, n):
            it = items[n]
            top, minus_max, _, _, sink_part = it.stats
            s, w = slice(2 * it.slot, 2 * it.slot + 2), it.keys[1][1]
            dve.wait_ge(*done((it.tag, "scores")))
            if n == 2:
                dve.wait_ge(*done(Misc.rope))
            if n >= 3:
                dve.wait_ge(*done((items[n - 3].tag, "turned")))
            dve.scalar_tensor_tensor(out=it.prob[:, :, 0:w], in0=ACC[:, s, 0:w], scalar=SCALE,
                                     in1=over(it.mask, 2), op0=ALU.mult, op1=ALU.add)\
                .then_inc(*raised("scores_masked", (it.tag, "masked")))
            dve.wait_ge(*done((it.tag, "masked")))
            for r, (lo, hi) in enumerate(it.keys):
                ins = dve.tensor_reduce(hr(top)[:, :, r], it.prob[:, :, lo:hi], AX.X, ALU.max)
            ins.then_inc(*raised("row_max", (it.tag, "mx")))
            dve.wait_ge(*done((it.tag, "mx")))
            if it.sink is not None:
                sink = it.sink.rearrange("p (h r) -> p h r", r=1).broadcast_to([P, 2, QT])
                dve.tensor_tensor(hr(top), hr(top), sink, ALU.max)\
                    .then_inc(*raised("row_max_with_sink", (it.tag, "mxs")))
                dve.wait_ge(*done((it.tag, "mxs")))
                dve.tensor_tensor(hr(sink_part), sink, hr(top), ALU.subtract)\
                    .then_inc(*raised("sink_less", (it.tag, "sink_less")))
            dve.tensor_scalar(minus_max, top, -1.0, None, ALU.mult).then_inc(*raised("negated_max", (it.tag, "max")))

        def high_act(act, it):
            act.wait_ge(*done((it.tag, "out")))
            act.activation(OH[:, it.tile, :], it.out, ACT.Copy)\
                .then_inc(*raised("o_high_ready", ("oh", it.m, it.tile)))

        def softmax_after(items):
            return {0: 2, 2: 3} if len(items) == 4 else {n: n + 2 for n in range(len(items) - 2)}

        def attention_act(act, items):
            for n, it in enumerate(items):
                act.wait_ge(*done((it.tag, "turned")))
                if n >= 2:
                    act.wait_ge(*done((items[n - 2].tag, "out")))
                s = slice(2 * it.slot, 2 * it.slot + 2)
                turned = turn_into(items, n)
                if it.keys is FULL:
                    ins = act.activation(PT[:, s, :], turned[:, :, 0:SEQ_K], ACT.Copy)
                else:
                    ins = act.activation(PT[0:NCMP, s, 0:T], turned[0:NCMP, :, 0:T], ACT.Copy)
                ins.then_inc(*raised("psum_copied", (it.tag, "copied")))
                if n and items[n - 1].last:
                    high_act(act, items[n - 1])
                if n in softmax_after(items):
                    exps_act(act, items, softmax_after(items)[n])

        def low_dve(dve, it):
            dve.wait_ge(*done(("oh", it.m, it.tile)))
            dve.tensor_tensor(OL[:, it.tile, :], it.out, OH[:, it.tile, :].bitcast(F32), ALU.subtract)\
                .then_inc(*raised("o_low_ready", ("o_split", it.m, it.tile)))

        def last_low_dve(dve, items):
            for it in items[-2:]:
                if it.last:
                    low_dve(dve, it)

        def attention_dve(dve, items, misc_last, outp_last, started=1):
            def normalise(it):
                _, _, total, factor, sink_part = it.stats
                dve.wait_ge(*done((it.tag, "exps")))
                if it.sink is not None:
                    dve.wait_ge(*done((it.tag, "sink_exp")))
                    dve.tensor_tensor(total, total, sink_part, ALU.add).then_inc(*raised("row_sum", (it.tag, "sum")))
                    dve.wait_ge(*done((it.tag, "sum")))
                dve.reciprocal(factor, total).then_inc(*raised("sum_inverted", (it.tag, "rc")))
                dve.wait_ge(*done((it.tag, "rc")))
                if it.any_key is not None:
                    dve.tensor_tensor(hr(factor), hr(factor), over(it.any_key, 2), ALU.mult)\
                        .then_inc(*raised("empty_rows_cleared", (it.tag, "rc_any")))
                    dve.wait_ge(*done((it.tag, "rc_any")))
                if it.gate is not None:
                    dve.tensor_tensor(hr(factor), hr(factor), it.gate, ALU.mult)\
                        .then_inc(*raised("gate_applied", (it.tag, "gated")))
                    dve.wait_ge(*done((it.tag, "gated")))
                for r, (lo, hi) in enumerate(it.keys):
                    ins = dve.tensor_tensor(it.prob[:, :, lo:hi], it.prob[:, :, lo:hi],
                                            hr(factor)[:, :, r:r + 1].broadcast_to([P, 2, hi - lo]), ALU.mult)
                ins.then_inc(*raised("probs_ready", (it.tag, "probs")))

            def zero(it):
                dve.memset(it.out, 0.0).then_inc(*raised("out_zeroed", ("zero", it.m, it.pair)))

            firsts = [it for it in items if it.first]
            for n, it in enumerate(items):
                normalise(it)
                if n == 0 and started == 1:
                    masked_max_dve(dve, items, 1)
                if n in softmax_after(items):
                    masked_max_dve(dve, items, softmax_after(items)[n])
                if n == 0:
                    dve.wait_ge(*done(outp_last))
                    zero(firsts[0])
                    dve.wait_ge(*done(misc_last))
                    zero(firsts[1])
                if n >= 2 and items[n - 2].last:
                    low_dve(dve, items[n - 2])
                    if items[n - 2].pair + 2 < len(firsts):
                        dve.wait_ge(*done(("o_split", items[n - 2].m, items[n - 2].tile)))
                        zero(firsts[items[n - 2].pair + 2])

        def split_w_act(act, m, tiles, after):
            for e in after:
                act.wait_ge(*done(e))
            act.activation(OH[:, tiles, :], W[:, tiles, :], ACT.Copy)\
                .then_inc(*raised("o_high_ready", ("oh", m, tiles.start)))

        def split_w_dve(dve, m, tiles):
            dve.wait_ge(*done(("oh", m, tiles.start)))
            dve.tensor_tensor(OL[:, tiles, :], W[:, tiles, :], OH[:, tiles, :].bitcast(F32), ALU.subtract)\
                .then_inc(*raised("o_low_ready", ("o_split", m, tiles.start)))
            K.alias(("o_split", m, tiles.start + 1), ("o_split", m, tiles.start))

        POOL0 = 6
        PUf = FEAT[:, 14:20, :].rearrange("p a t -> p (a t)")
        PU = [PUf[:, n * 2 * (T + POOL_PAD):(n + 1) * 2 * (T + POOL_PAD)].rearrange("p (a t) -> p a t", a=2)
              for n in range(2)]
        SMf = SM[:, :, :].rearrange("p a b -> p (a b)")
        SUMS = G2[:, 0]
        CV = QR[:, 2:6, :].rearrange("p a t -> p (a t)")[:, 0:2 * (T + 2)].rearrange("p (a t) -> p a t", a=2)

        def mix1_items(l):
            pairs = []
            for n in range(4):
                q = [FEAT[h * DH:(h + 1) * DH, n, :] for h in range(2)]
                k = [KD[h * DH:(h + 1) * DH, n // 2, :] for h in range(2)]
                pairs.append((2 + n, [Item(("att", l, n), q, k, lambda h, r, g=n // 2: VT[:, r, g * DH:(g + 1) * DH],
                                           FULL, prm("window"), after=[("kd", l), (("v", l), "copied")],
                                           sink=prm(f"sinks{l}")[:, 2 * n:2 * n + 2])]))
            return in_pairs(("mix", l), pairs)

        def gate_pe(pe, l, c1, j, g):
            pe_panel(pe, c1 + 4 * j + g, (j + g) % 2, ("gate", l, j, g))

        def merge_pe(pe, l, c1):
            for j in range(KT // 2):
                for g in range(0 if j else 2, 3):
                    gate_pe(pe, l, c1, j, g)
                c = c1 + 4 * j + 3
                weights_ready(pe, c)
                if j == 0:
                    for t in range(KT):
                        pe.wait_ge(*done(("o_split", ("mix", l), t)))
                else:
                    pe.wait_ge(*done(("merge", l, j - 1, 2)))
                for b, ks in enumerate((range(0, 2), range(2, 6), range(6, 8))):
                    multiply(pe, acc[b], c % RING, OH, OL, ks).then_inc(*raised("acc_done", ("branch", l, j, b)))
                K.alias(("used", c), ("branch", l, j, 2))
            Misc.accs = ("merge", l, KT // 2 - 1, 2)

        GS = FEAT

        def merge_act(act, l, c1, items):
            def high(j):
                act.wait_ge(*done(("merge_sum", l, j, 1)))
                act.activation(XH[:, 2 * j:2 * j + 2, :], W[:, 2 * j:2 * j + 2, :], ACT.Copy)\
                    .then_inc(*raised("merged_high", ("merged_high", l, j)))

            for j in range(KT // 2):
                for g in range(3):
                    act_ahead(act, c1 + 4 * j + g)
                    act.wait_ge(*done(("gate", l, j, g)))
                    if j:
                        act.wait_ge(*done(("merge", l, j - 1, g)))
                    act.activation(GS[:, 14 + 2 * g:16 + 2 * g, :], banks[(j + g) % 2], ACT.Sigmoid)\
                        .then_inc(*raised("panel_read", ("gate", l, j, g, "read")))
                    if j == 0 and g == 0:
                        split_w_act(act, ("mix", l), slice(6, 8), [("conv_out", l)])
                    if j == 0 and g == 1:
                        high_act(act, items[-1])
                if j == KT // 2 - 1:
                    for i in range(j):
                        high(i)
                act_ahead(act, c1 + 4 * j + 3)
            high(KT // 2 - 1)

        def merge_dve(dve, l, c1, items):
            def low(j):
                dve.wait_ge(*done(("merged_high", l, j)))
                dve.tensor_tensor(XL[:, 2 * j:2 * j + 2, :], W[:, 2 * j:2 * j + 2, :],
                                  XH[:, 2 * j:2 * j + 2, :].bitcast(F32), ALU.subtract)\
                    .then_inc(*raised("merged_low", ("merged_split", l, j)))

            for j in range(KT // 2):
                for g in range(4 if j < KT // 2 - 1 else 3):
                    dve_ahead(dve, c1 + 4 * j + g)
                    if j == 0 and g == 1:
                        split_w_dve(dve, ("mix", l), slice(6, 8))
                        last_low_dve(dve, items)
                w = W[:, 2 * j:2 * j + 2, :]
                for g in range(3):
                    if j == KT // 2 - 1 and g < 2:
                        for i in ((0,), (1, 2))[g]:
                            low(i)
                    dve.wait_ge(*done(("gate", l, j, g, "read")))
                    dve.wait_ge(*done(("branch", l, j, g)))
                    t = GS[:, 14 + 2 * g:16 + 2 * g, :]
                    dst = w if g == 0 else (G2[:, g - 1])
                    if g and j:
                        dve.wait_ge(*done(("merge_sum", l, j - 1, g - 1)))
                    dve.tensor_tensor(dst, t, acc[g], ALU.mult).then_inc(*raised("gate_times_branch", ("merge", l, j, g)))
                    if g:
                        dve.wait_ge(*done(("merge", l, j, g)))
                        if g == 2:
                            dve.wait_ge(*done(("merge_sum", l, j, 0)))
                        dve.tensor_tensor(w, w, G2[:, g - 1], ALU.add)\
                            .then_inc(*raised("merged", ("merge_sum", l, j, g - 1)))
            low(KT // 2 - 1)
            dve_ahead(dve, c1 + GATE1 - 1)

        def mix1_pe(pe, l, c0):
            m = ("mix", l)
            read = [("in", m, j, "read") for j in range(IN1)]
            items = mix1_items(l)
            for j in range(IN1):
                in_pe(pe, m, c0 + j, j, j)
                if l == 0 and j == 1:
                    pe.wait_ge(*done("params_loaded"))
                if 1 <= j <= 2:
                    rope_pe(pe, ("rope", l, j - 1), FEAT[:, 2 * j - 2:2 * j, :], read[j - 1], "rotate")
                if j == 3:
                    rope_pe(pe, ("rope", l, 2), FEAT[:, 4:5, :], read[2], "rotate")
                    turn_pe(pe, ("v", l), [FEAT[:, 5, :]], read[2])
                if j == 5:
                    pe.wait_ge(*done(("pooled", l)))
                    misc_free(pe)
                    for t in range(2):
                        mm = pe.matmul(misc[:, t, :], prm(f"w_pool{l}")[:, t * P:(t + 1) * P], SUMS[:, t, :],
                                       start=True, stop=True)
                    mm.then_inc(*raised("pool_mixed", ("pool_mixed", l)))
                    Misc.read = ("pool_out", l)
                    start_attention_pe(pe, items)
            scores_pe(pe, items, 2)
            attention_pe(pe, items)
            gate_pe(pe, l, c0 + IN1, 0, 0)
            turn_probs_pe(pe, items, 3)
            apply_pe(pe, items, 2)
            gate_pe(pe, l, c0 + IN1, 0, 1)
            apply_pe(pe, items, 3)
            merge_pe(pe, l, c0 + IN1)
            out_pe(pe, ("mix_out", l), c0 + IN1 + GATE1, XH, XL, [("merged_split", l, k // 2) for k in range(KT)])

        def mix1_act(act, l, c0):
            m = ("mix", l)
            items = mix1_items(l)
            for j in range(IN1):
                act_ahead(act, c0 + j)
                if l == 0 and j == 1:
                    rope_tables_act(act, 0)
                if j == 6:
                    exps_act(act, items, 0)
                    act.wait_ge(*done(("pool_mixed", l)))
                    for t in range(2):
                        ins = act.activation(W[:, t, :], misc[:, t, :], ACT.Copy,
                                             scale=prm(f"pool_scale{l}")[:, t:t + 1])
                    ins.then_inc(*raised("pool_out", ("pool_out", l)))
                in_act(act, m, j)
                if j == 4:
                    act.wait_ge(*done((("rope", l, 2), "done")))
                    for g in range(2):
                        for h in range(2):
                            ins = act.activation(KD[h * DH:(h + 1) * DH, g, :], FEAT[g * DH:(g + 1) * DH, 4, :],
                                                 ACT.Copy)
                    ins.then_inc(*raised("keys_doubled", ("kd", l)))
                    turn_act(act, ("v", l), 1, VT[:, :, 0:P])
            exps_act(act, items, 1)
            split_w_act(act, m, slice(0, 2), [("pool_out", l)])
            attention_act(act, items)
            merge_act(act, l, c0 + IN1, items)
            out_act(act, ("mix_out", l), c0 + IN1 + GATE1)

        def mix1_dve(dve, l, c0):
            m = ("mix", l)
            items = mix1_items(l)
            for j in range(IN1):
                dve_ahead(dve, c0 + j)
                if l == 0 and j == 0:
                    rope_tables(dve, 0)
                if l == 0 and j == 1:
                    dve.wait_ge(*done(("tables", 0, "done")))
                if 1 <= j <= 2:
                    rope_dve(dve, ("rope", l, j - 1), 0, 2)
                if j == 3:
                    rope_dve(dve, ("rope", l, 2), 0, 1)
                if j == 4:
                    pool_dve(dve, l, ("in", m, 3, "read"))
            for n in range(2):
                masked_max_dve(dve, items, n)
            attention_dve(dve, items, ("pool_out", l), (("v", l), "copied"), started=2)
            split_w_dve(dve, m, slice(0, 2))
            conv_dve(dve, l, m)
            merge_dve(dve, l, c0 + IN1, items)
            out_dve(dve, ("mix_out", l), c0 + IN1 + GATE1, True)

        def pool_dve(dve, l, after):
            for n in range(2):
                ins = dve.memset(PU[n][:, :, 0:POOL_PAD], 0.0)
            ins.then_inc(*raised("pool_zero", ("pool_zero", l)))
            dve.wait_ge(*done(after))
            dve.wait_ge(*done(("pool_zero", l)))
            u = FEAT[:, POOL0:POOL0 + 2, :]
            dve.tensor_copy(PU[0][:, :, POOL_PAD:], u).then_inc(*raised("pool_sum", ("pool_sum", l, 0)))
            for n in range(4):
                src, dst, shift = PU[n % 2], PU[(n + 1) % 2], 1 << n
                dve.wait_ge(*done(("pool_sum", l, n)))
                if n:
                    dve.wait_ge(*done(("pool_pick", l, n - 1)))
                dve.tensor_tensor(dst[:, :, POOL_PAD:], src[:, :, POOL_PAD:],
                                  src[:, :, POOL_PAD - shift:POOL_PAD - shift + T], ALU.add)\
                    .then_inc(*raised("pool_sum", ("pool_sum", l, n + 1)))
                dve.wait_ge(*done(("pool_sum", l, n + 1)))
                half = slice((n % 2) * DH, (n % 2 + 1) * DH)
                cnt = prm("per_count").rearrange("p (a t) -> p a t", a=2)
                dve.tensor_tensor(SUMS[half, n // 2, :], dst[half, n // 2, POOL_PAD:], cnt[half, n // 2, :],
                                  ALU.mult).then_inc(*raised("pool_pick", ("pool_pick", l, n)))
            dve.wait_ge(*done(("pool_pick", l, 3)))
            dve.tensor_tensor(SUMS, SUMS, u, ALU.subtract).then_inc(*raised("pooled", ("pooled", l)))

        def conv_dve(dve, l, m):
            dve.wait_ge(*done(("in", m, 5, "read")))
            dve.memset(CV[:, :, 0:2], 0.0).then_inc(*raised("conv_pad_zeroed", ("cv_zero", l)))
            dve.tensor_tensor(CV[:, :, 2:], FEAT[:, 10:12, :], FEAT[:, 8:10, :], ALU.mult)\
                .then_inc(*raised("conv_input", ("cv_in", l)))
            dve.wait_ge(*done(("cv_zero", l)))
            dve.wait_ge(*done(("cv_in", l)))
            cw = prm(f"conv_w{l}")
            for tap in range(3):
                if tap:
                    dve.wait_ge(*done(("cv_tap", l, tap - 1)))
                for t in range(2):
                    k = cw[:, 3 * t + tap:3 * t + tap + 1]
                    src = CV[:, t, tap:tap + T]
                    dst = W[:, 6 + t, :]
                    if tap == 0:
                        ins = dve.tensor_scalar(dst, src, k, None, ALU.mult)
                    else:
                        ins = dve.scalar_tensor_tensor(out=dst, in0=src, scalar=k, in1=dst, op0=ALU.mult, op1=ALU.add)
                ins.then_inc(*raised("conv_tap", ("cv_tap", l, tap)))
            dve.wait_ge(*done(("cv_tap", l, 2)))
            dve.wait_ge(*done(("in", m, 6, "read")))
            dve.tensor_tensor(W[:, 6:8, :], W[:, 6:8, :], FEAT[:, 12:14, :], ALU.mult)\
                .then_inc(*raised("conv_out", ("conv_out", l)))

        def half(col):
            return FEAT[(col % 2) * DH:(col % 2 + 1) * DH, col // 2, :]

        PTf = PT[:, :, :].rearrange("p a b -> p (a b)")
        UPf = UP[:, :, :, :].rearrange("p a b c -> p (a b c)")
        G2f = G2[:, :, :, :].rearrange("p a b c -> p (a b c)")
        SHW = T + CMP_STRIDE
        NB = B_KV * NCMP
        SHIFT = {x: t[:, 0:B_KV * SHW].rearrange("p (g t) -> p g t", g=B_KV) for x, t in (("k", SMf), ("v", PTf))}
        BLOCKS = {x: t[:, 0:CMP_STRIDE * NB] for x, t in (("k", G2f), ("v", UPf))}
        OHf = OH[:, :, :].rearrange("p k t -> p (k t)")
        OLf = OL[:, :, :].rearrange("p k t -> p (k t)")
        HIDDEN = W[0:NB, 4:6, :]
        VG = A
        RV = SIL[:, 0, :]
        GT = small[:, 64:64 + QT * 36].rearrange("p (r c) -> p r c", r=QT)
        GTh = small[:, 64:64 + QT * 36].rearrange("p (r h b) -> p b h r", r=QT, b=3)

        def ev_items(m):
            pairs = []
            for n in range(B_HEADS // 2):
                g = n // 2
                hs = [slice(h * DH, (h + 1) * DH) for h in range(2)]
                q_raw, q_rot = [[t[h, tile, :] for h in hs] for t, tile in ((FEAT, 4 + n), (QR, n))]
                gate = [GTh[:, b, 2 * n:2 * n + 2, :] for b in range(3)]
                items = [Item(("cmp_att", n), q_raw, [KC[h, g, :] for h in hs], lambda h, r, g=g: VC[0:NCMP, g, :],
                              BLOCKWISE, prm("cmp_mask"), after=[("kc",), ("in", m, 2 + n // 2, "read")],
                              gate=gate[0], any_key=prm("cmp_any"))]
                for b, name in enumerate(("sel_att", "win_att")):
                    items.append(Item((name, n), q_rot, [KD[h, 3 * b + g, :] for h in hs],
                                      lambda h, r, at=(3 * b + g) * DH: VT[:, r, at:at + DH], FULL, prm("causal"),
                                      after=[("kd", m), (("rope_q", m, n // 2), "done")], gate=gate[1 + b]))
                pairs.append((2 + n, items))
            return in_pairs(m, pairs)

        EV_STEPS = EV_ORDER[:EV_EARLY] + ("k0", "k1", "v0", "v1") + EV_ORDER[EV_EARLY:]

        def compress_pe(pe, c, x, j):
            n = "kv".index(x)
            if j == 0:
                pe.wait_ge(*done(("blocks", x)))
            weights_ready(pe, c)
            for k in range(KT):
                w = slice(k * 2 * P, (k + 1) * 2 * P)
                at0 = n * 768 + (j * KT + k) * NB
                hi, lo = OHf[:, at0:at0 + NB], OLf[:, at0:at0 + NB]
                dst = ACC[0:NB, n, 0:2 * P]
                s = c % RING
                pe.matmul(dst, hi, w_high[:, s, w], start=j == 0 and k == 0, stop=False)
                pe.matmul(dst, lo, w_high[:, s, w], start=False, stop=False)
                mm = pe.matmul(dst, hi, w_low[:, s, w], start=False, stop=j == 1 and k == KT - 1)
            mm.then_inc(*raised("panel_done", ("cmp", x, j)))
            K.alias(("used", c), ("cmp", x, j))

        def ev_pe(pe, m, c0, norm):
            items = ev_items(m)
            for step, j in enumerate(EV_STEPS):
                if j in ("k0", "k1", "v0", "v1"):
                    compress_pe(pe, c0 + step, j[0], int(j[1]))
                else:
                    in_pe(pe, m, c0 + step, step, j)
                if step == 0:
                    rms_pe(pe, norm)
                if step == 2:
                    pe.wait_ge(*done(("v_squares",)))
                    misc_free(pe)
                    for t in range(2):
                        mm = pe.matmul(MISC[:, 0:T], ones_v[:, :], W[:, 6 + t, :], start=t == 0, stop=t == 1)
                    mm.then_inc(*raised("v_mean", ("v_mean",)))
                    Misc.read = ("v_var",)
                if step == 4:
                    rope_pe(pe, ("rope_k", m, 0), FEAT[:, 13:14, :], ("in", m, 6, "read"), "rotate")
                if step == 5:
                    rope_pe(pe, ("rope_k", m, 1), FEAT[:, 14:16, :], ("in", m, 7, "read"), "rotate")
                    turn_pe(pe, ("vg",), [W[:, 4, :], W[:, 5, :]], ("v_scaled",))
                if step == 6:
                    pe.wait_ge(*done((("vg",), "copied")))
                    misc_free(pe)
                    for c in range(QT):
                        for g in range(4):
                            mm = pe.matmul(misc[(g % 2) * DH:(g % 2 + 1) * DH, g // 2, c * P:(c + 1) * P],
                                           VG[:, c, g * DH:(g + 1) * DH], prm("sgu_w")[:, g * P:(g + 1) * P],
                                           start=True, stop=True)
                    mm.then_inc(*raised("tokens_mixed", ("sgu",)))
                    Misc.read = ("sgu_bias",)
                if step == 7:
                    turn_pe(pe, ("v1",), [FEAT[:, 16, :], FEAT[:, 17, :]], ("in", m, 8, "read"))
                if step == 12:
                    turn_pe(pe, ("v2",), [FEAT[:, 18, :], FEAT[:, 19, :]], ("in", m, 9, "read"))
                if step == 10:
                    pe.wait_ge(*done(("hidden",)))
                    misc_free(pe)
                    for o in range(4):
                        mm = pe.transpose(MISC[:, o * NB:(o + 1) * NB], HIDDEN[:, o // 2, o % 2 * P:(o % 2 + 1) * P],
                                          ident[0:NB, 0:NB])
                    mm.then_inc(*raised("turned", ("hid", "turned")))
                    Misc.read = ("hid", "copied")
                if step == 11:
                    compressed_pe(pe)
                    rope_pe(pe, ("rope_q", m, 0), FEAT[:, 4:6, :], ("in", m, 2, "read"), "rotate")
                if step == 12:
                    start_attention_pe(pe, items)
            scores_pe(pe, items, 2)
            for n in (1, 2):
                rope_pe(pe, ("rope_q", m, n), FEAT[:, 4 + 2 * n:6 + 2 * n, :], ("in", m, 2 + n, "read"), "rotate")
            attention_pe(pe, items)
            last = len(items) - 1
            turn_probs_pe(pe, items, last)
            apply_pe(pe, items, last - 1)
            apply_pe(pe, items, last)
            out_pe(pe, ("mix_out", m), c0 + EV_IN + CMP, OH, OL, [("o_split", m, t) for t in range(KT)])

        def compressed_pe(pe):
            pe.wait_ge(*done(("hid", "copied")))
            misc_free(pe)
            w2k = prm("cmp_w2_k").rearrange("p (k c) -> p k c", k=2)
            w2v = prm("cmp_w2_v").rearrange("p (k c) -> p k c", k=2)
            for k in range(2):
                pe.matmul(MISC[:, 0:NB], w2k[:, k, :], HID[:, k, :], start=k == 0, stop=k == 1)
            for g in range(B_KV):
                for k in range(2):
                    mm = pe.matmul(MISC[0:NCMP, 64 + g * DH:64 + (g + 1) * DH],
                                   HID[:, 2 + k, g * NCMP:(g + 1) * NCMP], w2v[:, k, :], start=k == 0, stop=k == 1)
            mm.then_inc(*raised("compressed", ("compressed",)))
            Misc.read = ("kc",)

        def ev_act(act, m, c0, norm, after, gain):
            items = ev_items(m)

            def shift(x):
                n = "kv".index(x)
                act.wait_ge(*done(("shift_zero",)))
                for g in range(B_KV):
                    src = half(20 + 3 * n + g)
                    act.activation(SHIFT[x][0:DH, g, 0:T], src, ACT.Copy)
                    ins = act.activation(SHIFT[x][DH:P, g, 0:T - CMP_STRIDE], src[:, CMP_STRIDE:], ACT.Copy)
                ins.then_inc(*raised("tokens_shifted", ("shift", x)))
                act.wait_ge(*done(("blocks_full", x)))
                act.activation(OHf[:, 768 * n:768 * (n + 1)], BLOCKS[x], ACT.Copy)\
                    .then_inc(*raised("blocks_high", ("blocks_high", x)))

            for step, j in enumerate(EV_STEPS):
                act_ahead(act, c0 + step)
                if step == 0:
                    rms_act(act, norm)
                if step == 1:
                    rope_tables_act(act, 1)
                if step == 2:
                    act.wait_ge(*done(("in", m, 0, "read")))
                    act.wait_ge(*done(("in", m, 1, "read")))
                    act.activation(FEAT[:, 0:4, :], FEAT[:, 0:4, :], ACT.Gelu_apprx_tanh)\
                        .then_inc(*raised("gelu", ("gelu",)))
                    act.wait_ge(*done(("gelu",)))
                    act.activation(W[:, 6:8, :], FEAT[:, 2:4, :], ACT.Square)\
                        .then_inc(*raised("v_squares", ("v_squares",)))
                if step == 3:
                    act.wait_ge(*done(("in", m, 5, "read")))
                    shift("k")
                    act.wait_ge(*done(("v_var",)))
                    act.activation(RV, RV, ACT.Sqrt).then_inc(*raised("v_root", ("v_root",)))
                if step == 4:
                    act.wait_ge(*done(("in", m, 6, "read")))
                    shift("v")
                if step == 6:
                    turn_act(act, ("vg",), 2, VG[:, :, :])
                if step == 8:
                    act.wait_ge(*done((("rope_k", m, 1), "done")))
                    for h in range(2):
                        for p in range(2):
                            ins = act.activation(KD[h * DH:(h + 1) * DH, p::2, :], FEAT[p * DH:(p + 1) * DH, 13:16, :],
                                                 ACT.Copy)
                    ins.then_inc(*raised("keys_doubled", ("kd", m)))
                    turn_act(act, ("v1",), 2, VT[:, :, 0:2 * P])
                if step == 13:
                    exps_act(act, items, 0)
                    act.wait_ge(*done((("v2",), "turned")))
                    mr = OUTP[:, 0:512].rearrange("p (r c) -> p r c", r=QT)
                    act.activation(VT[:, :, 2 * P:3 * P], mr[:, :, 0:P], ACT.Copy)
                    act.activation(GT, mr[:, :, P:P + 36], ACT.Sigmoid).then_inc(*raised("v2_gates", (("v2",), "gates")))
                    K.alias((("v2",), "copied"), (("v2",), "gates"))
                if step == 10:
                    act.wait_ge(*done(("cmp", "v", 1)))
                    act.activation(HIDDEN, ACC[0:NB, 0:2, 0:2 * P], ACT.Gelu_apprx_tanh)\
                        .then_inc(*raised("hidden", ("hidden",)))
                if step == 11:
                    act.wait_ge(*done(("hid", "turned")))
                    act.activation(HID[:, :, :], MISC[:, 0:4 * NB].rearrange("p (o n) -> p o n", o=4), ACT.Copy)\
                        .then_inc(*raised("psum_copied", ("hid", "copied")))
                if step == 12:
                    act.wait_ge(*done(("compressed",)))
                    act.activation(KC[:, :, :], MISC[:, 0:NB].rearrange("p (g n) -> p g n", g=B_KV), ACT.Copy)
                    act.activation(VC[0:NCMP, :, :],
                                   MISC[0:NCMP, 64:64 + B_KV * DH].rearrange("p (g d) -> p g d", g=B_KV),
                                   ACT.Copy).then_inc(*raised("compressed_copied", ("kc",)))
                    split_w_act(act, m, slice(0, 2), [("gmlp",)])
            exps_act(act, items, 1)
            attention_act(act, items)
            high_act(act, items[-1])
            out_act(act, ("mix_out", m), c0 + EV_IN + CMP, after, gain)

        def ev_dve(dve, m, c0, norm, after, gain):
            items = ev_items(m)

            def blocks(x):
                n = "kv".index(x)
                dve.wait_ge(*done(("shift", x)))
                s, pos = SHIFT[x], prm(f"pos_{x}")
                for g in range(B_KV):
                    dst = BLOCKS[x].rearrange("p (l g n) -> p g l n", l=CMP_STRIDE, g=B_KV)[:, g]
                    src = s[:, g, 0:T].rearrange("p (n l) -> p l n", l=CMP_STRIDE)
                    ins = dve.tensor_tensor(dst, src, pos.rearrange("p (l n) -> p l n", n=1)
                                            .broadcast_to([P, CMP_STRIDE, NCMP]), ALU.add)
                ins.then_inc(*raised("blocks_full", ("blocks_full", x)))
                dve.wait_ge(*done(("blocks_high", x)))
                dve.tensor_tensor(OLf[:, 768 * n:768 * (n + 1)], BLOCKS[x],
                                  OHf[:, 768 * n:768 * (n + 1)].bitcast(F32), ALU.subtract)\
                    .then_inc(*raised("blocks", ("blocks", x)))

            dve.memset(SHIFT["k"][DH:P, :, T - CMP_STRIDE:T], 0.0)
            dve.memset(SHIFT["v"][DH:P, :, T - CMP_STRIDE:T], 0.0).then_inc(*raised("shift_zero", ("shift_zero",)))
            for step, j in enumerate(EV_STEPS):
                dve_ahead(dve, c0 + step)
                if step == 0:
                    rms_dve(dve, norm)
                if step == 3:
                    blocks("k")
                    dve.wait_ge(*done(("v_mean",)))
                    dve.tensor_scalar(RV, MISC[:, 0:T], RMS_EPS, None, ALU.add).then_inc(*raised("v_var", ("v_var",)))
                    dve.wait_ge(*done(("v_root",)))
                    dve.reciprocal(RV, RV).then_inc(*raised("v_rstd", ("v_rstd",)))
                    dve.wait_ge(*done(("v_rstd",)))
                    for t in range(2):
                        ins = dve.scalar_tensor_tensor(out=W[:, 4 + t, :], in0=FEAT[:, 2 + t, :],
                                                       scalar=prm("sgu_norm")[:, t:t + 1], in1=RV,
                                                       op0=ALU.mult, op1=ALU.mult)
                    ins.then_inc(*raised("v_scaled", ("v_scaled",)))
                if step == 4:
                    blocks("v")
                if step == 7:
                    dve.wait_ge(*done(("sgu",)))
                    for t in range(2):
                        ins = dve.tensor_tensor(W[:, t, :].rearrange("p (c s) -> p c s", c=QT),
                                                misc[:, t, :].rearrange("p (c s) -> p c s", c=QT),
                                                over(prm("sgu_b")[:, t * P:(t + 1) * P], QT), ALU.add)
                    ins.then_inc(*raised("sgu_bias", ("sgu_bias",)))
                    dve.wait_ge(*done(("sgu_bias",)))
                    dve.tensor_tensor(W[:, 0:2, :], W[:, 0:2, :], FEAT[:, 0:2, :], ALU.mult)\
                        .then_inc(*raised("gmlp", ("gmlp",)))
                if step == 13:
                    masked_max_dve(dve, items, 0)
                    masked_max_dve(dve, items, 1)
                if j not in ("k0", "k1", "v0", "v1"):
                    in_dve(dve, m, j)
                if step == 4:
                    dve.wait_ge(*done(("tables", 1, "done")))
                    rope_dve(dve, ("rope_k", m, 0), 0, 1)
                if step == 5:
                    rope_dve(dve, ("rope_k", m, 1), 0, 2)
                if step == 12:
                    rope_dve(dve, ("rope_q", m, 0), 0, 2)
            for n in (1, 2):
                rope_dve(dve, ("rope_q", m, n), 0, 2)
            split_w_dve(dve, m, slice(0, 2))
            dve.wait_ge(*done((("v2",), "gates")))
            attention_dve(dve, items, (("rope_q", m, 2), "sin"), (("v2",), "gates"), started=2)
            last_low_dve(dve, items)
            out_dve(dve, ("mix_out", m), c0 + EV_IN + CMP, False, after, gain)

        VW = SIL
        SC, WK = UPf[:, 0:SEQ_K], UPf[:, SEQ_K:2 * SEQ_K]
        M8 = [small[:, 40:48], small[:, 48:56]]
        DMASK = A[:, :, :].rearrange("p a t -> p (a t)")[:, 0:SEQ_K]

        def od_items(m):
            pairs = []
            for n in range(KT):
                hs = [slice(h * DH, (h + 1) * DH) for h in range(2)]
                if n < 4:
                    q, k = [FEAT[h, n, :] for h in hs], [FEAT[h, 4, :] for h in hs]
                    it = Item(("od", n), q, k, lambda h, r: VW[:, r, 0:DH], FULL, DMASK)
                else:
                    q, k = [FEAT[h, 4 + n, :] for h in hs], [FEAT[h, 8 + n, :] for h in hs]
                    it = Item(("od", n), q, k, lambda h, r, at=2 * (n - 4) * DH: VT[:, r, at + h * DH:at + (h + 1) * DH],
                              FULL, prm("causal"), after=[(("vd", 1), "copied")])
                it.after = list(it.after) + [od_roped(m, t) for t in ((n, 4) if n < 4 else (4 + n, 8 + n))]
                pairs.append((n, [it]))
            return in_pairs(m, pairs)

        def od_roped(m, tile):
            return ("rope_o", m, tile // 2), "done"

        def od_rope(m, step):
            j = OD_ORDER[step - 1] if step else None
            if j in (0, 1, 4, 5, 6, 7):
                return ("rope_o", m, j), FEAT[:, 2 * j:2 * j + 2, :]
            if j == 2:
                return ("rope_o", m, j), FEAT[:, 4:5, :]
            return None

        def od_pe(pe, m, c0, norm):
            items = od_items(m)
            for step, j in enumerate(OD_ORDER):
                in_pe(pe, m, c0 + step, step, j)
                if step == 0:
                    rms_pe(pe, norm)
                if step == 1:
                    rope_pe(pe, ("rope_i", m), FEAT[:, 6:8, :], ("in", m, 3, "read"), "rotate_i")
                if step == 2:
                    turn_pe(pe, ("vw",), [FEAT[:, 5, :]], ("in", m, 2, "read"))
                    pe.wait_ge(*done((("rope_i", m), "done")))
                    for h in range(IDX_HEADS):
                        for r, (lo, hi) in enumerate(FULL):
                            p = slice(h * IDX_DIM, (h + 1) * IDX_DIM)
                            mm = pe.matmul(ACC[:, h, lo:hi], FEAT[p, 6, r * P:(r + 1) * P], FEAT[p, 7, 0:hi - lo],
                                           start=True, stop=True)
                    mm.then_inc(*raised("scores_done", ("index",)))
                    Misc.accs = ("index_relu",)
                if od_rope(m, step):
                    tag, tiles = od_rope(m, step)
                    rope_pe(pe, tag, tiles, ("in", m, OD_ORDER[step - 1], "read"), "rotate")
                if step == 8:
                    start_attention_pe(pe, items)
                if step == 9:
                    scores_pe(pe, items, 2)
                    turn_pe(pe, ("vd", 0), [FEAT[:, 16, :], FEAT[:, 17, :]], ("in", m, 8, "read"))
            turn_pe(pe, ("vd", 1), [FEAT[:, 18, :], FEAT[:, 19, :]], ("in", m, 9, "read"))
            attention_pe(pe, items)
            last = len(items) - 1
            turn_probs_pe(pe, items, last)
            apply_pe(pe, items, last - 1)
            apply_pe(pe, items, last)
            out_pe(pe, ("mix_out", m), c0 + OD_IN, OH, OL, [("o_split", m, t) for t in range(KT)])

        def od_act(act, m, c0, norm, after, gain):
            items = od_items(m)
            for step in range(OD_IN):
                act_ahead(act, c0 + step)
                if step == 9:
                    exps_act(act, items, 0)
                if step == 0:
                    rms_act(act, norm)
                if step == 3:
                    turn_act(act, ("vw",), 1, VW[:, :, 0:P])
                    act.wait_ge(*done(("index",)))
                    act.activation(SM[:, :, :], ACC[:, :, 0:SEQ_K], ACT.Relu, scale=IDX_DIM ** -0.5)\
                        .then_inc(*raised("index_relu", ("index_relu",)))
            for n in range(2):
                turn_act(act, ("vd", n), 2, VT[:, :, 2 * n * P:2 * (n + 1) * P])
            exps_act(act, items, 1)
            attention_act(act, items)
            high_act(act, items[-1])
            out_act(act, ("mix_out", m), c0 + OD_IN, after, gain)

        def od_dve(dve, m, c0, norm, after, gain):
            items = od_items(m)
            rounds = TOPK // 8
            for step, j in enumerate(OD_ORDER):
                dve_ahead(dve, c0 + step)
                if step == 0:
                    rms_dve(dve, norm)
                if step == 9:
                    dve.wait_ge(*done(("taken", rounds - 1, 1)))
                    dve.tensor_scalar(DMASK, WK, TAKEN / 2, NEG, ALU.is_gt, ALU.mult)\
                        .then_inc(*raised("not_taken", ("not_taken",)))
                    dve.wait_ge(*done(("not_taken",)))
                    dve.tensor_tensor(DMASK, DMASK, prm("causal"), ALU.add)\
                        .then_inc(*raised("selected", ("selected",)))
                    dve.wait_ge(*done(("selected",)))
                    masked_max_dve(dve, items, 0)
                if step == 3:
                    index_dve(dve)
                if 4 <= step <= 8:
                    for n in range(rounds * (step - 4) // 5, rounds * (step - 3) // 5):
                        top_round_dve(dve, n)
                in_dve(dve, m, j)
                if step == 1:
                    rope_dve(dve, ("rope_i", m), 2, 2)
                if od_rope(m, step):
                    tag, tiles = od_rope(m, step)
                    rope_dve(dve, tag, 0, tiles.shape[1])
            attention_dve(dve, items, (("rope_o", m, 7), "sin"), (("vd", 1), "copied"))
            last_low_dve(dve, items)
            out_dve(dve, ("mix_out", m), c0 + OD_IN, False, after, gain)

        def index_dve(dve):
            dve.wait_ge(*done((("vw",), "copied")))
            dve.wait_ge(*done(("index_relu",)))
            for h in range(IDX_HEADS):
                if h:
                    dve.wait_ge(*done(("index_sum", h - 1)))
                for r, (lo, hi) in enumerate(FULL):
                    w = VW[:, r, DH + h:DH + h + 1]
                    if h == 0:
                        ins = dve.tensor_scalar(SC[:, lo:hi], SM[:, h, lo:hi], w, None, ALU.mult)
                    else:
                        ins = dve.scalar_tensor_tensor(out=SC[:, lo:hi], in0=SM[:, h, lo:hi], scalar=w,
                                                       in1=SC[:, lo:hi], op0=ALU.mult, op1=ALU.add)
                ins.then_inc(*raised("index_sum", ("index_sum", h)))
            dve.wait_ge(*done(("index_sum", IDX_HEADS - 1)))
            dve.scalar_tensor_tensor(out=WK, in0=SC, scalar=IDX_HEADS ** -0.5, in1=prm("causal"),
                                     op0=ALU.mult, op1=ALU.add)\
                .then_inc(*raised("index_score", ("index_score",)))
            dve.wait_ge(*done(("index_score",)))

        def top_round_dve(dve, n):
            for r, (lo, hi) in enumerate(FULL):
                if n:
                    dve.wait_ge(*done(("taken", n - 1, r)))
                dve.max(M8[r], WK[:, lo:hi]).then_inc(*raised("top_8_found", ("top8", n, r)))
            for r, (lo, hi) in enumerate(FULL):
                dve.wait_ge(*done(("top8", n, r)))
                dve.match_replace(WK[:, lo:hi], M8[r], WK[:, lo:hi], TAKEN)\
                    .then_inc(*raised("top_8_taken", ("taken", n, r)))

        HID = sb("HID", [P, 4, NB])
        KC = sb("KC", [P, B_KV, NCMP])
        VC = sb("VC", [P, B_KV, DH])
        c = 0
        stages = []
        for l in range(DEPTH):
            stages.append(("mix1", l, c))
            c += IN1 + GATE1 + OUT
            stages.append(("ffn1", l, c))
            c += FFN_CHUNKS
        for l in range(DEPTH):
            stages.append(("ffn2", 2 + 2 * l, c))
            c += FFN_CHUNKS
            stages.append(("ev" if l % 2 == 0 else "od", l, c))
            c += (EV_IN + CMP if l % 2 == 0 else OD_IN) + OUT
            stages.append(("ffn2", 3 + 2 * l, c))
            c += FFN_CHUNKS
        assert c == n_chunks, (c, n_chunks)

        M2 = {l: ("mix2", l) for l in range(DEPTH)}

        ANG = FEAT[:, 12:20, :]

        def rope_tables(dve, stack):
            two_pi = 2 * np.pi
            c1 = 6.28125
            c2 = float(np.float32(np.round((two_pi - c1) * 2 ** 22) / 2 ** 22))
            c3 = two_pi - c1 - c2
            dve.wait_ge(K.sem("positions_loaded"), 32)
            dve.wait_ge(*done("params_loaded"))
            tag = ("tables", stack)
            n = [0]

            def step(ins):
                ins.then_inc(*raised(f"table{stack}_step", (tag, n[0])))
                dve.wait_ge(*done((tag, n[0])))
                n[0] += 1

            step(dve.tensor_copy(posf, posi[:, stack, :]))
            for which, f in enumerate(("freq", "freq_i")[:1 + stack]):
                ang, turn = ANG[:, 4, :], ANG[:, 5, :]
                step(dve.tensor_scalar(ang, posf, prm(f), None, ALU.mult))
                step(dve.tensor_scalar(turn, ang, 1 / two_pi, 12582912.0, ALU.mult, ALU.add))
                step(dve.tensor_scalar(turn, turn, -12582912.0, None, ALU.add))
                for part in (c1, c2, c3):
                    step(dve.tensor_scalar(ANG[:, 7, :], turn, -part, None, ALU.mult))
                    step(dve.tensor_tensor(ang, ang, ANG[:, 7, :], ALU.add))
                step(dve.tensor_scalar(turn, ang, np.pi / 2, -two_pi, ALU.is_gt, ALU.mult))
                step(dve.tensor_scalar(ANG[:, 7, :], ang, np.pi / 2, None, ALU.add))
                step(dve.tensor_tensor(turn, turn, ANG[:, 7, :], ALU.add))
                lim = 3.1415925
                step(dve.tensor_scalar(ANG[:, 2 * which, :], turn, lim, -lim, ALU.min, ALU.max))
                dve.tensor_scalar(ANG[:, 2 * which + 1, :], ang, lim, -lim, ALU.min, ALU.max)\
                    .then_inc(*raised(f"angles{stack}", (tag, "angles", which)))
                dve.wait_ge(*done((tag, "angles", which)))

        def rope_tables_act(act, stack):
            for which in range(1 + stack):
                act.wait_ge(*done((("tables", stack), "angles", which)))
                ins = act.activation(ropes[:, 2 * which:2 * which + 2, :], ANG[:, 2 * which:2 * which + 2, :], ACT.Sin)
            ins.then_inc(*raised("tables_done", ("tables", stack, "done")))

        def mix1_pool(pool, l):
            if l == 0:
                pool.wait_ge(*done(("tables", 0, "done")))
            for j in range(3):
                tiles = FEAT[:, 2 * j:min(2 * j + 2, 5), :]
                rope_pool(pool, ("rope", l, j), tiles, tiles, 0)

        def ev_pool(pool, m):
            pool.wait_ge(*done(("tables", 1, "done")))
            rope_pool(pool, ("rope_k", m, 0), FEAT[:, 13:14, :], FEAT[:, 13:14, :], 0)
            rope_pool(pool, ("rope_k", m, 1), FEAT[:, 14:16, :], FEAT[:, 14:16, :], 0)
            for n in range(3):
                rope_pool(pool, ("rope_q", m, n), FEAT[:, 4 + 2 * n:6 + 2 * n, :], QR[:, 2 * n:2 * n + 2, :], 0)

        def od_pool(pool, m):
            rope_pool(pool, ("rope_i", m), FEAT[:, 6:8, :], FEAT[:, 6:8, :], 2)
            for step in range(OD_IN):
                if od_rope(m, step):
                    tag, tiles = od_rope(m, step)
                    rope_pool(pool, tag, tiles, tiles, 0)

        @block.sync
        def _(sp):
            for s in range(RING):
                sp.dma_start(raw[:, s, :], weights[s]).then_inc(K.sem(f"chunk_loaded{s}"), 16)
                if s == 0:
                    for j in range(4):
                        p = slice(2 * j, 2 * j + 2)
                        sp.dma_start(X[:, p, :], x_in[:, p, :])\
                            .then_inc(*raised(f"x_loaded{j}", ("x_loaded", j), 16))
                if s == RING - 1:
                    sp.dma_start(posi[:, 0, :], pos1.partition_broadcast(P)).then_inc(K.sem("positions_loaded"), 16)
                    sp.dma_start(posi[:, 1, :], pos2.partition_broadcast(P)).then_inc(K.sem("positions_loaded"), 16)
                    sp.dma_start(PRM[:, :], params).then_inc(*raised("params_loaded", "params_loaded", 16))
            turns = n_chunks // RING
            with sp.Fori(1, turns) as i:
                for s in range(RING):
                    sp.wait_ge(K.sem("w_low_ready"), i * RING + (s + 1 - RING))
                    sp.dma_start(raw[:, s, :], weights[bass.ds(i * RING + s, 1)]
                                 .rearrange("a p c -> (a p) c")).then_inc(K.sem(f"chunk_loaded{s}"), 16)
            for cc in range(turns * RING, n_chunks):
                sp.wait_ge(K.sem("w_low_ready"), cc + 1 - RING)
                sp.dma_start(raw[:, cc % RING, :], weights[cc]).then_inc(K.sem(f"chunk_loaded{cc % RING}"), 16)
            for j in range(4):
                p = slice(2 * j, 2 * j + 2)
                sp.wait_ge(*done(("result", j)))
                sp.dma_start(out[:, p, :], W[:, p, :]).then_inc(K.sem("out_stored"), 16)
            sp.wait_ge(K.sem("out_stored"), 4 * 16)

        @block.gpsimd
        def _(pool):
            pool.memset(ones_d[:, :], 1.0 / D).then_inc(*raised("constants_set", "ones_d"))
            pool.memset(ones_v[:, :], 1.0 / 256).then_inc(*raised("constants_set", "ones_v"))
            pool.memset(ones_1[:, :], 1.0).then_inc(*raised("constants_set", "ones_1"))
            pool.memset(UP[:, :, :, 0:2], 0.0).then_inc(*raised("constants_set", "up_zero"))
            pool.wait_ge(*done("params_loaded"))
            w = prm("sgu_w").rearrange("p (g t) -> p g t", g=4)
            pool.affine_select(out=w, in_=w, compare_op=ALU.is_ge, fill=0.0, base=0,
                               pattern=[[0, 4], [1, P]], channel_multiplier=-1)\
                .then_inc(*raised("constants_set", "sgu_masked"))
            for kind, n, c0 in stages:
                if kind == "mix1":
                    mix1_pool(pool, n)
                elif kind == "ffn1":
                    if n == DEPTH - 1:
                        pool.wait_ge(*done(("x_split", n, 3)))
                        rope_tables(pool, 1)
                        rms_squares_pool(pool, "stack2")
                elif kind == "ffn2":
                    rms_squares_pool(pool, n)
                else:
                    (ev_pool if kind == "ev" else od_pool)(pool, M2[n])
                    rms_squares_pool(pool, ("mix_out", M2[n]))

        @block.tensor
        def _(pe):
            pe.wait_ge(*done("ones_v"))
            norm = None
            for kind, n, c0 in stages:
                if kind == "mix1":
                    mix1_pe(pe, n, c0)
                    ln_pe(pe, ("mix_out", n))
                elif kind == "ffn1":
                    ffn_pe(pe, n, c0, None)
                    ln_pe(pe, n)
                    norm = "stack2"
                elif kind == "ffn2":
                    ffn_pe(pe, n, c0, norm)
                    norm = n
                elif kind == "ev":
                    pe.wait_ge(*done("sgu_masked"))
                    ev_pe(pe, M2[n], c0, norm)
                    norm = ("mix_out", M2[n])
                else:
                    od_pe(pe, M2[n], c0, norm)
                    norm = ("mix_out", M2[n])
            rms_pe(pe, norm)

        def next_norm(kind, n):
            if kind == "ffn2":
                return {2: (M2[0], "mix_norm0"), 3: (4, "ffn1_norm1"), 4: (M2[1], "mix_norm1"), 5: (None, None)}[n]
            return 3 + 2 * n, f"ffn2_norm{n}"

        @block.scalar
        def _(act):
            act.wait_ge(*done("ones_v"))
            warm(act, ACT.Copy)
            split_high(act, 0)
            for b in range(4):
                act.wait_ge(*done(("x_loaded", b)))
                act.activation(XH[:, 2 * b:2 * b + 2, :], X[:, 2 * b:2 * b + 2, :], ACT.Copy)\
                    .then_inc(*raised("x_high", ("x_high", ("mix", 0), b)))
            split_high(act, 1)
            norm = None
            for kind, n, c0 in stages:
                if kind == "mix1":
                    mix1_act(act, n, c0)
                    ln_act(act, ("mix_out", n), n, f"ln1_g{n}", f"ln1_b{n}")
                elif kind == "ffn1":
                    if n == 0:
                        act.wait_ge(*done("up_zero"))
                    ffn_act(act, n, c0, n, None)
                    last = n == DEPTH - 1
                    ln_act(act, n, None if last else ("mix", n + 1), f"ln2_g{n}", f"ln2_b{n}")
                    if last:
                        norm = "stack2"
                        for b in range(4):
                            rms_high_act(act, norm, 2, "ffn1_norm0", b)
                        rms_squares_act(act, norm)
                else:
                    after, gain = next_norm(kind, n)
                    if kind == "ffn2":
                        ffn_act(act, n, c0, None, norm)
                        for b in range(4 if after is not None else 0):
                            rms_high_act(act, n, after, gain, b)
                        norm = n
                    else:
                        (ev_act if kind == "ev" else od_act)(act, M2[n], c0, norm, after, gain)
                        norm = ("mix_out", M2[n])
                    rms_squares_act(act, norm)
            rms_act(act, norm)

        @block.vector
        def _(dve):
            split_low(dve, 0)
            for b in range(4):
                p = slice(2 * b, 2 * b + 2)
                dve.wait_ge(*done(("x_high", ("mix", 0), b)))
                dve.tensor_tensor(XL[:, p, :], X[:, p, :], XH[:, p, :].bitcast(F32), ALU.subtract)\
                    .then_inc(*raised("x_split", ("x_split", ("mix", 0), b)))
            split_low(dve, 1)
            norm = None
            for kind, n, c0 in stages:
                if kind == "mix1":
                    mix1_dve(dve, n, c0)
                    ln_dve(dve, ("mix_out", n), n, f"ln1_g{n}", f"ln1_b{n}")
                elif kind == "ffn1":
                    ffn_dve(dve, n, c0, n, None)
                    last = n == DEPTH - 1
                    ffn_residual_dve(dve, n, c0, True, None, None)
                    ln_dve(dve, n, None if last else ("mix", n + 1), f"ln2_g{n}", f"ln2_b{n}", c0 + FFN_CHUNKS - 1)
                    if last:
                        norm = "stack2"
                        rms_low_dve(dve, 2, "ffn1_norm0", 3)
                        rms_sums_dve(dve, norm)
                else:
                    after, gain = next_norm(kind, n)
                    if kind == "ffn2":
                        ffn_dve(dve, n, c0, None, norm)
                        ffn_residual_dve(dve, n, c0, False, after, gain)
                        norm = n
                    else:
                        (ev_dve if kind == "ev" else od_dve)(dve, M2[n], c0, norm, after, gain)
                        norm = ("mix_out", M2[n])
                        rms_sums_dve(dve, norm)
            for k in range(KT):
                ins = dve.tensor_scalar(W[:, k, :], X[:, k, :], prm("final_norm")[:, k:k + 1], None, ALU.mult)
            ins.then_inc(*raised("final_gain", "final_gain"))
            rms_dve(dve, norm)
            dve.wait_ge(*done("final_gain"))
            for j in range(4):
                w = W[:, 2 * j:2 * j + 2, :]
                dve.tensor_tensor(w, w, over(RS[:, :], 2), ALU.mult).then_inc(*raised("result_ready", ("result", j)))
        return K.now


def kernel(**inputs):
    import concourse.bacc as bacc
    from concourse.bass_utils import run_bass_kernel_spmd

    a = {k: np.asarray(v) for k, v in inputs.items()}
    params, at = small_parameters(a)
    arrays = {
        "weights": weight_stream(a),
        "params": params,
        "x_in": np.ascontiguousarray(a["x"][0].T.reshape(KT, P, T).transpose(1, 0, 2)),
        "pos1": np.ascontiguousarray(a["positions"].reshape(T)),
        "pos2": np.ascontiguousarray(a["positions_2"].reshape(T)),
    }
    seen = None
    for _ in range(2):
        nc = bacc.Bacc("TRN2", target_bir_lowering=False, num_devices=1)
        aps = {n: nc.dram_tensor(n, v.shape, mybir.dt.from_np(v.dtype), kind="ExternalInput").ap()
               for n, v in arrays.items()}
        out = nc.dram_tensor("out", (P, KT, T), F32, kind="ExternalOutput").ap()
        seen = build(nc, at=at, out=out, seen=seen, **aps)
    r = run_bass_kernel_spmd(nc, [arrays], core_ids=[0])
    got = r.results[0]["out"]
    return np.ascontiguousarray(got.transpose(2, 1, 0)).reshape(1, T, D)
```
